# Optimizing a Trainium2 kernel written in Bass

```python
import math
import jax, jax.numpy as jnp
from jax import lax
import numpy as np

D_MODEL = 1024
BATCH = 1
SEQ = 256
DEPTH = 2

N_A_LAYERS = DEPTH // 2
N_B_LAYERS = DEPTH - N_A_LAYERS

DIFF_HEADS = 8
DIFF_SUB_DIM = D_MODEL // (2 * DIFF_HEADS)
DIFF_V_DIM = 2 * DIFF_SUB_DIM

SWA_Q_HEADS = 16
SWA_KV_HEADS = 2
SWA_HEAD_DIM = D_MODEL // SWA_Q_HEADS
SWA_GROUP = SWA_Q_HEADS // SWA_KV_HEADS
SWA_KV_WIDTH = SWA_KV_HEADS * SWA_HEAD_DIM
WINDOW = 128
BLOCK = 128

D_FF = 2816

ROPE_THETA = 500000.0
ROT_DIM = SWA_HEAD_DIM // 4

NORM_EPS = 1e-5

kernel_name = "yoco_diffattn_swa_sink_macaron"

def rms_norm(x, g):
    xf = x.astype(jnp.float32)
    y = xf * lax.rsqrt(jnp.mean(xf * xf, axis=-1, keepdims=True) + NORM_EPS)
    return (y * g.astype(jnp.float32)).astype(x.dtype)

def rope_tables(positions):
    inv_freq = ROPE_THETA ** (-jnp.arange(0, ROT_DIM, 2, dtype=jnp.float32) / ROT_DIM)
    ang = positions.astype(jnp.float32)[..., None] * inv_freq
    return jnp.cos(ang), jnp.sin(ang)

def apply_partial_rope(x, cos, sin):
    half = cos.shape[-1]
    rot = 2 * half
    bshape = cos.shape[:2] + (1,) * (x.ndim - 3) + (half,)
    c = cos.reshape(bshape).astype(x.dtype)
    s = sin.reshape(bshape).astype(x.dtype)
    x1 = x[..., :half]
    x2 = x[..., half:rot]
    return jnp.concatenate([x1 * c - x2 * s, x2 * c + x1 * s, x[..., rot:]], axis=-1)

def swiglu(x, w_gate, w_up, w_down):
    return (jax.nn.silu(x @ w_gate) * (x @ w_up)) @ w_down

def diff_attention(u, w_qkv, w_o, lq1, lk1, lq2, lk2, g_sub, cos, sin, lambda_init):
    B, S, _ = u.shape
    nblk = S // BLOCK
    qkv = u @ w_qkv
    q, k, v = jnp.split(qkv, [D_MODEL, 2 * D_MODEL], axis=-1)
    q = apply_partial_rope(q.reshape(B, S, DIFF_HEADS, 2, DIFF_SUB_DIM), cos, sin)
    k = apply_partial_rope(k.reshape(B, S, DIFF_HEADS, 2, DIFF_SUB_DIM), cos, sin)
    v = v.reshape(B, S, DIFF_HEADS, DIFF_V_DIM)
    f32 = jnp.float32
    lam = (jnp.exp(jnp.sum(lq1.astype(f32) * lk1.astype(f32)))
           - jnp.exp(jnp.sum(lq2.astype(f32) * lk2.astype(f32))) + lambda_init)
    scale = DIFF_SUB_DIM ** -0.5
    q_blocks = q.reshape(B, nblk, BLOCK, DIFF_HEADS, 2, DIFF_SUB_DIM).transpose(1, 0, 2, 3, 4, 5)
    key_idx = jnp.arange(S)

    def one_block(args):
        q_blk, blk = args
        s = jnp.einsum('bqhcd,bkhcd->bhcqk', q_blk, k).astype(f32) * scale
        q_idx = blk * BLOCK + jnp.arange(BLOCK)
        causal = key_idx[None, :] <= q_idx[:, None]
        p = jax.nn.softmax(jnp.where(causal, s, -jnp.inf), axis=-1)
        a = p[:, :, 0] - lam * p[:, :, 1]
        return jnp.einsum('bhqk,bkhe->bqhe', a.astype(v.dtype), v)

    o = lax.map(one_block, (q_blocks, jnp.arange(nblk)))
    o = o.transpose(1, 0, 2, 3, 4).reshape(B, S, DIFF_HEADS, DIFF_V_DIM)
    o = rms_norm(o, g_sub) * (1.0 - lambda_init)
    return o.reshape(B, S, D_MODEL) @ w_o

def banded(t):
    B, S = t.shape[:2]
    tb = t.reshape(B, S // BLOCK, BLOCK, SWA_KV_HEADS, SWA_HEAD_DIM)
    prev = jnp.concatenate([jnp.zeros_like(tb[:, :1]), tb[:, :-1]], axis=1)
    return jnp.concatenate([prev, tb], axis=2)

def shared_kv(h, g_kv, w_k, b_k, w_v, b_v, cos, sin):
    B, S, _ = h.shape
    u = rms_norm(h, g_kv)
    k = apply_partial_rope((u @ w_k + b_k).reshape(B, S, SWA_KV_HEADS, SWA_HEAD_DIM), cos, sin)
    v = (u @ w_v + b_v).reshape(B, S, SWA_KV_HEADS, SWA_HEAD_DIM)
    return banded(k), banded(v)

def band_mask(nblk):
    i = jnp.arange(BLOCK)[:, None]
    j = jnp.arange(2 * BLOCK)[None, :]
    dist = i + BLOCK - j
    in_win = (dist >= 0) & (dist < WINDOW)
    has_prev = (jnp.arange(nblk) > 0)[:, None, None]
    return in_win[None] & (has_prev | (j >= BLOCK)[None])

def swa_sink_attention(u, w_q, b_q, sinks, w_o, b_o, k_band, v_band, cos, sin):
    B, S, _ = u.shape
    nblk = S // BLOCK
    q = apply_partial_rope((u @ w_q + b_q).reshape(B, S, SWA_Q_HEADS, SWA_HEAD_DIM), cos, sin)
    q = q.reshape(B, nblk, BLOCK, SWA_KV_HEADS, SWA_GROUP, SWA_HEAD_DIM)
    f32 = jnp.float32
    s = jnp.einsum('bnqhgd,bnkhd->bnhgqk', q, k_band).astype(f32) * (SWA_HEAD_DIM ** -0.5)
    mask = band_mask(nblk)[None, :, None, None]
    s = jnp.where(mask, s, -jnp.inf)
    sink = sinks.astype(f32).reshape(1, 1, SWA_KV_HEADS, SWA_GROUP, 1, 1)
    m = jnp.maximum(jnp.max(s, axis=-1, keepdims=True), sink)
    p = jnp.exp(s - m)
    p = p / (jnp.sum(p, axis=-1, keepdims=True) + jnp.exp(sink - m))
    o = jnp.einsum('bnhgqk,bnkhd->bnqhgd', p.astype(v_band.dtype), v_band)
    return o.reshape(B, S, D_MODEL) @ w_o + b_o

def setup_inputs(seed: int = 0) -> dict:
    key = jax.random.key(seed)
    ks = iter(jax.random.split(key, 40))
    f32 = jnp.float32

    def dense(shape, fan_in):
        return jax.random.normal(next(ks), shape, f32) * (fan_in ** -0.5)

    def gain(shape):
        return 1.0 + 0.02 * jax.random.normal(next(ks), shape, f32)

    def small(shape, s):
        return s * jax.random.normal(next(ks), shape, f32)

    x = jax.random.normal(next(ks), (BATCH, SEQ, D_MODEL), f32)
    offsets = jax.random.randint(next(ks), (BATCH, 1), 0, 4096, dtype=jnp.int32)
    positions = jnp.arange(SEQ, dtype=jnp.int32)[None, :] + offsets
    return {
        "x": x,
        "positions": positions,
        "ln_ffn1": gain((DEPTH, D_MODEL)),
        "ffn1_w_gate": dense((DEPTH, D_MODEL, D_FF), D_MODEL),
        "ffn1_w_up": dense((DEPTH, D_MODEL, D_FF), D_MODEL),
        "ffn1_w_down": dense((DEPTH, D_FF, D_MODEL), D_FF),
        "ln_mix": gain((DEPTH, D_MODEL)),
        "ln_ffn2": gain((DEPTH, D_MODEL)),
        "ffn2_w_gate": dense((DEPTH, D_MODEL, D_FF), D_MODEL),
        "ffn2_w_up": dense((DEPTH, D_MODEL, D_FF), D_MODEL),
        "ffn2_w_down": dense((DEPTH, D_FF, D_MODEL), D_FF),
        "a_w_qkv": dense((N_A_LAYERS, D_MODEL, 3 * D_MODEL), D_MODEL),
        "a_w_o": dense((N_A_LAYERS, D_MODEL, D_MODEL), D_MODEL),
        "a_lambda_q1": small((N_A_LAYERS, DIFF_SUB_DIM), 0.1),
        "a_lambda_k1": small((N_A_LAYERS, DIFF_SUB_DIM), 0.1),
        "a_lambda_q2": small((N_A_LAYERS, DIFF_SUB_DIM), 0.1),
        "a_lambda_k2": small((N_A_LAYERS, DIFF_SUB_DIM), 0.1),
        "a_subln": gain((N_A_LAYERS, DIFF_V_DIM)),
        "b_w_q": dense((N_B_LAYERS, D_MODEL, D_MODEL), D_MODEL),
        "b_b_q": small((N_B_LAYERS, D_MODEL), 0.02),
        "b_sinks": small((N_B_LAYERS, SWA_Q_HEADS), 0.5),
        "b_w_o": dense((N_B_LAYERS, D_MODEL, D_MODEL), D_MODEL),
        "b_b_o": small((N_B_LAYERS, D_MODEL), 0.02),
        "kv_norm": gain((D_MODEL,)),
        "kv_w_k": dense((D_MODEL, SWA_KV_WIDTH), D_MODEL),
        "kv_b_k": small((SWA_KV_WIDTH,), 0.02),
        "kv_w_v": dense((D_MODEL, SWA_KV_WIDTH), D_MODEL),
        "kv_b_v": small((SWA_KV_WIDTH,), 0.02),
        "final_norm": gain((D_MODEL,)),
    }

def reference(x, positions, ln_ffn1, ffn1_w_gate, ffn1_w_up, ffn1_w_down, ln_mix, ln_ffn2,
              ffn2_w_gate, ffn2_w_up, ffn2_w_down, a_w_qkv, a_w_o, a_lambda_q1, a_lambda_k1,
              a_lambda_q2, a_lambda_k2, a_subln, b_w_q, b_b_q, b_sinks, b_w_o, b_b_o,
              kv_norm, kv_w_k, kv_b_k, kv_w_v, kv_b_v, final_norm):
    cos, sin = rope_tables(positions)
    h = x
    k_band = None
    v_band = None
    for layer in range(DEPTH):
        h = h + 0.5 * swiglu(rms_norm(h, ln_ffn1[layer]), ffn1_w_gate[layer],
                             ffn1_w_up[layer], ffn1_w_down[layer])
        u = rms_norm(h, ln_mix[layer])
        if layer < N_A_LAYERS:
            a = layer
            lambda_init = 0.8 - 0.6 * math.exp(-0.3 * layer)
            h = h + diff_attention(u, a_w_qkv[a], a_w_o[a], a_lambda_q1[a], a_lambda_k1[a],
                                   a_lambda_q2[a], a_lambda_k2[a], a_subln[a], cos, sin,
                                   lambda_init)
        else:
            b = layer - N_A_LAYERS
            h = h + swa_sink_attention(u, b_w_q[b], b_b_q[b], b_sinks[b], b_w_o[b], b_b_o[b],
                                       k_band, v_band, cos, sin)
        h = h + 0.5 * swiglu(rms_norm(h, ln_ffn2[layer]), ffn2_w_gate[layer],
                             ffn2_w_up[layer], ffn2_w_down[layer])
        if layer == N_A_LAYERS - 1:
            k_band, v_band = shared_kv(h, kv_norm, kv_w_k, kv_b_k, kv_w_v, kv_b_v, cos, sin)
    return rms_norm(h, final_norm)


_drawn_inputs = setup_inputs


def setup_inputs(seed=0):
    import zlib

    import numpy as np

    out = dict(_drawn_inputs(seed))
    spreads = {}
    factors = {'ln_ffn1': 4.238,
     'ln_ffn2': 6.343,
     'a_subln': 4.293,
     'b_b_q': 8.0,
     'b_sinks': 28.689,
     'b_b_o': 31.84,
     'kv_norm': 8.0,
     'kv_b_k': 59.708,
     'kv_b_v': 35.688,
     'final_norm': 7.506}
    for name, (base, spread) in spreads.items():
        noise = np.random.default_rng([zlib.crc32(name.encode()), seed]).standard_normal(out[name].shape)
        drawn = base * np.exp(spread * noise) if base else spread * noise
        out[name] = __import__('jax').numpy.asarray(drawn.astype(out[name].dtype))
    for name, factor in factors.items():
        out[name] = (out[name] * factor).astype(out[name].dtype)
    return out
```

```python
import math
from contextlib import ExitStack

import numpy as np
import concourse.bass as bass
from concourse import mybir

F32 = mybir.dt.float32
F32R = mybir.dt.float32r
BF16 = mybir.dt.bfloat16
I32 = mybir.dt.int32
ALU = mybir.AluOpType
ACT = mybir.ActivationFunctionType
AX = mybir.AxisListType

P = 128
D = 1024
SEQ = 256
FF = 2816
KT = D // P
NPOS = SEQ // P
BANK = 512
UNIT = 2048
UNITS_HELD = 4
CH = 256
N_CHUNK = FF // CH
FT = FF // P
GU_UNITS = 2 * N_CHUNK
DN_UNITS = FT // 2
FFN_UNITS = GU_UNITS + DN_UNITS
HEADS = 8
HD = 64
ROT = 16
KVW = 128
EPS = 1e-5
THETA = 500000.0
LAMBDA_INIT = 0.8 - 0.6 * math.exp(-0.3 * 0)
SCALE = HD ** -0.5
MASKED = -3.0e38

U_FFN1_0 = 0
U_QKV = U_FFN1_0 + FFN_UNITS
U_WO_A = U_QKV + 12
U_FFN2_0 = U_WO_A + 4
U_KV = U_FFN2_0 + FFN_UNITS
U_FFN1_1 = U_KV + 1
U_WQ = U_FFN1_1 + FFN_UNITS
U_WO_B = U_WQ + 4
U_FFN2_1 = U_WO_B + 4
N_UNITS = U_FFN2_1 + FFN_UNITS

VECS = ["ln_ffn1_0", "ln_mix_0", "ln_ffn2_0", "kv_norm", "ln_ffn1_1", "ln_mix_1", "b_b_q",
        "b_b_o", "ln_ffn2_1", "final_norm"]
VEC_RING = 3


class Tally:

    def __init__(self):
        self.n = {}
        self.turn = None
        self.per_turn = {}

    def next(self, key):
        self.n[key] = self.n.get(key, 0) + 1
        return self.last(key)

    def last(self, key):
        n = self.n.get(key, 0)
        if self.turn is not None and key in self.per_turn:
            return self.turn * self.per_turn[key] + n
        return n

    def enter(self, turn, per_turn):
        self.turn, self.per_turn, self.before = turn, per_turn, dict(self.n)

    def leave(self, turns):
        for key in set(self.n) | set(self.per_turn):
            grew = self.n.get(key, 0) - self.before.get(key, 0)
            assert grew == self.per_turn.get(key, 0), (key, grew)
            self.n[key] = self.n.get(key, 0) + grew * (turns - 1)
        self.turn = None


def split_2pi():
    rest, parts = 2 * math.pi, []
    for _ in range(3):
        e = math.floor(math.log2(rest)) - 11
        part = math.floor(rest / 2.0 ** e) * 2.0 ** e
        parts.append(part)
        rest -= part
    return parts + [rest]


def trunk(nc, a, out):
    with ExitStack() as ctx:
        def sb(name, shape, dt=F32):
            return ctx.enter_context(nc.sbuf_tensor(name, shape, dt))

        def sem(name):
            return ctx.enter_context(nc.semaphore(name))

        raw = sb("raw", [P, UNITS_HELD, UNIT])
        w_hi = sb("w_hi", [P, UNITS_HELD, UNIT], F32R)
        w_lo = sb("w_lo", [P, UNITS_HELD, UNIT], F32R)
        xT_hi = sb("xT_hi", [P, KT, SEQ], F32R)
        xT_lo = sb("xT_lo", [P, KT, SEQ], F32R)
        with nc.sbuf_tensor("att_1", [P, FT * SEQ], F32) as att_1:
            pass
        hT_hi = sb("hT_hi", [P, FT, SEQ], F32R)
        with nc.sbuf_tensor("att_2", [P, FT * SEQ], F32) as att_2:
            pass
        hT_lo = sb("hT_lo", [P, FT, SEQ], F32R)
        x = sb("x", [P, NPOS, D])
        xn = sb("xn", [P, NPOS, D])
        junk = sb("junk", [P, D], BF16)
        vec = sb("vec", [P, VEC_RING, D])
        silu = sb("silu", [P, NPOS, 2, CH])
        h = sb("h", [P, NPOS, 2 * CH])
        shared = sb("shared", [P, 1536])
        bkv = sb("bkv", [P, 2 * KVW])
        gsub = sb("gsub", [P, KVW])
        sinks = sb("sinks", [P, 2 * HEADS])
        negsink = sb("negsink", [P, 2 * HEADS])
        lamd = sb("lamd", [P, 2])
        lame = sb("lame", [P, 2])
        neglam = sb("neglam", [P, 1])
        pos_i = sb("pos_i", [P, NPOS], I32)
        pos_f = sb("pos_f", [P, NPOS])
        inv_freq = sb("inv_freq", [P, ROT // 2])
        ang = sb("ang", [P, NPOS, ROT // 2])
        turns = sb("turns", [P, NPOS, ROT // 2])
        fold = sb("fold", [P, 2, NPOS, ROT // 2])
        cos2 = sb("cos2", [P, NPOS, 2, ROT // 2])
        sin2 = sb("sin2", [P, NPOS, 2, ROT // 2])
        rot = sb("rot", [P, 2, 2 * HEADS, ROT])
        ident = sb("ident", [P, P])
        identb = sb("identb", [P, P], BF16)
        mask_a = sb("mask_a", [P, 2, P], BF16)
        mask_b = sb("mask_b", [P, 2, P], BF16)
        ss = sb("ss", [P, NPOS])
        ms = sb("ms", [P, NPOS])
        rstd = sb("rstd", [P, NPOS])
        mhalf = sb("mhalf", [P, HEADS])
        mx = sb("mx", [P, NPOS, HEADS, 2])
        negm = sb("negm", [P, NPOS, HEADS, 2])
        den = sb("den", [P, NPOS, HEADS, 2])
        rden = sb("rden", [P, NPOS, HEADS, 2])
        sink_e = sb("sink_e", [P, NPOS, HEADS, 2])
        coef = sb("coef", [P, NPOS, HEADS])
        oss = sb("oss", [P, NPOS, HEADS])
        oms = sb("oms", [P, NPOS, HEADS])
        orstd = sb("orstd", [P, NPOS, HEADS])

        kvb = shared[:, 0:512].rearrange("p (t n) -> p t n", t=NPOS)
        kdup = shared[:, 512:1024].rearrange("p (t g e d) -> p t g e d", t=NPOS, g=2, e=2)
        kT_b = shared[:, 1024:1536].rearrange("p (g s) -> p g s", g=2)
        a_mix = shared[:, 0:1024].rearrange("p (r n) -> p r n", r=2)
        lams = vec[:, 2, 0:4 * HD].rearrange("p (i d) -> p i d", i=4)
        lamp = vec[:, 2, 4 * HD:6 * HD].rearrange("p (i d) -> p i d", i=2)

        q_a = att_1[:, 0:2 * D].rearrange("p (t n) -> p t n", t=NPOS)
        k_a = att_1[:, 2 * D:4 * D].rearrange("p (t n) -> p t n", t=NPOS)
        v_a = att_2[:, 0:2 * D].rearrange("p (t n) -> p t n", t=NPOS)
        qT = att_2[:, 2 * D:4 * D].rearrange("p (k s) -> p k s", k=HEADS)
        kT_a = [f[:, 4 * D:5 * D].rearrange("p (k s) -> p k s", k=HEADS // 2) for f in (att_1, att_2)]
        pT = att_1[:, 0:2 * D].rearrange("p (r n) -> p r n", r=2)
        probs = [silu[:, :, :, :].rearrange("p a b n -> p (a b n)"),
                 h[:, :, :].rearrange("p a n -> p (a n)")]

        bank = [ctx.enter_context(nc.psum_tensor(f"bank{b}", [P, BANK], F32)) for b in range(8)]

        s_x = [sem(f"s_x{i}") for i in range(NPOS)]
        s_pos = sem("s_pos")
        s_small = sem("s_small")
        s_raw = [sem(f"s_raw{i}") for i in range(UNITS_HELD)]
        s_vec = [sem(f"s_vec{i}") for i in range(VEC_RING)]
        s_hi = sem("s_hi")
        s_lo = sem("s_lo")
        s_used = sem("s_used")
        s_filled = sem("s_filled")
        s_read = [sem(f"s_read{b}") for b in range(8)]
        s_ident = sem("s_ident")
        s_mask = sem("s_mask")
        s_fold = sem("s_fold")
        s_trig = sem("s_trig")
        s_table = sem("s_table")
        s_lamd = sem("s_lamd")
        s_lame = sem("s_lame")
        s_silu = sem("s_silu")
        s_hipart = sem("s_hipart")
        s_ss = sem("s_ss")
        s_rstd = sem("s_rstd")
        s_xn = sem("s_xn")
        s_dve = sem("s_dve")
        s_pool = sem("s_pool")
        s_rope = sem("s_rope")
        s_negm = sem("s_negm")
        s_mix = sem("s_mix")
        s_earg = sem("s_earg")
        s_esink = sem("s_esink")
        s_oss = sem("s_oss")
        s_orstd = sem("s_orstd")
        s_on = sem("s_on")
        s_bo = sem("s_bo")
        s_kdup = sem("s_kdup")
        s_out = sem("s_out")

        block = ctx.enter_context(nc.Block())

        def acc(pos, j):
            return 2 * pos + j

        def slot(u):
            return u % UNITS_HELD

        def own(pos):
            return slice(P * pos, P * (pos + 1))

        def per_bank(pos):
            return BANK // (P * (pos + 1))

        def rounds(pos):
            return HEADS // per_bank(pos)

        def pair(r):
            return (4, 5) if r % 2 == 0 else (6, 7)

        def round_no(pos, r):
            return r + pos * rounds(0)

        ROUNDS = rounds(0) + rounds(1)
        NORMS = ["ln_ffn1_0", "ln_mix_0", "ln_ffn2_0", "kv_norm", "ln_ffn1_1", "ln_mix_1", "ln_ffn2_1",
                 "final_norm"]

        def xn_count(name, pos):
            return NPOS * NORMS.index(name) + pos + 1

        def vec_of(name):
            n = VECS.index(name)
            return n % VEC_RING, 16 * (n // VEC_RING + 1)

        filled = {}
        FILLED_PER_TURN = 4
        taken = {}

        def in_sbuf(eng, key):
            b, n = taken[key]
            eng.wait_ge(s_read[b], n)

        LOOP_TURNS = 3

        @block.tensor
        def _(pe):
            uses = [0] * 8
            count = [0]

            def take(b, turn=None):
                if turn is not None:
                    pe.wait_ge(s_read[b], turn + uses[b])
                elif uses[b]:
                    pe.wait_ge(s_read[b], uses[b])
                uses[b] += 1

            def fill(mm, key):
                mm.then_inc(s_filled, 1)
                count[0] += 1
                filled[key] = count[0]

            def note(key, b):
                taken[key] = b, uses[b]

            def unit_ready(u, turn=None):
                pe.wait_ge(s_lo, u + 1 if turn is None else turn * UNITS_HELD + (u + 1))

            def columns_pass(u, half, pos, j, key, turn=None):
                if pos == 0:
                    unit_ready(u, turn)
                b = acc(pos, j)
                if half == 0:
                    take(b, turn)
                for k in range(4):
                    kt = 4 * half + k
                    cols = slice(BANK * k, BANK * (k + 1))
                    for i, (xs, ws) in enumerate(((xT_hi, w_hi), (xT_hi, w_lo), (xT_lo, w_hi))):
                        mm = nc.tensor.matmul(bank[b][:, :], xs[:, kt, own(pos)], ws[:, slot(u), cols],
                                              start=(kt == 0 and i == 0), stop=(kt == KT - 1 and i == 2))
                if pos == 1:
                    mm.then_inc(s_used, 1)
                elif half == 1:
                    fill(mm, key)
                if half == 1:
                    note((*key, pos), b)

            def rows_pass(u, kt0, n_kt, pos, lhs_hi, lhs_lo, key):
                if pos == 0:
                    unit_ready(u)
                if kt0 == 0:
                    take(acc(pos, 0))
                    take(acc(pos, 1))
                for k in range(2):
                    kt = kt0 + k
                    for j in range(2):
                        cols = slice(D * k + BANK * j, D * k + BANK * (j + 1))
                        for i, ws in enumerate((w_hi, w_lo)):
                            nc.tensor.matmul(bank[acc(pos, j)][:, :], lhs_hi[:, kt, own(pos)],
                                             ws[:, slot(u), cols], start=(kt == 0 and i == 0), stop=False)
                    for j in range(2):
                        cols = slice(D * k + BANK * j, D * k + BANK * (j + 1))
                        mm = nc.tensor.matmul(bank[acc(pos, j)][:, :], lhs_lo[:, kt, own(pos)],
                                              w_hi[:, slot(u), cols], start=False, stop=(kt == n_kt - 1))
                if pos == 1:
                    mm.then_inc(s_used, 1)
                elif kt == n_kt - 1:
                    fill(mm, key)
                if kt == n_kt - 1:
                    for j in range(2):
                        note((*key, pos, j), acc(pos, j))

            def transposes(srcs, b, key, turn=None):
                take(b, turn)
                for i, src in enumerate(srcs):
                    mm = nc.tensor.transpose(bank[b][:, P * i:P * (i + 1)], src, ident[:, :])
                fill(mm, key)
                note(key, b)

            def tiles(view, j):
                return [view[:, BANK * j + P * i:BANK * j + P * (i + 1)] for i in range(4)]

            def x_transposes(name, pos):
                pe.wait_ge(s_xn, xn_count(name, pos))
                for j in range(2):
                    transposes(tiles(xn[:, pos, :], j), 4 + 2 * pos + j, ("xT", name, pos, j))

            def x_ready(pos):
                for j in range(2):
                    pe.wait_ge(s_read[4 + 2 * pos + j], uses[4 + 2 * pos + j])

            def h_transposes(pos, g, turn=None, n_tiles=4):
                b = acc(pos, 1 if n_tiles == 4 else 0)
                pe.wait_ge(s_read[b], uses[b] if turn is None else turn + uses[b])
                transposes([h[:, pos, P * i:P * (i + 1)] for i in range(n_tiles)], 4 + 2 * pos,
                           ("hT", g, pos), turn)

            def ffn(f, u0, name, next_name):
                def gate_up(u, pos, j, g, turn=None):
                    for half in range(2):
                        columns_pass(u0 + u + half, half, pos, j, ("gu", f, g, j), turn)

                def turn_of(g, turn=None):
                    columns_pass(u0 + 4 * g + 2, 0, 0, 1, ("gu", f, g, 1), turn)
                    if g == 0:
                        x_transposes(name, 1)
                    columns_pass(u0 + 4 * g + 3, 1, 0, 1, ("gu", f, g, 1), turn)
                    if g == 0:
                        x_ready(1)
                    gate_up(4 * g, 1, 0, g, turn)
                    h_transposes(0, (f, g), turn)
                    gate_up(4 * g + 2, 1, 1, g, turn)
                    gate_up(4 * g + 4, 0, 0, g + 1, turn)
                    h_transposes(1, (f, g), turn)

                x_ready(0)
                gate_up(0, 0, 0, 0)
                turn_of(0)
                at = count[0], list(uses)
                with pe.Fori(0, LOOP_TURNS) as turn:
                    turn_of(1, turn)
                assert count[0] - at[0] == FILLED_PER_TURN
                count[0] += FILLED_PER_TURN * (LOOP_TURNS - 1)
                for b in range(8):
                    uses[b] += (uses[b] - at[1][b]) * (LOOP_TURNS - 1)
                turn_of(4)
                gate_up(20, 1, 0, 5)
                h_transposes(0, (f, 5), n_tiles=2)

                def down(ts, pos):
                    for i in ts:
                        if i == DN_UNITS - 1:
                            pe.wait_ge(s_read[4 + 2 * pos], h_read[pos])
                        rows_pass(u0 + GU_UNITS + i, 2 * i, FT, pos, hT_hi, hT_lo, ("down", f))

                h_read = [uses[4], uses[6] + 1]
                pe.wait_ge(s_read[4], uses[4] - 1)
                down((0, 1), 0)
                h_transposes(1, (f, 5), n_tiles=2)
                down((2,), 0)
                pe.wait_ge(s_read[6], uses[6] - 1)
                down((0, 1, 2), 1)
                down((3, 4, 5, 6), 0)
                down((3, 4, 5, 6), 1)
                down((7, 8, 9, 10), 0)
                down((7, 8, 9), 1)
                if next_name:
                    x_transposes(next_name, 0)
                down((10,), 1)

            def scores(layer, pos, r):
                n, keys = per_bank(pos), P * (pos + 1)
                mask = mask_a if layer == 0 else mask_b
                mask = mask[:, 1 - pos:2, :].rearrange("p b k -> p (b k)").unsqueeze(1).to_broadcast([P, n, keys])
                for b in pair(r):
                    take(b)
                    nc.tensor.matmul(bank[b][:, :].rearrange("p (n k) -> p n k", n=n), identb[:, :], mask,
                                     start=True, stop=False, skip_group_check=True)
                for i in range(n):
                    head = n * r + i
                    for c, b in enumerate(pair(r)):
                        rows = slice(HD * c, HD * (c + 1))
                        kT = kT_a[head // 4][rows, head % 4, 0:keys] if layer == 0 else kT_b[rows, head // 4, 0:keys]
                        mm = nc.tensor.matmul(bank[b][:, keys * i:keys * (i + 1)], qT[rows, head, own(pos)], kT,
                                              start=False, stop=(i == n - 1), skip_group_check=True)
                        if i == n - 1:
                            fill(mm, ("scores", layer, pos, r, c))
                            note(("scores", layer, pos, r, c), b)

            def p_transposes(layer, pos, r):
                n, nk = per_bank(pos), pos + 1
                if layer == 0:
                    pe.wait_ge(s_mix, round_no(pos, r) + 1)
                    transposes(tiles(a_mix[:, r % 2, :], 0), pair(r)[1], ("pT", 0, pos, r, 1))
                    return
                in_sbuf(pe, ("scores", 1, pos, r, 1))
                view = probs[r % 2].rearrange("p (i c k q) -> p i c k q", i=n, c=2, k=nk)
                for c, b in enumerate(pair(r)):
                    transposes([view[:, i, c, k, :] for i in range(n) for k in range(nk)], b,
                               ("pT", 1, pos, r, c))

            def values(layer, pos, r):
                n, nk = per_bank(pos), pos + 1
                for c in (1,) if layer == 0 else (0, 1):
                    in_sbuf(pe, ("pT", layer, pos, r, c))
                if r == 0 and layer == 0:
                    for j in range(2):
                        in_sbuf(pe, ("qkv", 2, j, pos))
                for i in range(n):
                    head = n * r + i
                    j = head // 4
                    if head % 4 == 0:
                        take(acc(pos, j))
                    for c in range(1 if layer == 0 else 2):
                        for k in range(nk):
                            if layer == 0:
                                lhsT = pT[:, r % 2, P * (nk * i + k):P * (nk * i + k + 1)]
                                v = v_a[:, k, KVW * head:KVW * (head + 1)]
                                o = bank[acc(pos, j)][:, KVW * (head % 4):KVW * (head % 4 + 1)]
                            else:
                                lhsT = pT[:, r % 2, BANK * c + P * (nk * i + k):BANK * c + P * (nk * i + k + 1)]
                                v = kvb[:, k, KVW + HD * j:KVW + HD * (j + 1)]
                                at = HD * (2 * (head % 4) + c)
                                o = bank[acc(pos, j)][:, at:at + HD]
                            mm = nc.tensor.matmul(o, lhsT, v, start=(k == 0), stop=(k == nk - 1))
                    if head % 4 == 3:
                        fill(mm, ("o", layer, pos, j))
                        note(("o", layer, pos, j), acc(pos, j))

            def o_transposes(layer, pos, banks):
                if layer == 0:
                    pe.wait_ge(s_on, pos + 1)
                for j, b in enumerate(banks):
                    if layer == 1:
                        in_sbuf(pe, ("o", 1, pos, j))
                    transposes(tiles(xn[:, pos, :], j), b, ("oT", layer, pos, j))

            def attend(layer, u_wo, next_name):
                scores(layer, 1, 0)
                for r in range(rounds(0)):
                    values(layer, 0, r)
                scores(layer, 1, 1)
                p_transposes(layer, 1, 0)
                scores(layer, 1, 2)
                o_transposes(layer, 0, (acc(1, 0), acc(1, 1)))

                def wo(i, pos):
                    if i == 0:
                        for j in range(2):
                            in_sbuf(pe, ("oT", layer, pos, j))
                    rows_pass(u_wo + i, 2 * i, KT, pos, xT_hi, xT_lo, ("wo", layer))

                wo(0, 0)
                p_transposes(layer, 1, 1)
                values(layer, 1, 0)
                scores(layer, 1, 3)
                wo(1, 0)
                p_transposes(layer, 1, 2)
                values(layer, 1, 1)
                wo(2, 0)
                p_transposes(layer, 1, 3)
                values(layer, 1, 2)
                wo(3, 0)
                values(layer, 1, 3)
                o_transposes(layer, 1, (6, 7))
                for i in range(3):
                    wo(i, 1)
                x_transposes(next_name, 0)
                wo(3, 1)

            pe.wait_ge(s_ident, 2)
            x_transposes("ln_ffn1_0", 0)
            ffn(0, U_FFN1_0, "ln_ffn1_0", "ln_mix_0")

            x_ready(0)
            for part in range(3):
                u0 = U_QKV + 4 * part
                for pos in range(NPOS):
                    for i in range(4):
                        if part == 0 and pos == 0 and i == 3:
                            x_transposes("ln_mix_0", 1)
                        if part == 0 and pos == 1 and i == 0:
                            x_ready(1)
                        columns_pass(u0 + i, i % 2, pos, i // 2, ("qkv", part, i // 2))
                        if part == 2 and (pos, i) in ((0, 0), (0, 1), (0, 2), (1, 0)):
                            which, at = {(0, 0): (0, 0), (0, 1): (0, 1), (0, 2): (1, 0), (1, 0): (1, 1)}[pos, i]
                            pe.wait_ge(s_rope, 2 * which + at + 1)
                            src = (q_a, k_a)[which][:, at, :]
                            for j in range(2):
                                transposes(tiles(src, j), 4 + 2 * at + j, ("qkT", which, at, j))
                        if part == 2 and pos == 1 and i == 1:
                            pe.wait_ge(s_mask, 4)
                            for which in range(2):
                                for at in range(NPOS):
                                    for j in range(2):
                                        in_sbuf(pe, ("qkT", which, at, j))
                            for r in range(rounds(0)):
                                scores(0, 0, r)
                        if part == 2 and pos == 1 and i >= 2:
                            p_transposes(0, 0, i - 2)
            attend(0, U_WO_A, "ln_ffn2_0")
            ffn(1, U_FFN2_0, "ln_ffn2_0", "kv_norm")

            def kv_pass(pos):
                if pos == 0:
                    unit_ready(U_KV)
                take(acc(pos, 1))
                note(("kv", pos), acc(pos, 1))
                w = 2 * KVW
                for kt in range(KT):
                    cols = slice(w * kt, w * (kt + 1))
                    for i, (xs, ws) in enumerate(((xT_hi, w_hi), (xT_hi, w_lo), (xT_lo, w_hi))):
                        mm = nc.tensor.matmul(bank[acc(pos, 1)][:, 0:w], xs[:, kt, own(pos)],
                                              ws[:, slot(U_KV), cols],
                                              start=(kt == 0 and i == 0), stop=(kt == KT - 1 and i == 2))
                if pos == 0:
                    fill(mm, ("kv",))
                else:
                    mm.then_inc(s_used, 1)

            x_ready(0)
            kv_pass(0)
            x_transposes("kv_norm", 1)
            x_ready(1)
            kv_pass(1)
            x_transposes("ln_ffn1_1", 0)
            ffn(2, U_FFN1_1, "ln_ffn1_1", "ln_mix_1")

            x_ready(0)
            for pos in range(NPOS):
                for i in range(4):
                    if pos == 0 and i == 2:
                        pe.wait_ge(s_kdup, 2)
                        transposes([kdup[:, t, g, :, :].rearrange("p e d -> p (e d)")
                                    for g in range(2) for t in range(NPOS)], 4, ("kT",))
                    if pos == 0 and i == 3:
                        x_transposes("ln_mix_1", 1)
                    if pos == 1 and i == 0:
                        x_ready(1)
                    columns_pass(U_WQ + i, i % 2, pos, i // 2, ("q_b", i // 2))
                    if pos == 1 and i == 1:
                        pe.wait_ge(s_rope, 5)
                        for j in range(2):
                            transposes(tiles(xn[:, 0, :], j), 6 + j, ("qT_b", 0, j))
                    if pos == 1 and i == 2:
                        in_sbuf(pe, ("kT",))
                        for j in range(2):
                            in_sbuf(pe, ("qT_b", 0, j))
                        for r in range(rounds(0)):
                            scores(1, 0, r)
            p_transposes(1, 0, 0)
            pe.wait_ge(s_rope, 6)
            for j in range(2):
                transposes(tiles(xn[:, 1, :], j), acc(1, j), ("qT_b", 1, j))
            p_transposes(1, 0, 1)
            for j in range(2):
                in_sbuf(pe, ("qT_b", 1, j))
            attend(1, U_WO_B, "ln_ffn2_1")
            ffn(3, U_FFN2_1, "ln_ffn2_1", None)

        @block.sync
        def _(sp):
            def load(u, parts, turn=None):
                if u >= UNITS_HELD:
                    n = u - UNITS_HELD + 1
                    sp.wait_ge(s_lo, n if turn is None else turn * UNITS_HELD + n)
                for dst, src in parts:
                    sp.dma_start(dst, src).then_inc(s_raw[slot(u)], 16)

            def gate_up(u0, w_gate, w_up, l):
                gate = w_gate[l].rearrange("(k p) f -> p k f", p=P)
                up = w_up[l].rearrange("(k p) f -> p k f", p=P)

                def unit(u, half, col, turn=None):
                    dst = raw[:, slot(u), :].rearrange("p (k g c) -> p k g c", k=4, g=2)
                    load(u, [(dst[:, :, i, :], w[:, 4 * half:4 * half + 4, bass.ds(col, CH)])
                             for i, w in enumerate((gate, up))], turn)

                for k in range(4):
                    unit(u0 + k, k % 2, CH * (k // 2))
                with sp.Fori(0, 4) as turn:
                    for k in range(4):
                        unit(u0 + 4 + k, k % 2, turn * (2 * CH) + CH * (2 + k // 2), turn)
                for k in range(2):
                    unit(u0 + 20 + k, k, CH * (N_CHUNK - 1))

            def rows(u0, n, w):
                view = w.rearrange("(k p) n -> p k n", p=P)
                for i in range(n):
                    dst = raw[:, slot(u0 + i), :].rearrange("p (k n) -> p k n", k=2)
                    load(u0 + i, [(dst[:, k, :], view[:, 2 * i + k, :]) for k in range(2)])

            def columns(u0, n_chunks, w):
                view = w.rearrange("(k p) n -> p k n", p=P)
                for c in range(n_chunks):
                    for half in range(2):
                        u = u0 + 2 * c + half
                        dst = raw[:, slot(u), :].rearrange("p (k n) -> p k n", k=4)
                        load(u, [(dst[:, 2 * i:2 * i + 2, :],
                                  view[:, 4 * half + 2 * i:4 * half + 2 * i + 2, BANK * c:BANK * (c + 1)])
                                 for i in range(2)])

            def vector(name):
                src = {"ln_ffn1_0": a["ln_ffn1"][0:1], "ln_mix_0": a["ln_mix"][0:1],
                       "ln_ffn2_0": a["ln_ffn2"][0:1], "kv_norm": a["kv_norm"].unsqueeze(0),
                       "ln_ffn1_1": a["ln_ffn1"][1:2], "ln_mix_1": a["ln_mix"][1:2],
                       "b_b_q": a["b_b_q"][0:1], "b_b_o": a["b_b_o"][0:1],
                       "ln_ffn2_1": a["ln_ffn2"][1:2], "final_norm": a["final_norm"].unsqueeze(0)}[name]
                n = VECS.index(name)
                if n == 2:
                    sp.wait_ge(s_lamd, 1)
                elif n >= VEC_RING:
                    before = VECS[n - VEC_RING]
                    if before == "b_b_q":
                        in_sbuf(sp, ("q_b", 1, 1))
                    else:
                        sp.wait_ge(s_xn, xn_count(before, 1))
                sp.dma_start(vec[:, n % VEC_RING, :], src.to_broadcast([P, D])).then_inc(s_vec[n % VEC_RING], 16)

            for pos in range(NPOS):
                sp.dma_start(x[:, pos, :], a["x"][0, own(pos), :]).then_inc(s_x[pos], 16)
                if pos == 0:
                    vector("ln_ffn1_0")
            gate_up(U_FFN1_0, a["ffn1_w_gate"], a["ffn1_w_up"], 0)
            vector("ln_mix_0")
            vector("ln_ffn2_0")
            vector("kv_norm")
            rows(U_FFN1_0 + GU_UNITS, DN_UNITS, a["ffn1_w_down"][0])
            columns(U_QKV, 6, a["a_w_qkv"][0])
            rows(U_WO_A, 4, a["a_w_o"][0])
            vector("ln_ffn1_1")
            gate_up(U_FFN2_0, a["ffn2_w_gate"], a["ffn2_w_up"], 0)
            vector("ln_mix_1")
            rows(U_FFN2_0 + GU_UNITS, DN_UNITS, a["ffn2_w_down"][0])
            dst = raw[:, slot(U_KV), :].rearrange("p (k g c) -> p k g c", k=KT, g=2)
            load(U_KV, [(dst[:, :, i, :], a[w].rearrange("(k p) n -> p k n", p=P))
                        for i, w in enumerate(("kv_w_k", "kv_w_v"))])
            gate_up(U_FFN1_1, a["ffn1_w_gate"], a["ffn1_w_up"], 1)
            vector("b_b_q")
            vector("b_b_o")
            rows(U_FFN1_1 + GU_UNITS, DN_UNITS, a["ffn1_w_down"][1])
            columns(U_WQ, 2, a["b_w_q"][0])
            rows(U_WO_B, 4, a["b_w_o"][0])
            vector("ln_ffn2_1")
            gate_up(U_FFN2_1, a["ffn2_w_gate"], a["ffn2_w_up"], 1)
            vector("final_norm")
            rows(U_FFN2_1 + GU_UNITS, DN_UNITS, a["ffn2_w_down"][1])
            for pos in range(NPOS):
                sp.wait_ge(s_xn, xn_count("final_norm", pos))
                sp.dma_start(out[0, own(pos), :], xn[:, pos, :]).then_inc(s_out, 16)
            sp.wait_ge(s_out, 16 * NPOS)

        @block.gpsimd
        def _(pool):
            t = Tally()

            def link(ins):
                ins.then_inc(s_pool, 1)
                pool.wait_ge(s_pool, t.next("pool"))

            for pos in range(NPOS):
                pool.dma_start(pos_i[:, pos:pos + 1], a["positions"][0, own(pos)].unsqueeze(1)).then_inc(s_pos, 16)
            for i, name in enumerate(("a_lambda_q1", "a_lambda_k1", "a_lambda_q2", "a_lambda_k2")):
                pool.dma_start(lams[:, i, :], a[name][0:1].to_broadcast([P, HD])).then_inc(s_small, 16)
            pool.dma_start(gsub[:, :], a["a_subln"][0:1].to_broadcast([P, KVW])).then_inc(s_small, 16)
            pool.dma_start(sinks[:, :], a["b_sinks"][0:1].to_broadcast([P, 2 * HEADS])).then_inc(s_small, 16)
            for i, name in enumerate(("kv_b_k", "kv_b_v")):
                pool.dma_start(bkv[:, KVW * i:KVW * (i + 1)],
                               a[name].unsqueeze(0).to_broadcast([P, KVW])).then_inc(s_small, 16)

            link(nc.gpsimd.memset(ident[:, :], 0.0))
            nc.gpsimd.affine_select(out=ident[:, :], in_=ident[:, :], compare_op=ALU.not_equal, fill=1.0,
                                    base=0, pattern=[[-1, P]], channel_multiplier=1).then_inc(s_ident, 1)
            nc.gpsimd.memset(mhalf[:, :], -0.5).then_inc(s_ident, 1)
            pool.wait_ge(s_ident, 2)

            def norm_scale(pos):
                pool.wait_ge(s_ss, t.next("ss"))
                link(nc.gpsimd.tensor_scalar(ms[:, pos:pos + 1], ss[:, pos:pos + 1], 1.0 / D, EPS,
                                             ALU.mult, ALU.add))
                nc.gpsimd.tensor_tensor(rstd[:, pos:pos + 1], ms[:, pos:pos + 1], mhalf[:, 0:1],
                                        ALU.pow).then_inc(s_rstd, 1)

            norm_scale(0)
            norm_scale(1)

            for m in (identb[:, :], mask_a[:, :, :], mask_b[:, :, :]):
                link(nc.gpsimd.memset(m, 0.0))
            nc.gpsimd.affine_select(out=identb[:, :], in_=identb[:, :], compare_op=ALU.not_equal, fill=1.0,
                                    base=0, pattern=[[-1, P]], channel_multiplier=1).then_inc(s_mask, 1)
            for m in (mask_a, mask_b):
                nc.gpsimd.affine_select(out=m[:, 1, :], in_=m[:, 1, :], compare_op=ALU.is_ge, fill=MASKED,
                                        base=0, pattern=[[-1, P]], channel_multiplier=1).then_inc(s_mask, 1)
            nc.gpsimd.affine_select(out=mask_b[:, 0, :], in_=mask_b[:, 0, :], compare_op=ALU.is_gt, fill=MASKED,
                                    base=0, pattern=[[1, P]], channel_multiplier=-1).then_inc(s_mask, 1)

            def rope(view, n, pos):
                half = ROT // 2
                c = cos2[:, pos, :, :].rearrange("p a b -> p (a b)").unsqueeze(1).to_broadcast([P, n, ROT])
                straight, crossed = rot[:, 0, 0:n, :], rot[:, 1, 0:n, :]
                if t.last("rope"):
                    pool.wait_ge(s_rope, t.last("rope"))
                nc.gpsimd.tensor_tensor(straight, view[:, :, 0:ROT], c, ALU.mult).then_inc(s_pool, 1)
                t.next("pool")
                for i in range(2):
                    nc.gpsimd.tensor_tensor(crossed[:, :, half * i:half * (i + 1)],
                                            view[:, :, half * (1 - i):half * (2 - i)],
                                            sin2[:, pos, i:i + 1, :].to_broadcast([P, n, half]),
                                            ALU.mult).then_inc(s_pool, 1)
                    t.next("pool")
                pool.wait_ge(s_pool, t.last("pool"))
                return nc.gpsimd.tensor_tensor(view[:, :, 0:ROT], straight, crossed, ALU.add)

            norm_scale(0)
            norm_scale(1)
            pool.wait_ge(s_table, 3)
            for which, view in enumerate((q_a, k_a)):
                for pos in range(NPOS):
                    for j in range(2):
                        in_sbuf(pool, ("qkv", which, j, pos))
                    rope(view[:, pos, :].rearrange("p (g d) -> p g d", d=HD), 2 * HEADS, pos).then_inc(s_rope, 1)
                    t.next("rope")

            def sub_norm_scale(pos):
                pool.wait_ge(s_oss, pos + 1)
                link(nc.gpsimd.tensor_scalar(oms[:, pos, :], oss[:, pos, :], 1.0 / (2 * HD), EPS,
                                             ALU.mult, ALU.add))
                nc.gpsimd.tensor_tensor(orstd[:, pos, :], oms[:, pos, :], mhalf[:, :], ALU.pow).then_inc(s_orstd, 1)

            sub_norm_scale(0)
            norm_scale(0)
            sub_norm_scale(1)
            norm_scale(1)
            norm_scale(0)
            norm_scale(1)
            for pos in range(NPOS):
                in_sbuf(pool, ("kv", pos))
                keys = kvb[:, pos, 0:KVW].rearrange("p (g d) -> p g d", d=HD)
                link(rope(keys, 2, pos))
                for e in range(2):
                    ins = nc.gpsimd.tensor_copy(kdup[:, pos, :, e, :], keys)
                ins.then_inc(s_kdup, 1)
            norm_scale(0)
            norm_scale(1)
            for pos in range(NPOS):
                for j in range(2):
                    in_sbuf(pool, ("q_b", j, pos))
                rope(xn[:, pos, :].rearrange("p (g d) -> p g d", d=HD), 2 * HEADS, pos).then_inc(s_rope, 1)
                t.next("rope")
            v, n = vec_of("b_b_o")
            pool.wait_ge(s_vec[v], n)
            for pos in range(NPOS):
                nc.gpsimd.tensor_tensor(x[:, pos, :], x[:, pos, :], vec[:, v, :], ALU.add).then_inc(s_bo, 1)
            for _ in range(2):
                norm_scale(0)
                norm_scale(1)

        @block.scalar
        def _(act):
            def split(u, turn=None):
                if u >= N_UNITS:
                    return
                grow = 0 if turn is None else turn
                act.wait_ge(s_raw[slot(u)], 32 * (u // UNITS_HELD + 1) + (grow * 32 if turn is not None else 0))
                if u >= UNITS_HELD:
                    n = u - UNITS_HELD + 1
                    act.wait_ge(s_used, n if turn is None else turn * UNITS_HELD + n)
                nc.scalar.activation(w_hi[:, slot(u), :], raw[:, slot(u), :], ACT.Copy).then_inc(s_hi, 1)

            t = Tally()

            def junk_free():
                for key, done in (("ss", s_ss), ("oss", s_oss)):
                    if t.last(key):
                        act.wait_ge(done, t.last(key))

            def square(pos, key=None):
                if key is None:
                    act.wait_ge(s_x[pos], 16)
                else:
                    in_sbuf(act, (*key, pos, 1))
                junk_free()
                t.next("ss")
                nc.scalar.activation(junk[:, :], x[:, pos, :], ACT.Square,
                                     accum_out=ss[:, pos:pos + 1]).then_inc(s_ss, 1)

            def hi_part(dst, b, key, n_tiles=4, turn=None):
                act.wait_ge(s_filled, filled[key] if turn is None else turn * FILLED_PER_TURN + filled[key])
                src = bank[b][:, 0:P * n_tiles].rearrange("p (k s) -> p k s", k=n_tiles)
                nc.scalar.activation(dst, src, ACT.Copy).then_inc(s_hipart, 1)

            def x_hi(name, pos):
                for j in range(2):
                    hi_part(xT_hi[:, 4 * j:4 * j + 4, own(pos)], 4 + 2 * pos + j, ("xT", name, pos, j))

            def o_hi(layer, pos, banks):
                for j, b in enumerate(banks):
                    hi_part(xT_hi[:, 4 * j:4 * j + 4, own(pos)], b, ("oT", layer, pos, j))

            def ffn(f, u0, name):
                def silu_gate(pos, j, g, turn=None):
                    if pos == 0:
                        n = filled["gu", f, g, j]
                        act.wait_ge(s_filled, n if turn is None else turn * FILLED_PER_TURN + n)
                    else:
                        n = u0 + 4 * g + 2 * j + 2
                        act.wait_ge(s_used, n if turn is None else turn * UNITS_HELD + n)
                    nc.scalar.activation(silu[:, pos, j, :], bank[acc(pos, j)][:, 0:CH], ACT.Silu).then_inc(s_silu, 1)

                def h_hi(pos, g, turn=None, n_tiles=4):
                    k0 = 4 * g if turn is None else turn * 4 + 4 * g
                    hi_part(hT_hi[:, bass.ds(k0, n_tiles), own(pos)], 4 + 2 * pos, ("hT", (f, g), pos),
                            n_tiles, turn)

                def turn_of(g, turn=None):
                    if g == 0:
                        x_hi(name, 1)
                    silu_gate(0, 1, g, turn)
                    split(u0 + 4 * g + 4, turn)
                    split(u0 + 4 * g + 5, turn)
                    silu_gate(1, 0, g, turn)
                    h_hi(0, g, turn)
                    split(u0 + 4 * g + 6, turn)
                    split(u0 + 4 * g + 7, turn)
                    silu_gate(1, 1, g, turn)
                    silu_gate(0, 0, g + 1, turn)
                    h_hi(1, g, turn)

                silu_gate(0, 0, 0)
                turn_of(0)
                with act.Fori(0, LOOP_TURNS) as turn:
                    turn_of(1, turn)
                turn_of(4)
                split(u0 + 24)
                split(u0 + 25)
                silu_gate(1, 0, 5)
                h_hi(0, 5, n_tiles=2)
                h_hi(1, 5, n_tiles=2)
                for i in range(26, 33):
                    split(u0 + i)

            def boundary(key, u0, name):
                square(0, key)
                split(u0)
                split(u0 + 1)
                x_hi(name, 0)
                split(u0 + 2)
                split(u0 + 3)
                square(1, key)

            def copy_bank(dst, b, sem_full, n):
                act.wait_ge(sem_full, n)
                return nc.scalar.activation(dst, bank[b][:, :], ACT.Copy)

            def transposed(dst, b, key):
                copy_bank(dst, b, s_filled, filled[key]).then_inc(s_read[b], 1)

            def exps(layer, pos, r):
                act.wait_ge(s_negm, ROUNDS * layer + round_no(pos, r) + 1)
                n, keys = per_bank(pos), P * (pos + 1)
                p = probs[r % 2].rearrange("p (i c k) -> p i c k", i=n, c=2)
                for c, b in enumerate(pair(r)):
                    for i in range(n):
                        head = n * r + i
                        ins = nc.scalar.activation(p[:, i, c, :], bank[b][:, keys * i:keys * (i + 1)], ACT.Exp,
                                                   bias=negm[:, pos, head, c:c + 1], scale=SCALE,
                                                   accum_out=den[:, pos, head, c:c + 1])
                    ins.then_inc(s_read[b], 1)

            for pos in range(NPOS):
                square(pos)
            split(0)
            split(1)
            x_hi("ln_ffn1_0", 0)
            split(2)
            split(3)
            act.wait_ge(s_fold, 2)
            nc.scalar.activation(cos2[:, :, 0, :], fold[:, 1, :, :], ACT.Sin).then_inc(s_trig, 1)
            nc.scalar.activation(sin2[:, :, 1, :], fold[:, 0, :, :], ACT.Sin).then_inc(s_trig, 1)
            act.wait_ge(s_lamd, 1)
            nc.scalar.activation(lame[:, :], lamd[:, :], ACT.Exp).then_inc(s_lame, 1)
            ffn(0, U_FFN1_0, "ln_ffn1_0")
            boundary(("down", 0), U_QKV, "ln_mix_0")

            def projection(part, pos, j, dst):
                if pos == 0:
                    ins = copy_bank(dst, acc(0, j), s_filled, filled["qkv", part, j])
                else:
                    ins = copy_bank(dst, acc(1, j), s_used, U_QKV + 4 * part + 2 * j + 2)
                ins.then_inc(s_read[acc(pos, j)], 1)

            u_v = U_QKV + 8
            projection(0, 0, 0, q_a[:, 0, 0:BANK])
            x_hi("ln_mix_0", 1)
            projection(0, 0, 1, q_a[:, 0, BANK:D])
            split(U_QKV + 4)
            split(U_QKV + 5)
            projection(0, 1, 0, q_a[:, 1, 0:BANK])
            split(U_QKV + 6)
            split(U_QKV + 7)
            projection(0, 1, 1, q_a[:, 1, BANK:D])
            projection(1, 0, 0, k_a[:, 0, 0:BANK])
            projection(1, 0, 1, k_a[:, 0, BANK:D])
            split(u_v)
            split(u_v + 1)
            projection(1, 1, 0, k_a[:, 1, 0:BANK])
            split(u_v + 2)
            split(u_v + 3)
            projection(1, 1, 1, k_a[:, 1, BANK:D])

            def qk_transposed(which, pos):
                for j in range(2):
                    dst = qT[:, 4 * j:4 * j + 4, own(pos)] if which == 0 else kT_a[j][:, :, own(pos)]
                    transposed(dst, 4 + 2 * pos + j, ("qkT", which, pos, j))

            qk_transposed(0, 0)
            projection(2, 0, 0, v_a[:, 0, 0:BANK])
            qk_transposed(0, 1)
            qk_transposed(1, 0)
            projection(2, 0, 1, v_a[:, 0, BANK:D])
            split(U_WO_A)
            qk_transposed(1, 1)
            split(U_WO_A + 1)
            projection(2, 1, 0, v_a[:, 1, 0:BANK])
            exps(0, 0, 0)
            exps(0, 0, 1)
            split(U_WO_A + 2)
            split(U_WO_A + 3)
            projection(2, 1, 1, v_a[:, 1, BANK:D])

            def o_squares(pos):
                in_sbuf(act, ("o", 0, pos, 1))
                junk_free()
                t.next("oss")
                for head in range(HEADS):
                    ins = nc.scalar.activation(junk[:, KVW * head:KVW * (head + 1)],
                                               xn[:, pos, KVW * head:KVW * (head + 1)], ACT.Square,
                                               accum_out=oss[:, pos, head:head + 1])
                ins.then_inc(s_oss, 1)

            def sink_exp(pos):
                act.wait_ge(s_earg, pos + 1)
                nc.scalar.activation(sink_e[:, pos, :, :], sink_e[:, pos, :, :], ACT.Exp).then_inc(s_esink, 1)

            def attend(layer, u_next, name):
                key = ("wo", layer)
                exps(layer, 1, 0)
                if layer == 0:
                    o_squares(0)
                exps(layer, 1, 1)
                exps(layer, 1, 2)
                o_hi(layer, 0, (acc(1, 0), acc(1, 1)))
                exps(layer, 1, 3)
                if layer == 1:
                    sink_exp(1)
                square(0, key)
                if layer == 0:
                    o_squares(1)
                o_hi(layer, 1, (6, 7))
                split(u_next)
                split(u_next + 1)
                x_hi(name, 0)
                split(u_next + 2)
                split(u_next + 3)
                square(1, key)

            attend(0, U_FFN2_0, "ln_ffn2_0")
            ffn(1, U_FFN2_0, "ln_ffn2_0")
            boundary(("down", 1), U_KV, "kv_norm")
            x_hi("kv_norm", 1)
            x_hi("ln_ffn1_1", 0)
            split(U_FFN1_1 + 3)
            ffn(2, U_FFN1_1, "ln_ffn1_1")
            boundary(("down", 2), U_WQ, "ln_mix_1")
            transposed(kT_b.rearrange("p g s -> p (g s)"), 4, ("kT",))
            x_hi("ln_mix_1", 1)
            split(U_WO_B)
            split(U_WO_B + 1)
            for j in range(2):
                transposed(qT[:, 4 * j:4 * j + 4, own(0)], 6 + j, ("qT_b", 0, j))
            split(U_WO_B + 2)
            exps(1, 0, 0)
            exps(1, 0, 1)
            sink_exp(0)
            split(U_WO_B + 3)
            for j in range(2):
                transposed(qT[:, 4 * j:4 * j + 4, own(1)], acc(1, j), ("qT_b", 1, j))
            attend(1, U_FFN2_1, "ln_ffn2_1")
            ffn(3, U_FFN2_1, "ln_ffn2_1")
            for pos in range(NPOS):
                square(pos, ("down", 3))

        @block.vector
        def _(dve):
            t = Tally()

            def link(ins):
                ins.then_inc(s_dve, 1)
                dve.wait_ge(s_dve, t.next("dve"))

            def split(u, turn=None):
                if u >= N_UNITS:
                    return
                dve.wait_ge(s_hi, u + 1 if turn is None else turn * UNITS_HELD + (u + 1))
                nc.vector.tensor_tensor(w_lo[:, slot(u), :], raw[:, slot(u), :],
                                        w_hi[:, slot(u), :].bitcast(F32), ALU.subtract).then_inc(s_lo, 1)

            def lo_part(dst, hi, b, n_tiles=4):
                dve.wait_ge(s_hipart, t.next("hipart"))
                src = bank[b][:, 0:P * n_tiles].rearrange("p (k s) -> p k s", k=n_tiles)
                nc.vector.tensor_tensor(dst, src, hi.bitcast(F32), ALU.subtract).then_inc(s_read[b], 1)

            def x_lo(pos, banks=None):
                for j, b in enumerate(banks or (4 + 2 * pos, 5 + 2 * pos)):
                    lo_part(xT_lo[:, 4 * j:4 * j + 4, own(pos)], xT_hi[:, 4 * j:4 * j + 4, own(pos)], b)

            def norm(name, pos, fresh=True):
                if fresh:
                    dve.wait_ge(s_rstd, t.next("rstd"))
                v, n = vec_of(name)
                dve.wait_ge(s_vec[v], n)
                nc.vector.scalar_tensor_tensor(out=xn[:, pos, :], in0=x[:, pos, :], scalar=rstd[:, pos:pos + 1],
                                               in1=vec[:, v, :], op0=ALU.mult, op1=ALU.mult).then_inc(s_xn, 1)

            def residual(key, pos, scale, u_last):
                if pos == 0:
                    dve.wait_ge(s_filled, filled[key])
                else:
                    dve.wait_ge(s_used, u_last + 1)
                for j in range(2):
                    cols = slice(BANK * j, BANK * (j + 1))
                    nc.vector.scalar_tensor_tensor(out=x[:, pos, cols], in0=bank[acc(pos, j)][:, :], scalar=scale,
                                                   in1=x[:, pos, cols], op0=ALU.mult,
                                                   op1=ALU.add).then_inc(s_read[acc(pos, j)], 1)

            def boundary(key, u_last, u0, name, scale=0.5):
                residual(key, 0, scale, u_last)
                norm(name, 0)
                split(u0)
                split(u0 + 1)
                x_lo(0)
                residual(key, 1, scale, u_last)
                split(u0 + 2)
                split(u0 + 3)
                norm(name, 1)

            def ffn(f, u0):
                def mul(pos, j, turn=None):
                    dve.wait_ge(s_silu, t.next("silu"))
                    b = acc(pos, j)
                    nc.vector.tensor_tensor(h[:, pos, CH * j:CH * (j + 1)], silu[:, pos, j, :], bank[b][:, CH:2 * CH],
                                            ALU.mult).then_inc(s_read[b], 1)

                def h_lo(pos, g, turn=None, n_tiles=4):
                    k0 = 4 * g if turn is None else turn * 4 + 4 * g
                    tile = bass.ds(k0, n_tiles)
                    lo_part(hT_lo[:, tile, own(pos)], hT_hi[:, tile, own(pos)], 4 + 2 * pos, n_tiles)

                def turn_of(g, turn=None):
                    if g == 0:
                        x_lo(1)
                    mul(0, 1)
                    split(u0 + 4 * g + 4, turn)
                    split(u0 + 4 * g + 5, turn)
                    mul(1, 0)
                    h_lo(0, g, turn)
                    split(u0 + 4 * g + 6, turn)
                    split(u0 + 4 * g + 7, turn)
                    mul(1, 1)
                    mul(0, 0)
                    h_lo(1, g, turn)

                mul(0, 0)
                turn_of(0)
                with dve.Fori(0, LOOP_TURNS) as turn:
                    t.enter(turn, {"silu": 4, "hipart": 2})
                    turn_of(1, turn)
                t.leave(LOOP_TURNS)
                turn_of(4)
                split(u0 + 24)
                split(u0 + 25)
                mul(1, 0)
                h_lo(0, 5, n_tiles=2)
                h_lo(1, 5, n_tiles=2)
                for i in range(26, 33):
                    split(u0 + i)

            def maxima(layer, pos, r):
                n, keys = per_bank(pos), P * (pos + 1)
                heads = slice(n * r, n * (r + 1))
                for c, b in enumerate(pair(r)):
                    dve.wait_ge(s_filled, filled["scores", layer, pos, r, c])
                    nc.vector.tensor_reduce(mx[:, pos, heads, c], bank[b][:, :].rearrange("p (i k) -> p i k", i=n),
                                            AX.X, ALU.max).then_inc(s_dve, 1)
                    t.next("dve")
                dve.wait_ge(s_dve, t.last("dve"))
                if layer == 0:
                    ins = nc.vector.tensor_scalar(negm[:, pos, heads, :], mx[:, pos, heads, :], -SCALE, None, ALU.mult)
                else:
                    sink = negsink[:, :].rearrange("p (h c) -> p h c", c=2)
                    ins = nc.vector.scalar_tensor_tensor(out=negm[:, pos, heads, :], in0=mx[:, pos, heads, :],
                                                         scalar=-SCALE, in1=sink[:, heads, :],
                                                         op0=ALU.mult, op1=ALU.min)
                ins.then_inc(s_negm, 1)

            def combine(pos, r):
                n, keys = per_bank(pos), P * (pos + 1)
                heads = slice(n * r, n * (r + 1))
                in_sbuf(dve, ("scores", 0, pos, r, 1))
                link(nc.vector.reciprocal(rden[:, pos, heads, :], den[:, pos, heads, :]))
                link(nc.vector.scalar_tensor_tensor(out=coef[:, pos, heads], in0=den[:, pos, heads, 0],
                                                    scalar=neglam[:, 0:1], in1=rden[:, pos, heads, 1],
                                                    op0=ALU.mult, op1=ALU.mult))
                p = probs[r % 2].rearrange("p (i c k) -> p i c k", i=n, c=2)
                for i in range(n):
                    head = n * r + i
                    ins = nc.vector.scalar_tensor_tensor(out=a_mix[:, r % 2, keys * i:keys * (i + 1)],
                                                         in0=p[:, i, 1, :], scalar=coef[:, pos, head:head + 1],
                                                         in1=p[:, i, 0, :], op0=ALU.mult, op1=ALU.add)
                ins.then_inc(s_mix, 1)

            def p_transposed(layer, pos, r):
                for c in (1,) if layer == 0 else (0, 1):
                    b = pair(r)[c]
                    dve.wait_ge(s_filled, filled["pT", layer, pos, r, c])
                    at = 0 if layer == 0 else BANK * c
                    nc.vector.tensor_copy(pT[:, r % 2, at:at + BANK], bank[b][:, :]).then_inc(s_read[b], 1)

            def output(layer, pos):
                if layer == 1:
                    dve.wait_ge(s_esink, pos + 1)
                    link(nc.vector.tensor_tensor(den[:, pos, :, :], den[:, pos, :, :], sink_e[:, pos, :, :], ALU.add))
                    link(nc.vector.reciprocal(rden[:, pos, :, :], den[:, pos, :, :]))
                for j in range(2):
                    b = acc(pos, j)
                    dve.wait_ge(s_filled, filled["o", layer, pos, j])
                    if layer == 0:
                        w, r = 2 * HD, rden[:, pos, 4 * j:4 * j + 4, 0]
                    else:
                        w, r = HD, rden[:, pos, 4 * j:4 * j + 4, :].rearrange("p h c -> p (h c)")
                    n = BANK // w
                    nc.vector.tensor_tensor(
                        xn[:, pos, BANK * j:BANK * (j + 1)].rearrange("p (n d) -> p n d", n=n),
                        bank[b][:, :].rearrange("p (n d) -> p n d", n=n),
                        r.unsqueeze(2).to_broadcast([P, n, w]), ALU.mult).then_inc(s_read[b], 1)

            def sub_norm(pos):
                o = xn[:, pos, :].rearrange("p (h d) -> p h d", h=HEADS)
                dve.wait_ge(s_orstd, pos + 1)
                link(nc.vector.tensor_tensor(o, o, orstd[:, pos, :].unsqueeze(2).to_broadcast([P, HEADS, KVW]),
                                             ALU.mult))
                nc.vector.tensor_tensor(o, o, gsub[:, :].unsqueeze(1).to_broadcast([P, HEADS, KVW]),
                                        ALU.mult).then_inc(s_on, 1)

            norm("ln_ffn1_0", 0)
            split(0)
            split(1)
            x_lo(0)
            norm("ln_ffn1_0", 1)
            split(2)
            split(3)

            for i in range(ROT // 2):
                freq = float(np.float32(THETA ** (-2.0 * i / ROT)))
                nc.vector.memset(inv_freq[:, i:i + 1], freq).then_inc(s_dve, 1)
                t.next("dve")
            dve.wait_ge(s_pos, 32)
            link(nc.vector.tensor_copy(pos_f[:, :], pos_i[:, :]))
            for pos in range(NPOS):
                link(nc.vector.tensor_scalar(ang[:, pos, :], inv_freq[:, :], pos_f[:, pos:pos + 1], None, ALU.mult))
            NEAREST = 1.5 * 2.0 ** 23
            for unit in (4096.0, 1.0):
                link(nc.vector.tensor_scalar(turns[:, :, :], ang[:, :, :], 1.0 / (2 * math.pi * unit), NEAREST,
                                             ALU.mult, ALU.add))
                link(nc.vector.tensor_scalar(turns[:, :, :], turns[:, :, :], -NEAREST, None, ALU.add))
                for part in split_2pi():
                    link(nc.vector.scalar_tensor_tensor(out=ang[:, :, :], in0=turns[:, :, :], scalar=-part * unit,
                                                        in1=ang[:, :, :], op0=ALU.mult, op1=ALU.add))
            PI = 3.1415925
            nc.vector.tensor_scalar(fold[:, 0, :, :], ang[:, :, :], PI, -PI, ALU.min, ALU.max).then_inc(s_fold, 1)
            link(nc.vector.scalar_tensor_tensor(out=turns[:, :, :], in0=ang[:, :, :], scalar=-1.0, in1=ang[:, :, :],
                                                op0=ALU.mult, op1=ALU.max))
            nc.vector.tensor_scalar(fold[:, 1, :, :], turns[:, :, :], -1.0, math.pi / 2,
                                    ALU.mult, ALU.add).then_inc(s_fold, 1)
            dve.wait_ge(s_small, 16 * 8)
            pairs = lams.rearrange("p (i e) d -> p i e d", e=2)
            link(nc.vector.tensor_tensor(lamp, pairs[:, :, 0, :], pairs[:, :, 1, :], ALU.mult))
            nc.vector.tensor_reduce(lamd[:, :], lamp, AX.X, ALU.add).then_inc(s_lamd, 1)
            nc.vector.tensor_scalar(gsub[:, :], gsub[:, :], 1.0 - LAMBDA_INIT, None, ALU.mult)
            nc.vector.tensor_scalar(negsink[:, :], sinks[:, :], -1.0, None, ALU.mult)
            dve.wait_ge(s_trig, 2)
            nc.vector.tensor_copy(cos2[:, :, 1, :], cos2[:, :, 0, :]).then_inc(s_table, 1)
            nc.vector.tensor_scalar(sin2[:, :, 0, :], sin2[:, :, 1, :], -1.0, None, ALU.mult).then_inc(s_table, 1)
            dve.wait_ge(s_lame, 1)
            nc.vector.scalar_tensor_tensor(out=neglam[:, :], in0=lame[:, 1:2], scalar=LAMBDA_INIT, in1=lame[:, 0:1],
                                           op0=ALU.subtract, op1=ALU.subtract).then_inc(s_table, 1)
            dve.wait_ge(s_table, 3)
            ffn(0, U_FFN1_0)
            boundary(("down", 0), U_QKV - 1, U_QKV, "ln_mix_0")

            x_lo(1)
            for i in range(4, 14):
                split(U_QKV + i)
            for r in range(rounds(0)):
                maxima(0, 0, r)
            for r in range(rounds(0)):
                combine(0, r)
            for r in range(rounds(0)):
                split(U_WO_A + 2 + r)
                p_transposed(0, 0, r)
            maxima(0, 1, 0)
            output(0, 0)
            maxima(0, 1, 1)
            combine(1, 0)
            p_transposed(0, 1, 0)
            sub_norm(0)
            maxima(0, 1, 2)
            x_lo(0, (acc(1, 0), acc(1, 1)))
            combine(1, 1)
            p_transposed(0, 1, 1)
            maxima(0, 1, 3)
            combine(1, 2)
            p_transposed(0, 1, 2)
            combine(1, 3)
            p_transposed(0, 1, 3)
            residual(("wo", 0), 0, 1.0, None)
            output(0, 1)
            norm("ln_ffn2_0", 0)
            sub_norm(1)
            x_lo(1, (6, 7))
            split(U_FFN2_0)
            split(U_FFN2_0 + 1)
            x_lo(0)
            residual(("wo", 0), 1, 1.0, U_FFN2_0 - 1)
            split(U_FFN2_0 + 2)
            split(U_FFN2_0 + 3)
            norm("ln_ffn2_0", 1)

            ffn(1, U_FFN2_0)
            boundary(("down", 1), U_KV - 1, U_KV, "kv_norm")

            def add_bias(dst, key, pos, b, w, bias, u_last):
                if pos == 0:
                    dve.wait_ge(s_filled, filled[key])
                else:
                    dve.wait_ge(s_used, u_last + 1)
                nc.vector.tensor_tensor(dst, bank[b][:, 0:w], bias, ALU.add).then_inc(s_read[b], 1)

            norm("ln_ffn1_1", 0, fresh=False)
            x_lo(1)
            add_bias(kvb[:, 0, :], ("kv",), 0, acc(0, 1), 2 * KVW, bkv[:, :], None)
            norm("ln_ffn1_1", 1, fresh=False)
            add_bias(kvb[:, 1, :], ("kv",), 1, acc(1, 1), 2 * KVW, bkv[:, :], U_KV)
            x_lo(0)
            split(U_FFN1_1 + 3)
            ffn(2, U_FFN1_1)
            boundary(("down", 2), U_WQ - 1, U_WQ, "ln_mix_1")

            v, n = vec_of("b_b_q")
            dve.wait_ge(s_vec[v], n)

            def queries(pos, j):
                cols = slice(BANK * j, BANK * (j + 1))
                add_bias(xn[:, pos, cols], ("q_b", j), pos, acc(pos, j), BANK, vec[:, v, cols], U_WQ + 2 * j + 1)

            def sink_minus_max(pos):
                nc.vector.tensor_tensor(sink_e[:, pos, :, :], negm[:, pos, :, :],
                                        sinks[:, :].rearrange("p (h c) -> p h c", c=2), ALU.add).then_inc(s_earg, 1)

            queries(0, 0)
            x_lo(1)
            queries(0, 1)
            split(U_WO_B)
            split(U_WO_B + 1)
            queries(1, 0)
            split(U_WO_B + 2)
            for r in range(rounds(0)):
                maxima(1, 0, r)
            dve.wait_ge(s_negm, ROUNDS + rounds(0))
            sink_minus_max(0)
            queries(1, 1)
            split(U_WO_B + 3)
            for r in range(rounds(0)):
                p_transposed(1, 0, r)
            maxima(1, 1, 0)
            output(1, 0)
            maxima(1, 1, 1)
            p_transposed(1, 1, 0)
            maxima(1, 1, 2)
            x_lo(0, (acc(1, 0), acc(1, 1)))
            p_transposed(1, 1, 1)
            maxima(1, 1, 3)
            dve.wait_ge(s_negm, 2 * ROUNDS)
            sink_minus_max(1)
            p_transposed(1, 1, 2)
            p_transposed(1, 1, 3)
            dve.wait_ge(s_bo, 2)
            residual(("wo", 1), 0, 1.0, None)
            output(1, 1)
            x_lo(1, (6, 7))
            norm("ln_ffn2_1", 0)
            split(U_FFN2_1)
            split(U_FFN2_1 + 1)
            x_lo(0)
            residual(("wo", 1), 1, 1.0, U_FFN2_1 - 1)
            split(U_FFN2_1 + 2)
            split(U_FFN2_1 + 3)
            norm("ln_ffn2_1", 1)

            ffn(3, U_FFN2_1)
            for pos in range(NPOS):
                residual(("down", 3), pos, 0.5, N_UNITS - 1)
                norm("final_norm", pos)


_INS = ["x", "positions", "ln_ffn1", "ffn1_w_gate", "ffn1_w_up", "ffn1_w_down", "ln_mix", "ln_ffn2",
        "ffn2_w_gate", "ffn2_w_up", "ffn2_w_down", "a_w_qkv", "a_w_o", "a_lambda_q1", "a_lambda_k1",
        "a_lambda_q2", "a_lambda_k2", "a_subln", "b_w_q", "b_b_q", "b_sinks", "b_w_o", "b_b_o", "kv_norm",
        "kv_w_k", "kv_b_k", "kv_w_v", "kv_b_v", "final_norm"]


def kernel(**inputs):
    import concourse.bacc as bacc
    from concourse.bass_utils import run_bass_kernel_spmd

    nc = bacc.Bacc("TRN2", target_bir_lowering=False, num_devices=1)
    arrays, args = {}, {}
    for name in _INS:
        arr = np.ascontiguousarray(inputs[name])
        arrays[f"in_{name}"] = arr
        args[name] = nc.dram_tensor(f"in_{name}", arr.shape, mybir.dt.from_np(arr.dtype), kind="ExternalInput").ap()
    out = nc.dram_tensor("out_h", (1, SEQ, D), F32, kind="ExternalOutput").ap()
    trunk(nc, args, out)
    r = run_bass_kernel_spmd(nc, [arrays], core_ids=[0])
    return r.results[0]["out_h"]
```

```python
import math
from contextlib import ExitStack

import numpy as np
import concourse.bass as bass
from concourse import mybir

F32 = mybir.dt.float32
F32R = mybir.dt.float32r
BF16 = mybir.dt.bfloat16
I32 = mybir.dt.int32
ALU = mybir.AluOpType
ACT = mybir.ActivationFunctionType
AX = mybir.AxisListType

P = 128
D = 1024
SEQ = 256
FF = 2816
KT = D // P
NPOS = SEQ // P
BANK = 512
UNIT = 2048
UNITS_HELD = 4
CH = 256
N_CHUNK = FF // CH
FT = FF // P
GU_UNITS = 2 * N_CHUNK
DN_UNITS = FT // 2
FFN_UNITS = GU_UNITS + DN_UNITS
HEADS = 8
HD = 64
ROT = 16
KVW = 128
EPS = 1e-5
THETA = 500000.0
LAMBDA_INIT = 0.8 - 0.6 * math.exp(-0.3 * 0)
SCALE = HD ** -0.5
MASKED = -3.0e38

U_FFN1_0 = 0
U_QKV = U_FFN1_0 + FFN_UNITS
U_WO_A = U_QKV + 12
U_FFN2_0 = U_WO_A + 4
U_KV = U_FFN2_0 + FFN_UNITS
U_FFN1_1 = U_KV + 1
U_WQ = U_FFN1_1 + FFN_UNITS
U_WO_B = U_WQ + 4
U_FFN2_1 = U_WO_B + 4
N_UNITS = U_FFN2_1 + FFN_UNITS

VECS = ["ln_ffn1_0", "ln_mix_0", "ln_ffn2_0", "kv_norm", "ln_ffn1_1", "ln_mix_1", "b_b_q",
        "b_b_o", "ln_ffn2_1", "final_norm"]
VEC_RING = 3


class Tally:

    def __init__(self):
        self.n = {}
        self.turn = None
        self.per_turn = {}

    def next(self, key):
        self.n[key] = self.n.get(key, 0) + 1
        return self.last(key)

    def last(self, key):
        n = self.n.get(key, 0)
        if self.turn is not None and key in self.per_turn:
            return self.turn * self.per_turn[key] + n
        return n

    def enter(self, turn, per_turn):
        self.turn, self.per_turn, self.before = turn, per_turn, dict(self.n)

    def leave(self, turns):
        for key in set(self.n) | set(self.per_turn):
            grew = self.n.get(key, 0) - self.before.get(key, 0)
            assert grew == self.per_turn.get(key, 0), (key, grew)
            self.n[key] = self.n.get(key, 0) + grew * (turns - 1)
        self.turn = None


def split_2pi():
    rest, parts = 2 * math.pi, []
    for _ in range(3):
        e = math.floor(math.log2(rest)) - 11
        part = math.floor(rest / 2.0 ** e) * 2.0 ** e
        parts.append(part)
        rest -= part
    return parts + [rest]


def trunk(nc, a, out):
    with ExitStack() as ctx:
        def sb(name, shape, dt=F32):
            return ctx.enter_context(nc.sbuf_tensor(name, shape, dt))

        def sem(name):
            return ctx.enter_context(nc.semaphore(name))

        raw = sb("raw", [P, UNITS_HELD, UNIT])
        w_hi = sb("w_hi", [P, UNITS_HELD, UNIT], F32R)
        w_lo = sb("w_lo", [P, UNITS_HELD, UNIT], F32R)
        xT_hi = sb("xT_hi", [P, KT, SEQ], F32R)
        xT_lo = sb("xT_lo", [P, KT, SEQ], F32R)
        with nc.sbuf_tensor("att_1", [P, FT * SEQ], F32) as att_1:
            pass
        hT_hi = sb("hT_hi", [P, FT, SEQ], F32R)
        with nc.sbuf_tensor("att_2", [P, FT * SEQ], F32) as att_2:
            pass
        hT_lo = sb("hT_lo", [P, FT, SEQ], F32R)
        x = sb("x", [P, NPOS, D])
        xn = sb("xn", [P, NPOS, D])
        junk = sb("junk", [P, D], BF16)
        vec = sb("vec", [P, VEC_RING, D])
        silu = sb("silu", [P, NPOS, 2, CH])
        h = sb("h", [P, NPOS, 2 * CH])
        shared = sb("shared", [P, 1536])
        bkv = sb("bkv", [P, 2 * KVW])
        gsub = sb("gsub", [P, KVW])
        sinks = sb("sinks", [P, 2 * HEADS])
        negsink = sb("negsink", [P, 2 * HEADS])
        lamd = sb("lamd", [P, 2])
        lame = sb("lame", [P, 2])
        neglam = sb("neglam", [P, 1])
        pos_i = sb("pos_i", [P, NPOS], I32)
        pos_f = sb("pos_f", [P, NPOS])
        inv_freq = sb("inv_freq", [P, ROT // 2])
        ang = sb("ang", [P, NPOS, ROT // 2])
        turns = sb("turns", [P, NPOS, ROT // 2])
        whole = sb("whole", [P, NPOS, ROT // 2])
        half_sin = sb("half_sin", [P, NPOS, ROT // 2])
        cos2 = sb("cos2", [P, NPOS, 2, ROT // 2])
        sin2 = sb("sin2", [P, NPOS, 2, ROT // 2])
        rot = sb("rot", [P, 2, 2 * HEADS, ROT])
        ident = sb("ident", [P, P])
        identb = sb("identb", [P, P], BF16)
        mask_a = sb("mask_a", [P, 2, P], BF16)
        mask_b = sb("mask_b", [P, 2, P], BF16)
        ss = sb("ss", [P, NPOS])
        ss_part = sb("ss_part", [P, 2])
        ms = sb("ms", [P, NPOS])
        rstd = sb("rstd", [P, NPOS])
        mhalf = sb("mhalf", [P, HEADS])
        mx = sb("mx", [P, NPOS, HEADS, 2])
        negm = sb("negm", [P, NPOS, HEADS, 2])
        den = sb("den", [P, NPOS, HEADS, 2])
        rden = sb("rden", [P, NPOS, HEADS, 2])
        sink_e = sb("sink_e", [P, NPOS, HEADS, 2])
        coef = sb("coef", [P, NPOS, HEADS])
        oss = sb("oss", [P, NPOS, HEADS])
        oms = sb("oms", [P, NPOS, HEADS])
        orstd = sb("orstd", [P, NPOS, HEADS])

        kvb = shared[:, 0:512].rearrange("p (t n) -> p t n", t=NPOS)
        kdup = shared[:, 512:1024].rearrange("p (t g e d) -> p t g e d", t=NPOS, g=2, e=2)
        kT_b = shared[:, 1024:1536].rearrange("p (g s) -> p g s", g=2)
        a_mix = shared[:, 0:1024].rearrange("p (r n) -> p r n", r=2)
        lams = vec[:, 2, 0:4 * HD].rearrange("p (i d) -> p i d", i=4)
        lamp = vec[:, 2, 4 * HD:6 * HD].rearrange("p (i d) -> p i d", i=2)

        q_a = att_1[:, 0:2 * D].rearrange("p (t n) -> p t n", t=NPOS)
        k_a = att_1[:, 2 * D:4 * D].rearrange("p (t n) -> p t n", t=NPOS)
        v_a = att_2[:, 0:2 * D].rearrange("p (t n) -> p t n", t=NPOS)
        qT = att_2[:, 2 * D:4 * D].rearrange("p (k s) -> p k s", k=HEADS)
        kT_a = [f[:, 4 * D:5 * D].rearrange("p (k s) -> p k s", k=HEADS // 2) for f in (att_1, att_2)]
        pT = att_1[:, 0:2 * D].rearrange("p (r n) -> p r n", r=2)
        probs = [silu[:, :, :, :].rearrange("p a b n -> p (a b n)"),
                 h[:, :, :].rearrange("p a n -> p (a n)")]

        bank = [ctx.enter_context(nc.psum_tensor(f"bank{b}", [P, BANK], F32)) for b in range(8)]

        s_x = [sem(f"s_x{i}") for i in range(NPOS)]
        s_pos = sem("s_pos")
        s_small = sem("s_small")
        s_raw = [sem(f"s_raw{i}") for i in range(UNITS_HELD)]
        s_gate0 = sem("s_gate0")
        s_gate0_hi = sem("s_gate0_hi")
        s_vec = [sem(f"s_vec{i}") for i in range(VEC_RING)]
        s_hi = sem("s_hi")
        s_lo = sem("s_lo")
        s_used = sem("s_used")
        s_filled = sem("s_filled")
        s_read = [sem(f"s_read{b}") for b in range(8)]
        s_ident = sem("s_ident")
        s_mask = sem("s_mask")
        s_fold = sem("s_fold")
        s_trig = sem("s_trig")
        s_table = sem("s_table")
        s_lamd = sem("s_lamd")
        s_lame = sem("s_lame")
        s_res = sem("s_res")
        s_silu = sem("s_silu")
        s_hipart = sem("s_hipart")
        s_ss = sem("s_ss")
        s_rstd = sem("s_rstd")
        s_xn = sem("s_xn")
        s_dve = sem("s_dve")
        s_pool = sem("s_pool")
        s_rope = sem("s_rope")
        s_negm = sem("s_negm")
        s_mix = sem("s_mix")
        s_earg = sem("s_earg")
        s_esink = sem("s_esink")
        s_oss = sem("s_oss")
        s_orstd = sem("s_orstd")
        s_on = sem("s_on")
        s_bo = sem("s_bo")
        s_kdup = sem("s_kdup")
        s_out = sem("s_out")

        block = ctx.enter_context(nc.Block())

        def acc(pos, j):
            return 2 * pos + j

        def slot(u):
            return u % UNITS_HELD

        def own(pos):
            return slice(P * pos, P * (pos + 1))

        def per_bank(pos):
            return BANK // (P * (pos + 1))

        def rounds(pos):
            return HEADS // per_bank(pos)

        def pair(r):
            return (4, 5) if r % 2 == 0 else (6, 7)

        def round_no(pos, r):
            return r + pos * rounds(0)

        ROUNDS = rounds(0) + rounds(1)
        NORMS = ["ln_ffn1_0", "ln_mix_0", "ln_ffn2_0", "kv_norm", "ln_ffn1_1", "ln_mix_1", "ln_ffn2_1",
                 "final_norm"]

        def xn_count(name, pos):
            return NPOS * NORMS.index(name) + pos + 1

        def vec_of(name):
            n = VECS.index(name)
            return n % VEC_RING, 16 * (n // VEC_RING + 1)

        filled = {}
        FILLED_PER_TURN = 4
        taken = {}

        def in_sbuf(eng, key):
            b, n = taken[key]
            eng.wait_ge(s_read[b], n)

        LOOP_TURNS = 3
        TABLES = 5

        def half_of(view, i):
            return view[:, 0, :].rearrange("p (k g c) -> p k g c", k=4, g=2)[:, :, i, :]

        @block.tensor
        def _(pe):
            uses = [0] * 8
            count = [0]

            def take(b, turn=None):
                if turn is not None:
                    pe.wait_ge(s_read[b], turn + uses[b])
                elif uses[b]:
                    pe.wait_ge(s_read[b], uses[b])
                uses[b] += 1

            def fill(mm, key):
                mm.then_inc(s_filled, 1)
                count[0] += 1
                filled[key] = count[0]

            def note(key, b):
                taken[key] = b, uses[b]

            def unit_ready(u, turn=None):
                pe.wait_ge(s_lo, u + 1 if turn is None else turn * UNITS_HELD + (u + 1))

            def columns_pass(u, half, pos, j, key, turn=None):
                if pos == 0:
                    unit_ready(u, turn)
                b = acc(pos, j)
                if half == 0:
                    take(b, turn)
                for k in range(4):
                    kt = 4 * half + k
                    cols = slice(BANK * k, BANK * (k + 1))
                    for i, (xs, ws) in enumerate(((xT_hi, w_hi), (xT_hi, w_lo), (xT_lo, w_hi))):
                        mm = nc.tensor.matmul(bank[b][:, :], xs[:, kt, own(pos)], ws[:, slot(u), cols],
                                              start=(kt == 0 and i == 0), stop=(kt == KT - 1 and i == 2))
                if pos == 1:
                    mm.then_inc(s_used, 1)
                elif half == 1:
                    fill(mm, key)
                if half == 1:
                    note((*key, pos), b)

            def last_rows_pass(u, kt0, key):
                for j in range(2):
                    for k in range(2):
                        kt = kt0 + k
                        cols = slice(D * k + BANK * j, D * k + BANK * (j + 1))
                        for i, (lhs, ws) in enumerate(((hT_hi, w_hi), (hT_hi, w_lo), (hT_lo, w_hi))):
                            mm = nc.tensor.matmul(bank[acc(1, j)][:, :], lhs[:, kt, own(1)], ws[:, slot(u), cols],
                                                  start=False, stop=(k == 1 and i == 2))
                    if j == 0:
                        fill(mm, (*key, 0))
                    note((*key, 1, j), acc(1, j))
                mm.then_inc(s_used, 1)

            def rows_pass(u, kt0, n_kt, pos, lhs_hi, lhs_lo, key):
                if pos == 0:
                    unit_ready(u)
                if kt0 == 0:
                    take(acc(pos, 0))
                    take(acc(pos, 1))
                for k in range(2):
                    kt = kt0 + k
                    for j in range(2):
                        cols = slice(D * k + BANK * j, D * k + BANK * (j + 1))
                        for i, ws in enumerate((w_hi, w_lo)):
                            nc.tensor.matmul(bank[acc(pos, j)][:, :], lhs_hi[:, kt, own(pos)],
                                             ws[:, slot(u), cols], start=(kt == 0 and i == 0), stop=False)
                    for j in range(2):
                        cols = slice(D * k + BANK * j, D * k + BANK * (j + 1))
                        mm = nc.tensor.matmul(bank[acc(pos, j)][:, :], lhs_lo[:, kt, own(pos)],
                                              w_hi[:, slot(u), cols], start=False, stop=(kt == n_kt - 1))
                if pos == 1:
                    mm.then_inc(s_used, 1)
                elif kt == n_kt - 1:
                    fill(mm, key)
                if kt == n_kt - 1:
                    for j in range(2):
                        note((*key, pos, j), acc(pos, j))

            def transposes(srcs, b, key, turn=None):
                take(b, turn)
                for i, src in enumerate(srcs):
                    mm = nc.tensor.transpose(bank[b][:, P * i:P * (i + 1)], src, ident[:, :])
                fill(mm, key)
                note(key, b)

            def tiles(view, j):
                return [view[:, BANK * j + P * i:BANK * j + P * (i + 1)] for i in range(4)]

            def x_transposes(name, pos):
                pe.wait_ge(s_xn, xn_count(name, pos))
                for j in range(2):
                    transposes(tiles(xn[:, pos, :], j), 4 + 2 * pos + j, ("xT", name, pos, j))

            def x_ready(pos):
                for j in range(2):
                    pe.wait_ge(s_read[4 + 2 * pos + j], uses[4 + 2 * pos + j])

            def h_transposes(pos, g, turn=None, n_tiles=4):
                b = acc(pos, 1 if n_tiles == 4 else 0)
                pe.wait_ge(s_read[b], uses[b] if turn is None else turn + uses[b])
                transposes([h[:, pos, P * i:P * (i + 1)] for i in range(n_tiles)], 4 + 2 * pos,
                           ("hT", g, pos), turn)

            def ffn(f, u0, name, next_name):
                def gate_up(u, pos, j, g, turn=None):
                    for half in range(2):
                        columns_pass(u0 + u + half, half, pos, j, ("gu", f, g, j), turn)

                def turn_of(g, turn=None):
                    columns_pass(u0 + 4 * g + 2, 0, 0, 1, ("gu", f, g, 1), turn)
                    if g == 0:
                        x_transposes(name, 1)
                    columns_pass(u0 + 4 * g + 3, 1, 0, 1, ("gu", f, g, 1), turn)
                    if g == 0:
                        x_ready(1)
                    gate_up(4 * g, 1, 0, g, turn)
                    h_transposes(0, (f, g), turn)
                    gate_up(4 * g + 2, 1, 1, g, turn)
                    gate_up(4 * g + 4, 0, 0, g + 1, turn)
                    h_transposes(1, (f, g), turn)

                x_ready(0)
                gate_up(0, 0, 0, 0)
                turn_of(0)
                at = count[0], list(uses)
                with pe.Fori(0, LOOP_TURNS) as turn:
                    turn_of(1, turn)
                assert count[0] - at[0] == FILLED_PER_TURN
                count[0] += FILLED_PER_TURN * (LOOP_TURNS - 1)
                for b in range(8):
                    uses[b] += (uses[b] - at[1][b]) * (LOOP_TURNS - 1)
                turn_of(4)
                gate_up(20, 1, 0, 5)
                h_transposes(0, (f, 5), n_tiles=2)

                def down(ts, pos):
                    for i in ts:
                        if i == DN_UNITS - 1:
                            pe.wait_ge(s_read[4 + 2 * pos], h_read[pos])
                        rows_pass(u0 + GU_UNITS + i, 2 * i, FT, pos, hT_hi, hT_lo, ("down", f))

                h_read = [uses[4], uses[6] + 1]
                pe.wait_ge(s_read[4], uses[4] - 1)
                down((0, 1), 0)
                h_transposes(1, (f, 5), n_tiles=2)
                down((2,), 0)
                pe.wait_ge(s_read[6], uses[6] - 1)
                down((0, 1, 2), 1)
                down((3, 4, 5, 6), 0)
                down((3, 4, 5, 6), 1)
                down((7, 8, 9, 10), 0)
                down((7, 8, 9), 1)
                if next_name:
                    x_transposes(next_name, 0)
                    down((10,), 1)
                else:
                    last_rows_pass(u0 + FFN_UNITS - 1, FT - 2, ("down", f))

            def scores(layer, pos, r):
                if layer == 1 and pos == 1 and r == 2:
                    in_sbuf(pe, ("qT_b", 1, 1))
                n, keys = per_bank(pos), P * (pos + 1)
                mask = mask_a if layer == 0 else mask_b
                mask = mask[:, 1 - pos:2, :].rearrange("p b k -> p (b k)").unsqueeze(1).to_broadcast([P, n, keys])
                for b in pair(r):
                    take(b)
                    nc.tensor.matmul(bank[b][:, :].rearrange("p (n k) -> p n k", n=n), identb[:, :], mask,
                                     start=True, stop=False, skip_group_check=True)
                for i in range(n):
                    head = n * r + i
                    for c, b in enumerate(pair(r)):
                        rows = slice(HD * c, HD * (c + 1))
                        kT = kT_a[head // 4][rows, head % 4, 0:keys] if layer == 0 else kT_b[rows, head // 4, 0:keys]
                        mm = nc.tensor.matmul(bank[b][:, keys * i:keys * (i + 1)], qT[rows, head, own(pos)], kT,
                                              start=False, stop=(i == n - 1), skip_group_check=True)
                        if i == n - 1:
                            fill(mm, ("scores", layer, pos, r, c))
                            note(("scores", layer, pos, r, c), b)

            def p_transposes(layer, pos, r):
                n, nk = per_bank(pos), pos + 1
                if layer == 0:
                    pe.wait_ge(s_mix, round_no(pos, r) + 1)
                    transposes(tiles(a_mix[:, r % 2, :], 0), pair(r)[1], ("pT", 0, pos, r, 1))
                    return
                in_sbuf(pe, ("scores", 1, pos, r, 1))
                view = probs[r % 2].rearrange("p (i c k q) -> p i c k q", i=n, c=2, k=nk)
                for c, b in enumerate(pair(r)):
                    transposes([view[:, i, c, k, :] for i in range(n) for k in range(nk)], b,
                               ("pT", 1, pos, r, c))

            def values(layer, pos, r):
                n, nk = per_bank(pos), pos + 1
                for c in (1,) if layer == 0 else (0, 1):
                    in_sbuf(pe, ("pT", layer, pos, r, c))
                if layer == 0 and r % (rounds(pos) // 2) == 0:
                    in_sbuf(pe, ("qkv", 2, 2 * r // rounds(pos), pos))
                for i in range(n):
                    head = n * r + i
                    j = head // 4
                    if head % 4 == 0:
                        take(acc(pos, j))
                    for c in range(1 if layer == 0 else 2):
                        for k in range(nk):
                            if layer == 0:
                                lhsT = pT[:, r % 2, P * (nk * i + k):P * (nk * i + k + 1)]
                                v = v_a[:, k, KVW * head:KVW * (head + 1)]
                                o = bank[acc(pos, j)][:, KVW * (head % 4):KVW * (head % 4 + 1)]
                            else:
                                lhsT = pT[:, r % 2, BANK * c + P * (nk * i + k):BANK * c + P * (nk * i + k + 1)]
                                v = kvb[:, k, KVW + HD * j:KVW + HD * (j + 1)]
                                at = HD * (2 * (head % 4) + c)
                                o = bank[acc(pos, j)][:, at:at + HD]
                            mm = nc.tensor.matmul(o, lhsT, v, start=(k == 0), stop=(k == nk - 1))
                    if head % 4 == 3:
                        fill(mm, ("o", layer, pos, j))
                        note(("o", layer, pos, j), acc(pos, j))

            def o_transposes(layer, pos, banks):
                if layer == 0:
                    pe.wait_ge(s_on, pos + 1)
                for j, b in enumerate(banks):
                    if layer == 1:
                        in_sbuf(pe, ("o", 1, pos, j))
                    transposes(tiles(xn[:, pos, :], j), b, ("oT", layer, pos, j))

            def attend(layer, u_wo, next_name):
                def wo(i, pos):
                    if i == 0:
                        for j in range(2):
                            in_sbuf(pe, ("oT", layer, pos, j))
                    rows_pass(u_wo + i, 2 * i, KT, pos, xT_hi, xT_lo, ("wo", layer))

                p_transposes(layer, 1, 0)
                if layer == 1:
                    q_transposes(1, 1, acc(1, 1))
                    o_transposes(1, 0, (acc(0, 0), acc(0, 1)))
                values(layer, 1, 0)
                scores(layer, 1, 2)
                p_transposes(layer, 1, 1)
                values(layer, 1, 1)
                scores(layer, 1, 3)
                if layer == 0:
                    o_transposes(0, 0, (acc(0, 0), acc(0, 1)))
                p_transposes(layer, 1, 2)
                wo(0, 0)
                values(layer, 1, 2)
                p_transposes(layer, 1, 3)
                wo(1, 0)
                values(layer, 1, 3)
                wo(2, 0)
                o_transposes(layer, 1, (6, 7))
                wo(3, 0)
                for i in range(3):
                    wo(i, 1)
                x_transposes(next_name, 0)
                wo(3, 1)

            def q_transposes(pos, j, b):
                pe.wait_ge(s_rope, 4 + 2 * pos + j + 1)
                transposes(tiles(xn[:, pos, :], j), b, ("qT_b", pos, j))

            def warm(n):
                for _ in range(n):
                    nc.tensor.transpose(bank[7][:, 0:P], ident[:, :], ident[:, :])

            pe.wait_ge(s_ident, 2)
            warm(28)
            x_transposes("ln_ffn1_0", 0)
            warm(12)
            ffn(0, U_FFN1_0, "ln_ffn1_0", "ln_mix_0")

            x_ready(0)
            for part in range(3):
                u0 = U_QKV + 4 * part
                for pos in range(NPOS):
                    for i in range(4):
                        if part == 0 and pos == 0 and i == 3:
                            x_transposes("ln_mix_0", 1)
                        if part == 0 and pos == 1 and i == 0:
                            x_ready(1)
                        columns_pass(u0 + i, i % 2, pos, i // 2, ("qkv", part, i // 2))
                        if part < 2:
                            continue
                        if pos == 0 and i < 3:
                            for which, at in (((0, 0), (0, 1)), ((1, 0),), ((1, 1),))[i]:
                                pe.wait_ge(s_rope, 2 * which + at + 1)
                                for j in range(2):
                                    transposes(tiles((q_a, k_a)[which][:, at, :], j), 4 + 2 * at + j,
                                               ("qkT", which, at, j))
                        if (pos, i) == (0, 3):
                            pe.wait_ge(s_mask, 4)
                            for which in range(2):
                                for at in range(NPOS):
                                    for j in range(2):
                                        in_sbuf(pe, ("qkT", which, at, j))
                            scores(0, 0, 0)
                            scores(0, 0, 1)
                        if (pos, i) == (1, 1):
                            p_transposes(0, 0, 0)
                        if (pos, i) == (1, 2):
                            values(0, 0, 0)
                            p_transposes(0, 0, 1)
                            scores(0, 1, 0)
            values(0, 0, 1)
            scores(0, 1, 1)
            attend(0, U_WO_A, "ln_ffn2_0")
            ffn(1, U_FFN2_0, "ln_ffn2_0", "kv_norm")

            def kv_pass(pos):
                if pos == 0:
                    unit_ready(U_KV)
                take(acc(pos, 1))
                note(("kv", pos), acc(pos, 1))
                w = 2 * KVW
                for kt in range(KT):
                    cols = slice(w * kt, w * (kt + 1))
                    for i, (xs, ws) in enumerate(((xT_hi, w_hi), (xT_hi, w_lo), (xT_lo, w_hi))):
                        mm = nc.tensor.matmul(bank[acc(pos, 1)][:, 0:w], xs[:, kt, own(pos)],
                                              ws[:, slot(U_KV), cols],
                                              start=(kt == 0 and i == 0), stop=(kt == KT - 1 and i == 2))
                if pos == 0:
                    fill(mm, ("kv",))
                else:
                    mm.then_inc(s_used, 1)

            x_ready(0)
            kv_pass(0)
            x_transposes("kv_norm", 1)
            x_ready(1)
            kv_pass(1)
            x_transposes("ln_ffn1_1", 0)
            ffn(2, U_FFN1_1, "ln_ffn1_1", "ln_mix_1")

            x_ready(0)
            for pos in range(NPOS):
                for i in range(4):
                    if pos == 0 and i == 2:
                        pe.wait_ge(s_kdup, 2)
                        transposes([kdup[:, t, g, :, :].rearrange("p e d -> p (e d)")
                                    for g in range(2) for t in range(NPOS)], 4, ("kT",))
                    if pos == 0 and i == 3:
                        x_transposes("ln_mix_1", 1)
                    if pos == 1 and i == 0:
                        x_ready(1)
                    columns_pass(U_WQ + i, i % 2, pos, i // 2, ("q_b", i // 2))
                    if (pos, i) == (0, 3):
                        q_transposes(0, 0, 4)
                    if (pos, i) == (1, 0):
                        in_sbuf(pe, ("kT",))
                        in_sbuf(pe, ("qT_b", 0, 0))
                        q_transposes(0, 1, 6)
                        scores(1, 0, 0)
                    if (pos, i) == (1, 1):
                        in_sbuf(pe, ("qT_b", 0, 1))
                        scores(1, 0, 1)
                        p_transposes(1, 0, 0)
                    if (pos, i) == (1, 2):
                        q_transposes(1, 0, acc(0, 1))
                        values(1, 0, 0)
                        p_transposes(1, 0, 1)
            in_sbuf(pe, ("qT_b", 1, 0))
            scores(1, 1, 0)
            values(1, 0, 1)
            scores(1, 1, 1)
            attend(1, U_WO_B, "ln_ffn2_1")
            ffn(3, U_FFN2_1, "ln_ffn2_1", None)

        @block.sync
        def _(sp):
            def load(u, parts, turn=None):
                if u >= UNITS_HELD:
                    n = u - UNITS_HELD + 1
                    sp.wait_ge(s_lo, n if turn is None else turn * UNITS_HELD + n)
                for i, (dst, src) in enumerate(parts):
                    full = s_gate0 if (u, i) == (0, 0) else s_raw[slot(u)]
                    sp.dma_start(dst, src).then_inc(full, 16)

            def gate_up(u0, w_gate, w_up, l):
                gate = w_gate[l].rearrange("(k p) f -> p k f", p=P)
                up = w_up[l].rearrange("(k p) f -> p k f", p=P)

                def unit(u, half, col, turn=None):
                    dst = raw[:, slot(u), :].rearrange("p (k g c) -> p k g c", k=4, g=2)
                    load(u, [(dst[:, :, i, :], w[:, 4 * half:4 * half + 4, bass.ds(col, CH)])
                             for i, w in enumerate((gate, up))], turn)

                for k in range(4):
                    unit(u0 + k, k % 2, CH * (k // 2))
                    if u0 + k == 1:
                        load_x(1)
                with sp.Fori(0, 4) as turn:
                    for k in range(4):
                        unit(u0 + 4 + k, k % 2, turn * (2 * CH) + CH * (2 + k // 2), turn)
                for k in range(2):
                    unit(u0 + 20 + k, k, CH * (N_CHUNK - 1))

            def rows(u0, n, w):
                view = w.rearrange("(k p) n -> p k n", p=P)
                for i in range(n):
                    dst = raw[:, slot(u0 + i), :].rearrange("p (k n) -> p k n", k=2)
                    load(u0 + i, [(dst[:, k, :], view[:, 2 * i + k, :]) for k in range(2)])

            def columns(u0, n_chunks, w):
                view = w.rearrange("(k p) n -> p k n", p=P)
                for c in range(n_chunks):
                    for half in range(2):
                        u = u0 + 2 * c + half
                        dst = raw[:, slot(u), :].rearrange("p (k n) -> p k n", k=4)
                        load(u, [(dst[:, 2 * i:2 * i + 2, :],
                                  view[:, 4 * half + 2 * i:4 * half + 2 * i + 2, BANK * c:BANK * (c + 1)])
                                 for i in range(2)])

            def vector(name):
                src = {"ln_ffn1_0": a["ln_ffn1"][0:1], "ln_mix_0": a["ln_mix"][0:1],
                       "ln_ffn2_0": a["ln_ffn2"][0:1], "kv_norm": a["kv_norm"].unsqueeze(0),
                       "ln_ffn1_1": a["ln_ffn1"][1:2], "ln_mix_1": a["ln_mix"][1:2],
                       "b_b_q": a["b_b_q"][0:1], "b_b_o": a["b_b_o"][0:1],
                       "ln_ffn2_1": a["ln_ffn2"][1:2], "final_norm": a["final_norm"].unsqueeze(0)}[name]
                n = VECS.index(name)
                if n == 2:
                    sp.wait_ge(s_lamd, 1)
                elif n >= VEC_RING:
                    before = VECS[n - VEC_RING]
                    if before == "b_b_q":
                        in_sbuf(sp, ("q_b", 1, 1))
                    else:
                        sp.wait_ge(s_xn, xn_count(before, 1))
                sp.dma_start(vec[:, n % VEC_RING, :], src.to_broadcast([P, D])).then_inc(s_vec[n % VEC_RING], 16)

            def load_x(pos):
                sp.dma_start(x[:, pos, :], a["x"][0, own(pos), :]).then_inc(s_x[pos], 16)

            load_x(0)
            vector("ln_ffn1_0")
            gate_up(U_FFN1_0, a["ffn1_w_gate"], a["ffn1_w_up"], 0)
            vector("ln_mix_0")
            vector("ln_ffn2_0")
            vector("kv_norm")
            rows(U_FFN1_0 + GU_UNITS, DN_UNITS, a["ffn1_w_down"][0])
            columns(U_QKV, 6, a["a_w_qkv"][0])
            rows(U_WO_A, 4, a["a_w_o"][0])
            vector("ln_ffn1_1")
            gate_up(U_FFN2_0, a["ffn2_w_gate"], a["ffn2_w_up"], 0)
            vector("ln_mix_1")
            rows(U_FFN2_0 + GU_UNITS, DN_UNITS, a["ffn2_w_down"][0])
            dst = raw[:, slot(U_KV), :].rearrange("p (k g c) -> p k g c", k=KT, g=2)
            load(U_KV, [(dst[:, :, i, :], a[w].rearrange("(k p) n -> p k n", p=P))
                        for i, w in enumerate(("kv_w_k", "kv_w_v"))])
            gate_up(U_FFN1_1, a["ffn1_w_gate"], a["ffn1_w_up"], 1)
            vector("b_b_q")
            vector("b_b_o")
            rows(U_FFN1_1 + GU_UNITS, DN_UNITS, a["ffn1_w_down"][1])
            columns(U_WQ, 2, a["b_w_q"][0])
            rows(U_WO_B, 4, a["b_w_o"][0])
            vector("ln_ffn2_1")
            gate_up(U_FFN2_1, a["ffn2_w_gate"], a["ffn2_w_up"], 1)
            vector("final_norm")
            rows(U_FFN2_1 + GU_UNITS, DN_UNITS, a["ffn2_w_down"][1])
            sp.wait_ge(s_xn, xn_count("final_norm", 0))
            sp.dma_start(out[0, own(0), :], xn[:, 0, :]).then_inc(s_out, 16)
            for j in range(2):
                cols = slice(BANK * j, BANK * (j + 1))
                sp.wait_ge(s_xn, xn_count("final_norm", 1) + j)
                sp.dma_start(out[0, own(1), cols], xn[:, 1, cols]).then_inc(s_out, 16)
            sp.wait_ge(s_out, 16 * 3)

        @block.gpsimd
        def _(pool):
            t = Tally()

            def link(ins):
                ins.then_inc(s_pool, 1)
                pool.wait_ge(s_pool, t.next("pool"))

            link(nc.gpsimd.memset(ident[:, :], 0.0))
            nc.gpsimd.affine_select(out=ident[:, :], in_=ident[:, :], compare_op=ALU.not_equal, fill=1.0,
                                    base=0, pattern=[[-1, P]], channel_multiplier=1).then_inc(s_ident, 1)
            nc.gpsimd.memset(mhalf[:, :], -0.5).then_inc(s_ident, 1)
            pool.wait_ge(s_ident, 2)

            def norm_scale(pos):
                pool.wait_ge(s_ss, t.next("ss"))
                link(nc.gpsimd.tensor_scalar(ms[:, pos:pos + 1], ss[:, pos:pos + 1], 1.0 / D, EPS,
                                             ALU.mult, ALU.add))
                nc.gpsimd.tensor_tensor(rstd[:, pos:pos + 1], ms[:, pos:pos + 1], mhalf[:, 0:1],
                                        ALU.pow).then_inc(s_rstd, 1)

            norm_scale(0)
            for pos in range(NPOS):
                pool.dma_start(pos_i[:, pos:pos + 1], a["positions"][0, own(pos)].unsqueeze(1)).then_inc(s_pos, 16)
            for i, name in enumerate(("a_lambda_q1", "a_lambda_k1", "a_lambda_q2", "a_lambda_k2")):
                pool.dma_start(lams[:, i, :], a[name][0:1].to_broadcast([P, HD])).then_inc(s_small, 16)
            pool.dma_start(gsub[:, :], a["a_subln"][0:1].to_broadcast([P, KVW])).then_inc(s_small, 16)
            pool.dma_start(sinks[:, :], a["b_sinks"][0:1].to_broadcast([P, 2 * HEADS])).then_inc(s_small, 16)
            for i, name in enumerate(("kv_b_k", "kv_b_v")):
                pool.dma_start(bkv[:, KVW * i:KVW * (i + 1)],
                               a[name].unsqueeze(0).to_broadcast([P, KVW])).then_inc(s_small, 16)
            norm_scale(1)

            for m in (identb[:, :], mask_a[:, :, :], mask_b[:, :, :]):
                link(nc.gpsimd.memset(m, 0.0))
            nc.gpsimd.affine_select(out=identb[:, :], in_=identb[:, :], compare_op=ALU.not_equal, fill=1.0,
                                    base=0, pattern=[[-1, P]], channel_multiplier=1).then_inc(s_mask, 1)
            for m in (mask_a, mask_b):
                nc.gpsimd.affine_select(out=m[:, 1, :], in_=m[:, 1, :], compare_op=ALU.is_ge, fill=MASKED,
                                        base=0, pattern=[[-1, P]], channel_multiplier=1).then_inc(s_mask, 1)
            nc.gpsimd.affine_select(out=mask_b[:, 0, :], in_=mask_b[:, 0, :], compare_op=ALU.is_gt, fill=MASKED,
                                    base=0, pattern=[[1, P]], channel_multiplier=-1).then_inc(s_mask, 1)

            for i in range(ROT // 2):
                freq = float(np.float32(THETA ** (-2.0 * i / ROT)))
                nc.gpsimd.memset(inv_freq[:, i:i + 1], freq).then_inc(s_pool, 1)
                t.next("pool")
            pool.wait_ge(s_pos, 32)
            link(nc.gpsimd.tensor_copy(pos_f[:, :], pos_i[:, :]))
            for pos in range(NPOS):
                link(nc.gpsimd.tensor_scalar(ang[:, pos, :], inv_freq[:, :], pos_f[:, pos:pos + 1], None, ALU.mult))
            NEAREST = 1.5 * 2.0 ** 23
            for unit in (4096.0, 1.0):
                link(nc.gpsimd.tensor_scalar(turns[:, :, :], ang[:, :, :], 1.0 / (2 * math.pi * unit), NEAREST,
                                             ALU.mult, ALU.add))
                link(nc.gpsimd.tensor_scalar(turns[:, :, :], turns[:, :, :], -NEAREST, None, ALU.add))
                for part in split_2pi():
                    link(nc.gpsimd.tensor_scalar(whole[:, :, :], turns[:, :, :], part * unit, None, ALU.mult))
                    link(nc.gpsimd.tensor_tensor(ang[:, :, :], ang[:, :, :], whole[:, :, :], ALU.subtract))
            PI = 3.1415925
            nc.gpsimd.tensor_scalar(ang[:, :, :], ang[:, :, :], PI, -PI, ALU.min, ALU.max).then_inc(s_fold, 1)
            pool.wait_ge(s_small, 16 * 8)
            pairs = lams.rearrange("p (i e) d -> p i e d", e=2)
            link(nc.gpsimd.tensor_tensor(lamp, pairs[:, :, 0, :], pairs[:, :, 1, :], ALU.mult))
            w = HD // 2
            while w:
                dst = lamd[:, :].unsqueeze(2) if w == 1 else lamp[:, :, 0:w]
                ins = nc.gpsimd.tensor_tensor(dst, lamp[:, :, 0:w], lamp[:, :, w:2 * w], ALU.add)
                if w > 1:
                    link(ins)
                w //= 2
            ins.then_inc(s_lamd, 1)
            nc.gpsimd.tensor_scalar(gsub[:, :], gsub[:, :], 1.0 - LAMBDA_INIT, None, ALU.mult).then_inc(s_table, 1)
            nc.gpsimd.tensor_scalar(negsink[:, :], sinks[:, :], -1.0, None, ALU.mult).then_inc(s_table, 1)
            pool.wait_ge(s_trig, 2)
            link(nc.gpsimd.tensor_tensor(turns[:, :, :], half_sin[:, :, :], half_sin[:, :, :], ALU.mult))
            link(nc.gpsimd.tensor_scalar(cos2[:, :, 0, :], turns[:, :, :], -2.0, 1.0, ALU.mult, ALU.add))
            nc.gpsimd.tensor_copy(cos2[:, :, 1, :], cos2[:, :, 0, :]).then_inc(s_table, 1)
            nc.gpsimd.tensor_scalar(sin2[:, :, 0, :], sin2[:, :, 1, :], -1.0, None, ALU.mult).then_inc(s_table, 1)
            pool.wait_ge(s_lame, 1)
            link(nc.gpsimd.tensor_tensor(neglam[:, :], lame[:, 1:2], lame[:, 0:1], ALU.subtract))
            nc.gpsimd.tensor_scalar(neglam[:, :], neglam[:, :], -LAMBDA_INIT, None, ALU.add).then_inc(s_table, 1)

            def rope(view, n, pos):
                half = ROT // 2
                c = cos2[:, pos, :, :].rearrange("p a b -> p (a b)").unsqueeze(1).to_broadcast([P, n, ROT])
                straight, crossed = rot[:, 0, 0:n, :], rot[:, 1, 0:n, :]
                if t.last("rope"):
                    pool.wait_ge(s_rope, t.last("rope"))
                nc.gpsimd.tensor_tensor(straight, view[:, :, 0:ROT], c, ALU.mult).then_inc(s_pool, 1)
                t.next("pool")
                for i in range(2):
                    nc.gpsimd.tensor_tensor(crossed[:, :, half * i:half * (i + 1)],
                                            view[:, :, half * (1 - i):half * (2 - i)],
                                            sin2[:, pos, i:i + 1, :].to_broadcast([P, n, half]),
                                            ALU.mult).then_inc(s_pool, 1)
                    t.next("pool")
                pool.wait_ge(s_pool, t.last("pool"))
                return nc.gpsimd.tensor_tensor(view[:, :, 0:ROT], straight, crossed, ALU.add)

            norm_scale(0)
            norm_scale(1)
            pool.wait_ge(s_table, TABLES)
            for which, view in enumerate((q_a, k_a)):
                for pos in range(NPOS):
                    for j in range(2):
                        in_sbuf(pool, ("qkv", which, j, pos))
                    rope(view[:, pos, :].rearrange("p (g d) -> p g d", d=HD), 2 * HEADS, pos).then_inc(s_rope, 1)
                    t.next("rope")

            def sub_norm_scale(pos):
                pool.wait_ge(s_oss, pos + 1)
                link(nc.gpsimd.tensor_scalar(oms[:, pos, :], oss[:, pos, :], 1.0 / (2 * HD), EPS,
                                             ALU.mult, ALU.add))
                nc.gpsimd.tensor_tensor(orstd[:, pos, :], oms[:, pos, :], mhalf[:, :], ALU.pow).then_inc(s_orstd, 1)

            sub_norm_scale(0)
            sub_norm_scale(1)
            norm_scale(0)
            norm_scale(1)
            norm_scale(0)
            norm_scale(1)
            for pos in range(NPOS):
                in_sbuf(pool, ("kv", pos))
                keys = kvb[:, pos, 0:KVW].rearrange("p (g d) -> p g d", d=HD)
                link(rope(keys, 2, pos))
                for e in range(2):
                    ins = nc.gpsimd.tensor_copy(kdup[:, pos, :, e, :], keys)
                ins.then_inc(s_kdup, 1)
            norm_scale(0)
            norm_scale(1)
            for pos in range(NPOS):
                for j in range(2):
                    in_sbuf(pool, ("q_b", j, pos))
                    cols = slice(BANK * j, BANK * (j + 1))
                    rope(xn[:, pos, cols].rearrange("p (g d) -> p g d", d=HD), HEADS, pos).then_inc(s_rope, 1)
                    t.next("rope")
            v, n = vec_of("b_b_o")
            pool.wait_ge(s_vec[v], n)
            for pos in range(NPOS):
                nc.gpsimd.tensor_tensor(x[:, pos, :], x[:, pos, :], vec[:, v, :], ALU.add).then_inc(s_bo, 1)
            norm_scale(0)
            norm_scale(1)
            norm_scale(0)
            pool.wait_ge(s_ss, t.next("ss") + 1)
            link(nc.gpsimd.tensor_tensor(ss[:, 1:2], ss_part[:, 0:1], ss_part[:, 1:2], ALU.add))
            link(nc.gpsimd.tensor_scalar(ms[:, 1:2], ss[:, 1:2], 1.0 / D, EPS, ALU.mult, ALU.add))
            nc.gpsimd.tensor_tensor(rstd[:, 1:2], ms[:, 1:2], mhalf[:, 0:1], ALU.pow).then_inc(s_rstd, 1)

        @block.scalar
        def _(act):
            def split(u, turn=None):
                if u >= N_UNITS:
                    return
                grow = 0 if turn is None else turn
                act.wait_ge(s_raw[slot(u)], grow * 32 + 32 * (u // UNITS_HELD + 1) - (16 if slot(u) == 0 else 0))
                if u >= UNITS_HELD:
                    n = u - UNITS_HELD + 1
                    act.wait_ge(s_used, n if turn is None else turn * UNITS_HELD + n)
                nc.scalar.activation(w_hi[:, slot(u), :], raw[:, slot(u), :], ACT.Copy).then_inc(s_hi, 1)

            t = Tally()

            def junk_free():
                for key, done in (("ss", s_ss), ("oss", s_oss)):
                    if t.last(key):
                        act.wait_ge(done, t.last(key))

            def square(pos, key=None):
                if key is None:
                    act.wait_ge(s_x[pos], 16)
                else:
                    in_sbuf(act, (*key, pos, 1))
                junk_free()
                t.next("ss")
                nc.scalar.activation(junk[:, :], x[:, pos, :], ACT.Square,
                                     accum_out=ss[:, pos:pos + 1]).then_inc(s_ss, 1)

            def hi_part(dst, b, key, n_tiles=4, turn=None):
                act.wait_ge(s_filled, filled[key] if turn is None else turn * FILLED_PER_TURN + filled[key])
                src = bank[b][:, 0:P * n_tiles].rearrange("p (k s) -> p k s", k=n_tiles)
                nc.scalar.activation(dst, src, ACT.Copy).then_inc(s_hipart, 1)

            def x_hi(name, pos):
                for j in range(2):
                    hi_part(xT_hi[:, 4 * j:4 * j + 4, own(pos)], 4 + 2 * pos + j, ("xT", name, pos, j))

            def o_hi(layer, pos, banks):
                for j, b in enumerate(banks):
                    hi_part(xT_hi[:, 4 * j:4 * j + 4, own(pos)], b, ("oT", layer, pos, j))

            def ffn(f, u0, name, aside=None):
                def silu_gate(pos, j, g, turn=None):
                    if pos == 0:
                        n = filled["gu", f, g, j]
                        act.wait_ge(s_filled, n if turn is None else turn * FILLED_PER_TURN + n)
                    else:
                        n = u0 + 4 * g + 2 * j + 2
                        act.wait_ge(s_used, n if turn is None else turn * UNITS_HELD + n)
                    nc.scalar.activation(silu[:, pos, j, :], bank[acc(pos, j)][:, 0:CH], ACT.Silu).then_inc(s_silu, 1)

                def h_hi(pos, g, turn=None, n_tiles=4):
                    k0 = 4 * g if turn is None else turn * 4 + 4 * g
                    hi_part(hT_hi[:, bass.ds(k0, n_tiles), own(pos)], 4 + 2 * pos, ("hT", (f, g), pos),
                            n_tiles, turn)

                def turn_of(g, turn=None):
                    if g == 0:
                        x_hi(name, 1)
                    silu_gate(0, 1, g, turn)
                    split(u0 + 4 * g + 4, turn)
                    split(u0 + 4 * g + 5, turn)
                    silu_gate(1, 0, g, turn)
                    h_hi(0, g, turn)
                    split(u0 + 4 * g + 6, turn)
                    split(u0 + 4 * g + 7, turn)
                    silu_gate(1, 1, g, turn)
                    silu_gate(0, 0, g + 1, turn)
                    h_hi(1, g, turn)

                silu_gate(0, 0, 0)
                turn_of(0)
                if aside:
                    aside()
                with act.Fori(0, LOOP_TURNS) as turn:
                    turn_of(1, turn)
                turn_of(4)
                split(u0 + 24)
                split(u0 + 25)
                silu_gate(1, 0, 5)
                h_hi(0, 5, n_tiles=2)
                h_hi(1, 5, n_tiles=2)
                for i in range(26, 33):
                    split(u0 + i)

            def boundary(key, u0, name):
                square(0, key)
                split(u0)
                split(u0 + 1)
                x_hi(name, 0)
                split(u0 + 2)
                split(u0 + 3)
                square(1, key)

            def copy_bank(dst, b, sem_full, n):
                act.wait_ge(sem_full, n)
                return nc.scalar.activation(dst, bank[b][:, :], ACT.Copy)

            def transposed(dst, b, key):
                copy_bank(dst, b, s_filled, filled[key]).then_inc(s_read[b], 1)

            def exps(layer, pos, r):
                act.wait_ge(s_negm, ROUNDS * layer + round_no(pos, r) + 1)
                n, keys = per_bank(pos), P * (pos + 1)
                p = probs[r % 2].rearrange("p (i c k) -> p i c k", i=n, c=2)
                for c, b in enumerate(pair(r)):
                    for i in range(n):
                        head = n * r + i
                        ins = nc.scalar.activation(p[:, i, c, :], bank[b][:, keys * i:keys * (i + 1)], ACT.Exp,
                                                   bias=negm[:, pos, head, c:c + 1], scale=SCALE,
                                                   accum_out=den[:, pos, head, c:c + 1])
                    ins.then_inc(s_read[b], 1)

            square(0)
            for i, full in enumerate((s_gate0, s_raw[0])):
                act.wait_ge(full, 16)
                nc.scalar.activation(half_of(w_hi, i), half_of(raw, i), ACT.Copy).then_inc((s_gate0_hi, s_hi)[i], 1)
            x_hi("ln_ffn1_0", 0)
            split(1)
            square(1)
            split(2)
            split(3)
            def tables():
                act.wait_ge(s_fold, 1)
                nc.scalar.activation(half_sin[:, :, :], ang[:, :, :], ACT.Sin, scale=0.5).then_inc(s_trig, 1)
                nc.scalar.activation(sin2[:, :, 1, :], ang[:, :, :], ACT.Sin).then_inc(s_trig, 1)
                act.wait_ge(s_lamd, 1)
                nc.scalar.activation(lame[:, :], lamd[:, :], ACT.Exp).then_inc(s_lame, 1)

            ffn(0, U_FFN1_0, "ln_ffn1_0", tables)
            boundary(("down", 0), U_QKV, "ln_mix_0")

            def projection(part, pos, j, dst):
                if pos == 0:
                    ins = copy_bank(dst, acc(0, j), s_filled, filled["qkv", part, j])
                else:
                    ins = copy_bank(dst, acc(1, j), s_used, U_QKV + 4 * part + 2 * j + 2)
                ins.then_inc(s_read[acc(pos, j)], 1)

            u_v = U_QKV + 8
            projection(0, 0, 0, q_a[:, 0, 0:BANK])
            x_hi("ln_mix_0", 1)
            projection(0, 0, 1, q_a[:, 0, BANK:D])
            split(U_QKV + 4)
            split(U_QKV + 5)
            projection(0, 1, 0, q_a[:, 1, 0:BANK])
            split(U_QKV + 6)
            split(U_QKV + 7)
            projection(0, 1, 1, q_a[:, 1, BANK:D])
            projection(1, 0, 0, k_a[:, 0, 0:BANK])
            projection(1, 0, 1, k_a[:, 0, BANK:D])
            split(u_v)
            split(u_v + 1)
            projection(1, 1, 0, k_a[:, 1, 0:BANK])
            split(u_v + 2)
            split(u_v + 3)
            projection(1, 1, 1, k_a[:, 1, BANK:D])

            def qk_transposed(which, pos):
                for j in range(2):
                    dst = qT[:, 4 * j:4 * j + 4, own(pos)] if which == 0 else kT_a[j][:, :, own(pos)]
                    transposed(dst, 4 + 2 * pos + j, ("qkT", which, pos, j))

            qk_transposed(0, 0)
            qk_transposed(0, 1)
            projection(2, 0, 0, v_a[:, 0, 0:BANK])
            qk_transposed(1, 0)
            qk_transposed(1, 1)
            projection(2, 0, 1, v_a[:, 0, BANK:D])
            exps(0, 0, 0)
            split(U_WO_A)
            exps(0, 0, 1)
            projection(2, 1, 0, v_a[:, 1, 0:BANK])
            split(U_WO_A + 1)
            exps(0, 1, 0)
            projection(2, 1, 1, v_a[:, 1, BANK:D])
            split(U_WO_A + 2)

            def o_squares(pos):
                in_sbuf(act, ("o", 0, pos, 1))
                junk_free()
                t.next("oss")
                for head in range(HEADS):
                    ins = nc.scalar.activation(junk[:, KVW * head:KVW * (head + 1)],
                                               xn[:, pos, KVW * head:KVW * (head + 1)], ACT.Square,
                                               accum_out=oss[:, pos, head:head + 1])
                ins.then_inc(s_oss, 1)

            def sink_exp(pos):
                act.wait_ge(s_earg, pos + 1)
                nc.scalar.activation(sink_e[:, pos, :, :], sink_e[:, pos, :, :], ACT.Exp).then_inc(s_esink, 1)

            def attend(layer, u_next, name):
                exps(layer, 1, 1)
                if layer == 0:
                    split(U_WO_A + 3)
                    o_squares(0)
                else:
                    transposed(qT[:, 4:8, own(1)], acc(1, 1), ("qT_b", 1, 1))
                    o_hi(1, 0, (acc(0, 0), acc(0, 1)))
                exps(layer, 1, 2)
                if layer == 0:
                    o_hi(0, 0, (acc(0, 0), acc(0, 1)))
                exps(layer, 1, 3)
                if layer == 1:
                    sink_exp(1)
                else:
                    o_squares(1)
                o_hi(layer, 1, (6, 7))
                square(0, ("wo", layer))
                split(u_next)
                split(u_next + 1)
                x_hi(name, 0)
                split(u_next + 2)
                split(u_next + 3)
                square(1, ("wo", layer))

            attend(0, U_FFN2_0, "ln_ffn2_0")
            ffn(1, U_FFN2_0, "ln_ffn2_0")
            boundary(("down", 1), U_KV, "kv_norm")
            x_hi("kv_norm", 1)
            x_hi("ln_ffn1_1", 0)
            split(U_FFN1_1 + 3)
            ffn(2, U_FFN1_1, "ln_ffn1_1")
            boundary(("down", 2), U_WQ, "ln_mix_1")
            transposed(kT_b.rearrange("p g s -> p (g s)"), 4, ("kT",))
            x_hi("ln_mix_1", 1)
            transposed(qT[:, 0:4, own(0)], 4, ("qT_b", 0, 0))
            split(U_WO_B)
            transposed(qT[:, 4:8, own(0)], 6, ("qT_b", 0, 1))
            exps(1, 0, 0)
            split(U_WO_B + 1)
            exps(1, 0, 1)
            sink_exp(0)
            split(U_WO_B + 2)
            transposed(qT[:, 0:4, own(1)], acc(0, 1), ("qT_b", 1, 0))
            exps(1, 1, 0)
            split(U_WO_B + 3)
            attend(1, U_FFN2_1, "ln_ffn2_1")
            ffn(3, U_FFN2_1, "ln_ffn2_1")
            square(0, ("down", 3))
            act.wait_ge(s_ss, t.last("ss"))
            for j in range(2):
                cols = slice(BANK * j, BANK * (j + 1))
                act.wait_ge(s_res, j + 1)
                nc.scalar.activation(junk[:, cols], x[:, 1, cols], ACT.Square,
                                     accum_out=ss_part[:, j:j + 1]).then_inc(s_ss, 1)

        @block.vector
        def _(dve):
            t = Tally()

            def link(ins):
                ins.then_inc(s_dve, 1)
                dve.wait_ge(s_dve, t.next("dve"))

            def split(u, turn=None):
                if u >= N_UNITS:
                    return
                dve.wait_ge(s_hi, u + 1 if turn is None else turn * UNITS_HELD + (u + 1))
                nc.vector.tensor_tensor(w_lo[:, slot(u), :], raw[:, slot(u), :],
                                        w_hi[:, slot(u), :].bitcast(F32), ALU.subtract).then_inc(s_lo, 1)

            def lo_part(dst, hi, b, n_tiles=4):
                dve.wait_ge(s_hipart, t.next("hipart"))
                src = bank[b][:, 0:P * n_tiles].rearrange("p (k s) -> p k s", k=n_tiles)
                nc.vector.tensor_tensor(dst, src, hi.bitcast(F32), ALU.subtract).then_inc(s_read[b], 1)

            def x_lo(pos, banks=None):
                for j, b in enumerate(banks or (4 + 2 * pos, 5 + 2 * pos)):
                    lo_part(xT_lo[:, 4 * j:4 * j + 4, own(pos)], xT_hi[:, 4 * j:4 * j + 4, own(pos)], b)

            def norm(name, pos, fresh=True):
                if fresh:
                    dve.wait_ge(s_rstd, t.next("rstd"))
                v, n = vec_of(name)
                dve.wait_ge(s_vec[v], n)
                nc.vector.scalar_tensor_tensor(out=xn[:, pos, :], in0=x[:, pos, :], scalar=rstd[:, pos:pos + 1],
                                               in1=vec[:, v, :], op0=ALU.mult, op1=ALU.mult).then_inc(s_xn, 1)

            def residual(key, pos, scale, u_last):
                if pos == 0:
                    dve.wait_ge(s_filled, filled[key])
                else:
                    dve.wait_ge(s_used, u_last + 1)
                for j in range(2):
                    cols = slice(BANK * j, BANK * (j + 1))
                    nc.vector.scalar_tensor_tensor(out=x[:, pos, cols], in0=bank[acc(pos, j)][:, :], scalar=scale,
                                                   in1=x[:, pos, cols], op0=ALU.mult,
                                                   op1=ALU.add).then_inc(s_read[acc(pos, j)], 1)

            def boundary(key, u_last, u0, name, scale=0.5):
                residual(key, 0, scale, u_last)
                norm(name, 0)
                split(u0)
                split(u0 + 1)
                x_lo(0)
                residual(key, 1, scale, u_last)
                split(u0 + 2)
                split(u0 + 3)
                norm(name, 1)

            def ffn(f, u0):
                def mul(pos, j, turn=None):
                    dve.wait_ge(s_silu, t.next("silu"))
                    b = acc(pos, j)
                    nc.vector.tensor_tensor(h[:, pos, CH * j:CH * (j + 1)], silu[:, pos, j, :], bank[b][:, CH:2 * CH],
                                            ALU.mult).then_inc(s_read[b], 1)

                def h_lo(pos, g, turn=None, n_tiles=4):
                    k0 = 4 * g if turn is None else turn * 4 + 4 * g
                    tile = bass.ds(k0, n_tiles)
                    lo_part(hT_lo[:, tile, own(pos)], hT_hi[:, tile, own(pos)], 4 + 2 * pos, n_tiles)

                def turn_of(g, turn=None):
                    if g == 0:
                        x_lo(1)
                    mul(0, 1)
                    split(u0 + 4 * g + 4, turn)
                    split(u0 + 4 * g + 5, turn)
                    mul(1, 0)
                    h_lo(0, g, turn)
                    split(u0 + 4 * g + 6, turn)
                    split(u0 + 4 * g + 7, turn)
                    mul(1, 1)
                    mul(0, 0)
                    h_lo(1, g, turn)

                mul(0, 0)
                turn_of(0)
                with dve.Fori(0, LOOP_TURNS) as turn:
                    t.enter(turn, {"silu": 4, "hipart": 2})
                    turn_of(1, turn)
                t.leave(LOOP_TURNS)
                turn_of(4)
                split(u0 + 24)
                split(u0 + 25)
                mul(1, 0)
                h_lo(0, 5, n_tiles=2)
                h_lo(1, 5, n_tiles=2)
                for i in range(26, 33):
                    split(u0 + i)

            def maxima(layer, pos, r):
                n, keys = per_bank(pos), P * (pos + 1)
                heads = slice(n * r, n * (r + 1))
                for c, b in enumerate(pair(r)):
                    dve.wait_ge(s_filled, filled["scores", layer, pos, r, c])
                    nc.vector.tensor_reduce(mx[:, pos, heads, c], bank[b][:, :].rearrange("p (i k) -> p i k", i=n),
                                            AX.X, ALU.max).then_inc(s_dve, 1)
                    t.next("dve")
                dve.wait_ge(s_dve, t.last("dve"))
                if layer == 0:
                    ins = nc.vector.tensor_scalar(negm[:, pos, heads, :], mx[:, pos, heads, :], -SCALE, None, ALU.mult)
                else:
                    sink = negsink[:, :].rearrange("p (h c) -> p h c", c=2)
                    ins = nc.vector.scalar_tensor_tensor(out=negm[:, pos, heads, :], in0=mx[:, pos, heads, :],
                                                         scalar=-SCALE, in1=sink[:, heads, :],
                                                         op0=ALU.mult, op1=ALU.min)
                ins.then_inc(s_negm, 1)

            def combine(pos, r):
                n, keys = per_bank(pos), P * (pos + 1)
                heads = slice(n * r, n * (r + 1))
                in_sbuf(dve, ("scores", 0, pos, r, 1))
                link(nc.vector.reciprocal(rden[:, pos, heads, :], den[:, pos, heads, :]))
                link(nc.vector.scalar_tensor_tensor(out=coef[:, pos, heads], in0=den[:, pos, heads, 0],
                                                    scalar=neglam[:, 0:1], in1=rden[:, pos, heads, 1],
                                                    op0=ALU.mult, op1=ALU.mult))
                p = probs[r % 2].rearrange("p (i c k) -> p i c k", i=n, c=2)
                for i in range(n):
                    head = n * r + i
                    ins = nc.vector.scalar_tensor_tensor(out=a_mix[:, r % 2, keys * i:keys * (i + 1)],
                                                         in0=p[:, i, 1, :], scalar=coef[:, pos, head:head + 1],
                                                         in1=p[:, i, 0, :], op0=ALU.mult, op1=ALU.add)
                ins.then_inc(s_mix, 1)

            def p_transposed(layer, pos, r):
                for c in (1,) if layer == 0 else (0, 1):
                    b = pair(r)[c]
                    dve.wait_ge(s_filled, filled["pT", layer, pos, r, c])
                    at = 0 if layer == 0 else BANK * c
                    nc.vector.tensor_copy(pT[:, r % 2, at:at + BANK], bank[b][:, :]).then_inc(s_read[b], 1)

            def output(layer, pos):
                if layer == 1:
                    dve.wait_ge(s_esink, pos + 1)
                    link(nc.vector.tensor_tensor(den[:, pos, :, :], den[:, pos, :, :], sink_e[:, pos, :, :], ALU.add))
                    link(nc.vector.reciprocal(rden[:, pos, :, :], den[:, pos, :, :]))
                for j in range(2):
                    b = acc(pos, j)
                    dve.wait_ge(s_filled, filled["o", layer, pos, j])
                    if layer == 0:
                        w, r = 2 * HD, rden[:, pos, 4 * j:4 * j + 4, 0]
                    else:
                        w, r = HD, rden[:, pos, 4 * j:4 * j + 4, :].rearrange("p h c -> p (h c)")
                    n = BANK // w
                    nc.vector.tensor_tensor(
                        xn[:, pos, BANK * j:BANK * (j + 1)].rearrange("p (n d) -> p n d", n=n),
                        bank[b][:, :].rearrange("p (n d) -> p n d", n=n),
                        r.unsqueeze(2).to_broadcast([P, n, w]), ALU.mult).then_inc(s_read[b], 1)

            def sub_norm(pos):
                o = xn[:, pos, :].rearrange("p (h d) -> p h d", h=HEADS)
                dve.wait_ge(s_orstd, pos + 1)
                for head in range(HEADS):
                    ins = nc.vector.scalar_tensor_tensor(out=o[:, head, :], in0=o[:, head, :],
                                                         scalar=orstd[:, pos, head:head + 1], in1=gsub[:, :],
                                                         op0=ALU.mult, op1=ALU.mult)
                ins.then_inc(s_on, 1)

            norm("ln_ffn1_0", 0)
            for i, full in enumerate((s_gate0_hi, s_hi)):
                dve.wait_ge(full, 1)
                ins = nc.vector.tensor_tensor(half_of(w_lo, i), half_of(raw, i), half_of(w_hi, i).bitcast(F32),
                                              ALU.subtract)
            ins.then_inc(s_lo, 1)
            x_lo(0)
            split(1)
            split(2)
            norm("ln_ffn1_0", 1)
            split(3)

            ffn(0, U_FFN1_0)
            boundary(("down", 0), U_QKV - 1, U_QKV, "ln_mix_0")

            dve.wait_ge(s_table, TABLES)
            x_lo(1)
            for i in range(4, 12):
                split(U_QKV + i)
            maxima(0, 0, 0)
            maxima(0, 0, 1)
            combine(0, 0)
            split(U_WO_A)
            combine(0, 1)
            p_transposed(0, 0, 0)
            split(U_WO_A + 1)
            p_transposed(0, 0, 1)
            maxima(0, 1, 0)
            split(U_WO_A + 2)
            output(0, 0)
            combine(1, 0)
            maxima(0, 1, 1)
            p_transposed(0, 1, 0)
            combine(1, 1)
            split(U_WO_A + 3)
            sub_norm(0)
            maxima(0, 1, 2)
            p_transposed(0, 1, 1)
            combine(1, 2)
            maxima(0, 1, 3)
            x_lo(0, (acc(0, 0), acc(0, 1)))
            p_transposed(0, 1, 2)
            combine(1, 3)
            p_transposed(0, 1, 3)
            output(0, 1)
            sub_norm(1)
            x_lo(1, (6, 7))
            residual(("wo", 0), 0, 1.0, None)
            norm("ln_ffn2_0", 0)
            split(U_FFN2_0)
            split(U_FFN2_0 + 1)
            x_lo(0)
            residual(("wo", 0), 1, 1.0, U_FFN2_0 - 1)
            split(U_FFN2_0 + 2)
            split(U_FFN2_0 + 3)
            norm("ln_ffn2_0", 1)

            ffn(1, U_FFN2_0)
            boundary(("down", 1), U_KV - 1, U_KV, "kv_norm")

            def add_bias(dst, key, pos, b, w, bias, u_last):
                if pos == 0:
                    dve.wait_ge(s_filled, filled[key])
                else:
                    dve.wait_ge(s_used, u_last + 1)
                nc.vector.tensor_tensor(dst, bank[b][:, 0:w], bias, ALU.add).then_inc(s_read[b], 1)

            norm("ln_ffn1_1", 0, fresh=False)
            x_lo(1)
            add_bias(kvb[:, 0, :], ("kv",), 0, acc(0, 1), 2 * KVW, bkv[:, :], None)
            norm("ln_ffn1_1", 1, fresh=False)
            add_bias(kvb[:, 1, :], ("kv",), 1, acc(1, 1), 2 * KVW, bkv[:, :], U_KV)
            x_lo(0)
            split(U_FFN1_1 + 3)
            ffn(2, U_FFN1_1)
            boundary(("down", 2), U_WQ - 1, U_WQ, "ln_mix_1")

            v, n = vec_of("b_b_q")
            dve.wait_ge(s_vec[v], n)

            def queries(pos, j):
                cols = slice(BANK * j, BANK * (j + 1))
                add_bias(xn[:, pos, cols], ("q_b", j), pos, acc(pos, j), BANK, vec[:, v, cols], U_WQ + 2 * j + 1)

            def sink_minus_max(pos):
                nc.vector.tensor_tensor(sink_e[:, pos, :, :], negm[:, pos, :, :],
                                        sinks[:, :].rearrange("p (h c) -> p h c", c=2), ALU.add).then_inc(s_earg, 1)

            queries(0, 0)
            x_lo(1)
            queries(0, 1)
            split(U_WO_B)
            maxima(1, 0, 0)
            queries(1, 0)
            split(U_WO_B + 1)
            maxima(1, 0, 1)
            dve.wait_ge(s_negm, ROUNDS + rounds(0))
            sink_minus_max(0)
            p_transposed(1, 0, 0)
            split(U_WO_B + 2)
            p_transposed(1, 0, 1)
            queries(1, 1)
            maxima(1, 1, 0)
            output(1, 0)
            maxima(1, 1, 1)
            split(U_WO_B + 3)
            p_transposed(1, 1, 0)
            x_lo(0, (acc(0, 0), acc(0, 1)))
            maxima(1, 1, 2)
            p_transposed(1, 1, 1)
            maxima(1, 1, 3)
            dve.wait_ge(s_negm, 2 * ROUNDS)
            sink_minus_max(1)
            p_transposed(1, 1, 2)
            p_transposed(1, 1, 3)
            output(1, 1)
            x_lo(1, (6, 7))
            dve.wait_ge(s_bo, 2)
            residual(("wo", 1), 0, 1.0, None)
            norm("ln_ffn2_1", 0)
            split(U_FFN2_1)
            split(U_FFN2_1 + 1)
            x_lo(0)
            residual(("wo", 1), 1, 1.0, U_FFN2_1 - 1)
            split(U_FFN2_1 + 2)
            split(U_FFN2_1 + 3)
            norm("ln_ffn2_1", 1)

            ffn(3, U_FFN2_1)
            residual(("down", 3), 0, 0.5, None)
            norm("final_norm", 0)
            for j in range(2):
                cols = slice(BANK * j, BANK * (j + 1))
                if j == 0:
                    dve.wait_ge(s_filled, filled["down", 3, 0])
                else:
                    dve.wait_ge(s_used, N_UNITS)
                nc.vector.scalar_tensor_tensor(out=x[:, 1, cols], in0=bank[acc(1, j)][:, :], scalar=0.5,
                                               in1=x[:, 1, cols], op0=ALU.mult, op1=ALU.add).then_inc(s_res, 1)
            dve.wait_ge(s_rstd, t.next("rstd"))
            v, _ = vec_of("final_norm")
            for j in range(2):
                cols = slice(BANK * j, BANK * (j + 1))
                nc.vector.scalar_tensor_tensor(out=xn[:, 1, cols], in0=x[:, 1, cols], scalar=rstd[:, 1:2],
                                               in1=vec[:, v, cols], op0=ALU.mult, op1=ALU.mult).then_inc(s_xn, 1)


_INS = ["x", "positions", "ln_ffn1", "ffn1_w_gate", "ffn1_w_up", "ffn1_w_down", "ln_mix", "ln_ffn2",
        "ffn2_w_gate", "ffn2_w_up", "ffn2_w_down", "a_w_qkv", "a_w_o", "a_lambda_q1", "a_lambda_k1",
        "a_lambda_q2", "a_lambda_k2", "a_subln", "b_w_q", "b_b_q", "b_sinks", "b_w_o", "b_b_o", "kv_norm",
        "kv_w_k", "kv_b_k", "kv_w_v", "kv_b_v", "final_norm"]


def kernel(**inputs):
    import concourse.bacc as bacc
    from concourse.bass_utils import run_bass_kernel_spmd

    nc = bacc.Bacc("TRN2", target_bir_lowering=False, num_devices=1)
    arrays, args = {}, {}
    for name in _INS:
        arr = np.ascontiguousarray(inputs[name])
        arrays[f"in_{name}"] = arr
        args[name] = nc.dram_tensor(f"in_{name}", arr.shape, mybir.dt.from_np(arr.dtype), kind="ExternalInput").ap()
    out = nc.dram_tensor("out_h", (1, SEQ, D), F32, kind="ExternalOutput").ap()
    trunk(nc, args, out)
    r = run_bass_kernel_spmd(nc, [arrays], core_ids=[0])
    return r.results[0]["out_h"]
```

```python
import math
from contextlib import ExitStack

import numpy as np
import concourse.bass as bass
from concourse import mybir

F32 = mybir.dt.float32
F32R = mybir.dt.float32r
BF16 = mybir.dt.bfloat16
I32 = mybir.dt.int32
ALU = mybir.AluOpType
ACT = mybir.ActivationFunctionType
AX = mybir.AxisListType

P = 128
D = 1024
SEQ = 256
FF = 2816
KT = D // P
NPOS = SEQ // P
BANK = 512
UNIT = 2048
UNITS_HELD = 4
CH = 256
N_CHUNK = FF // CH
FT = FF // P
GU_UNITS = 2 * N_CHUNK
DN_UNITS = FT // 2
FFN_UNITS = GU_UNITS + DN_UNITS
HEADS = 8
HD = 64
ROT = 16
KVW = 128
EPS = 1e-5
THETA = 500000.0
LAMBDA_INIT = 0.8 - 0.6 * math.exp(-0.3 * 0)
SCALE = HD ** -0.5
MASKED = -3.0e38

U_FFN1_0 = 0
U_QKV = U_FFN1_0 + FFN_UNITS
U_WO_A = U_QKV + 12
U_FFN2_0 = U_WO_A + 4
U_KV = U_FFN2_0 + FFN_UNITS
U_FFN1_1 = U_KV + 1
U_WQ = U_FFN1_1 + FFN_UNITS
U_WO_B = U_WQ + 4
U_FFN2_1 = U_WO_B + 4
N_UNITS = U_FFN2_1 + FFN_UNITS

VECS = ["ln_ffn1_0", "ln_mix_0", "ln_ffn2_0", "kv_norm", "ln_ffn1_1", "ln_mix_1", "b_b_q",
        "b_b_o", "ln_ffn2_1", "final_norm"]
VEC_RING = 3


class Tally:

    def __init__(self):
        self.n = {}
        self.turn = None
        self.per_turn = {}

    def next(self, key):
        self.n[key] = self.n.get(key, 0) + 1
        return self.last(key)

    def last(self, key):
        n = self.n.get(key, 0)
        if self.turn is not None and key in self.per_turn:
            return self.turn * self.per_turn[key] + n
        return n

    def enter(self, turn, per_turn):
        self.turn, self.per_turn, self.before = turn, per_turn, dict(self.n)

    def leave(self, turns):
        for key in set(self.n) | set(self.per_turn):
            grew = self.n.get(key, 0) - self.before.get(key, 0)
            assert grew == self.per_turn.get(key, 0), (key, grew)
            self.n[key] = self.n.get(key, 0) + grew * (turns - 1)
        self.turn = None


def split_2pi():
    rest, parts = 2 * math.pi, []
    for _ in range(3):
        e = math.floor(math.log2(rest)) - 11
        part = math.floor(rest / 2.0 ** e) * 2.0 ** e
        parts.append(part)
        rest -= part
    return parts + [rest]


def trunk(nc, a, out):
    with ExitStack() as ctx:
        def sb(name, shape, dt=F32):
            return ctx.enter_context(nc.sbuf_tensor(name, shape, dt))

        def sem(name):
            return ctx.enter_context(nc.semaphore(name))

        raw = sb("raw", [P, UNITS_HELD, UNIT])
        w_hi = sb("w_hi", [P, UNITS_HELD, UNIT], F32R)
        w_lo = sb("w_lo", [P, UNITS_HELD, UNIT], F32R)
        xT_hi = sb("xT_hi", [P, KT, SEQ], F32R)
        xT_lo = sb("xT_lo", [P, KT, SEQ], F32R)
        with nc.sbuf_tensor("att_1", [P, FT * SEQ], F32) as att_1:
            pass
        hT_hi = sb("hT_hi", [P, FT, SEQ], F32R)
        with nc.sbuf_tensor("att_2", [P, FT * SEQ], F32) as att_2:
            pass
        hT_lo = sb("hT_lo", [P, FT, SEQ], F32R)
        x = sb("x", [P, NPOS, D])
        xn = sb("xn", [P, NPOS, D])
        junk = sb("junk", [P, D], BF16)
        vec = sb("vec", [P, VEC_RING, D])
        silu = sb("silu", [P, NPOS, 2, CH])
        h = sb("h", [P, NPOS, 2 * CH])
        shared = sb("shared", [P, 1536])
        bkv = sb("bkv", [P, 2 * KVW])
        gsub = sb("gsub", [P, KVW])
        sinks = sb("sinks", [P, 2 * HEADS])
        negsink = sb("negsink", [P, 2 * HEADS])
        lamd = sb("lamd", [P, 2])
        lame = sb("lame", [P, 2])
        neglam = sb("neglam", [P, 1])
        pos_i = sb("pos_i", [P, NPOS], I32)
        pos_f = sb("pos_f", [P, NPOS])
        inv_freq = sb("inv_freq", [P, ROT // 2])
        ang = sb("ang", [P, NPOS, ROT // 2])
        turns = sb("turns", [P, NPOS, ROT // 2])
        whole = sb("whole", [P, NPOS, ROT // 2])
        half_sin = sb("half_sin", [P, NPOS, ROT // 2])
        cos2 = sb("cos2", [P, NPOS, 2, ROT // 2])
        sin2 = sb("sin2", [P, NPOS, 2, ROT // 2])
        rot = sb("rot", [P, 2, 2 * HEADS, ROT])
        ident = sb("ident", [P, P])
        identb = sb("identb", [P, P], BF16)
        mask_a = sb("mask_a", [P, 2, P], BF16)
        mask_b = sb("mask_b", [P, 2, P], BF16)
        ss = sb("ss", [P, NPOS])
        ss_part = sb("ss_part", [P, 2])
        ms = sb("ms", [P, NPOS])
        rstd = sb("rstd", [P, NPOS])
        mhalf = sb("mhalf", [P, HEADS])
        mx = sb("mx", [P, NPOS, HEADS, 2])
        negm = sb("negm", [P, NPOS, HEADS, 2])
        den = sb("den", [P, NPOS, HEADS, 2])
        rden = sb("rden", [P, NPOS, HEADS, 2])
        sink_e = sb("sink_e", [P, NPOS, HEADS, 2])
        coef = sb("coef", [P, NPOS, HEADS])
        oss = sb("oss", [P, NPOS, HEADS])
        oms = sb("oms", [P, NPOS, HEADS])
        orstd = sb("orstd", [P, NPOS, HEADS])

        kvb = shared[:, 0:512].rearrange("p (t n) -> p t n", t=NPOS)
        kdup = shared[:, 512:1024].rearrange("p (t g e d) -> p t g e d", t=NPOS, g=2, e=2)
        kT_b = shared[:, 1024:1536].rearrange("p (g s) -> p g s", g=2)
        a_mix = shared[:, 0:1024].rearrange("p (r n) -> p r n", r=2)
        lams = vec[:, 2, 0:4 * HD].rearrange("p (i d) -> p i d", i=4)
        lamp = vec[:, 2, 4 * HD:6 * HD].rearrange("p (i d) -> p i d", i=2)

        q_a = att_1[:, 0:2 * D].rearrange("p (t n) -> p t n", t=NPOS)
        k_a = att_1[:, 2 * D:4 * D].rearrange("p (t n) -> p t n", t=NPOS)
        v_a = att_2[:, 0:2 * D].rearrange("p (t n) -> p t n", t=NPOS)
        qT = att_2[:, 2 * D:4 * D].rearrange("p (k s) -> p k s", k=HEADS)
        kT_a = [f[:, 4 * D:5 * D].rearrange("p (k s) -> p k s", k=HEADS // 2) for f in (att_1, att_2)]
        pT = att_1[:, 0:2 * D].rearrange("p (r n) -> p r n", r=2)
        kv_xn = [h[:, :, :].rearrange("p a n -> p (a n)"), att_1[:, 2 * KT * SEQ:2 * KT * SEQ + D]]
        probs = [silu[:, :, :, :].rearrange("p a b n -> p (a b n)"),
                 h[:, :, :].rearrange("p a n -> p (a n)")]

        bank = [ctx.enter_context(nc.psum_tensor(f"bank{b}", [P, BANK], F32)) for b in range(8)]

        s_x = [sem(f"s_x{i}") for i in range(NPOS)]
        s_pos = sem("s_pos")
        s_small = sem("s_small")
        s_raw = [sem(f"s_raw{i}") for i in range(UNITS_HELD)]
        s_gate = [sem(f"s_gate{i}") for i in range(UNITS_HELD)]
        s_gate_hi = sem("s_gate_hi")
        s_vec = [sem(f"s_vec{i}") for i in range(VEC_RING)]
        s_hi = sem("s_hi")
        s_lo = sem("s_lo")
        s_used = sem("s_used")
        s_filled = sem("s_filled")
        s_read = [sem(f"s_read{b}") for b in range(8)]
        s_ident = sem("s_ident")
        s_mask = sem("s_mask")
        s_fold = sem("s_fold")
        s_trig = sem("s_trig")
        s_table = sem("s_table")
        s_lamd = sem("s_lamd")
        s_lame = sem("s_lame")
        s_res = sem("s_res")
        s_silu = sem("s_silu")
        s_hipart = sem("s_hipart")
        s_ss = sem("s_ss")
        s_rstd = sem("s_rstd")
        s_xn = sem("s_xn")
        s_dve = sem("s_dve")
        s_pool = sem("s_pool")
        s_rope = sem("s_rope")
        s_negm = sem("s_negm")
        s_mix = sem("s_mix")
        s_earg = sem("s_earg")
        s_esink = sem("s_esink")
        s_oss = sem("s_oss")
        s_orstd = sem("s_orstd")
        s_on = sem("s_on")
        s_bo = sem("s_bo")
        s_kdup = sem("s_kdup")
        s_out = sem("s_out")

        block = ctx.enter_context(nc.Block())

        def acc(pos, j):
            return 2 * pos + j

        def slot(u):
            return u % UNITS_HELD

        def own(pos):
            return slice(P * pos, P * (pos + 1))

        def per_bank(pos):
            return BANK // (P * (pos + 1))

        def rounds(pos):
            return HEADS // per_bank(pos)

        def pair(r):
            return (4, 5) if r % 2 == 0 else (6, 7)

        def round_no(pos, r):
            return r + pos * rounds(0)

        ROUNDS = rounds(0) + rounds(1)
        NORMS = ["ln_ffn1_0", "ln_mix_0", "ln_ffn2_0", "kv_norm", "ln_ffn1_1", "ln_mix_1", "ln_ffn2_1",
                 "final_norm"]

        def xn_count(name, pos):
            if name in ("kv_norm", "ln_ffn1_1"):
                return NPOS * NORMS.index("kv_norm") + 2 * pos + (1 if name == "kv_norm" else 2)
            return NPOS * NORMS.index(name) + pos + 1

        def xn_of(name, pos):
            return kv_xn[pos] if name == "kv_norm" else xn[:, pos, :]

        def x_banks(name, pos):
            if name in ("kv_norm", "ln_ffn1_1"):
                return (4, 5) if name == "kv_norm" else (6, 7)
            return 4 + 2 * pos, 5 + 2 * pos

        def x_parts(name):
            return (hT_hi, hT_lo) if name == "kv_norm" else (xT_hi, xT_lo)

        def w_parts(u):
            if u == U_KV:
                return [f[:, KT:2 * KT, :].rearrange("p k s -> p (k s)") for f in (hT_hi, hT_lo)]
            return [f[:, slot(u), :] for f in (w_hi, w_lo)]

        def half_no(pos, j):
            return NPOS * pos + j + 1

        ROTATED = {"q_a": 0, "k_a": 2 * NPOS, "q_b": 4 * NPOS}

        def rotated(what, pos, j):
            return ROTATED[what] + half_no(pos, j)

        def qk_bank(which, pos, j):
            return acc(1, j) if (which, pos) == (1, 1) else 4 + 2 * (pos if which == 0 else 0) + j

        def o_bank(pos, j):
            return ((acc(0, 0), acc(1, 1)), (4, 6))[pos][j]

        def vec_of(name):
            n = VECS.index(name)
            return n % VEC_RING, 16 * (n // VEC_RING + 1)

        filled = {}
        FILLED_PER_TURN = 4
        taken = {}

        def in_sbuf(eng, key):
            b, n = taken[key]
            eng.wait_ge(s_read[b], n)

        LOOP_TURNS = 3
        TABLES = 5

        def half_of(view, u, i):
            return view[:, u, :].rearrange("p (k g c) -> p k g c", k=4, g=2)[:, :, i, :]

        @block.tensor
        def _(pe):
            uses = [0] * 8
            count = [0]

            def take(b, turn=None):
                if turn is not None:
                    pe.wait_ge(s_read[b], turn + uses[b])
                elif uses[b]:
                    pe.wait_ge(s_read[b], uses[b])
                uses[b] += 1

            def fill(mm, key):
                mm.then_inc(s_filled, 1)
                count[0] += 1
                filled[key] = count[0]

            def note(key, b):
                taken[key] = b, uses[b]

            def unit_ready(u, turn=None):
                pe.wait_ge(s_lo, u + 1 if turn is None else turn * UNITS_HELD + (u + 1))

            def columns_pass(u, half, pos, j, key, turn=None):
                if pos == 0:
                    unit_ready(u, turn)
                b = acc(pos, j)
                if half == 0:
                    take(b, turn)
                for k in range(4):
                    kt = 4 * half + k
                    cols = slice(BANK * k, BANK * (k + 1))
                    for i, (xs, ws) in enumerate(((xT_hi, w_hi), (xT_hi, w_lo), (xT_lo, w_hi))):
                        mm = nc.tensor.matmul(bank[b][:, :], xs[:, kt, own(pos)], ws[:, slot(u), cols],
                                              start=(kt == 0 and i == 0), stop=(kt == KT - 1 and i == 2))
                if pos == 1:
                    mm.then_inc(s_used, 1)
                elif half == 1:
                    fill(mm, key)
                if half == 1:
                    note((*key, pos), b)

            def last_rows_pass(u, kt0, key):
                for j in range(2):
                    for k in range(2):
                        kt = kt0 + k
                        cols = slice(D * k + BANK * j, D * k + BANK * (j + 1))
                        for i, (lhs, ws) in enumerate(((hT_hi, w_hi), (hT_hi, w_lo), (hT_lo, w_hi))):
                            mm = nc.tensor.matmul(bank[acc(1, j)][:, :], lhs[:, kt, own(1)], ws[:, slot(u), cols],
                                                  start=False, stop=(k == 1 and i == 2))
                    if j == 0:
                        fill(mm, (*key, 0))
                    note((*key, 1, j), acc(1, j))
                mm.then_inc(s_used, 1)

            def rows_pass(u, kt0, n_kt, pos, lhs_hi, lhs_lo, key):
                if pos == 0:
                    unit_ready(u)
                if kt0 == 0:
                    take(acc(pos, 0))
                    take(acc(pos, 1))
                for k in range(2):
                    kt = kt0 + k
                    for j in range(2):
                        cols = slice(D * k + BANK * j, D * k + BANK * (j + 1))
                        for i, ws in enumerate((w_hi, w_lo)):
                            nc.tensor.matmul(bank[acc(pos, j)][:, :], lhs_hi[:, kt, own(pos)],
                                             ws[:, slot(u), cols], start=(kt == 0 and i == 0), stop=False)
                    for j in range(2):
                        cols = slice(D * k + BANK * j, D * k + BANK * (j + 1))
                        mm = nc.tensor.matmul(bank[acc(pos, j)][:, :], lhs_lo[:, kt, own(pos)],
                                              w_hi[:, slot(u), cols], start=False, stop=(kt == n_kt - 1))
                if pos == 1:
                    mm.then_inc(s_used, 1)
                elif kt == n_kt - 1:
                    fill(mm, key)
                if kt == n_kt - 1:
                    for j in range(2):
                        note((*key, pos, j), acc(pos, j))

            def transposes(srcs, b, key, turn=None):
                take(b, turn)
                for i, src in enumerate(srcs):
                    mm = nc.tensor.transpose(bank[b][:, P * i:P * (i + 1)], src, ident[:, :])
                fill(mm, key)
                note(key, b)

            def tiles(view, j):
                return [view[:, BANK * j + P * i:BANK * j + P * (i + 1)] for i in range(4)]

            def x_transposes(name, pos):
                pe.wait_ge(s_xn, xn_count(name, pos))
                for j, b in enumerate(x_banks(name, pos)):
                    transposes(tiles(xn_of(name, pos), j), b, ("xT", name, pos, j))

            def x_ready(name, pos):
                for j in range(2):
                    in_sbuf(pe, ("xT", name, pos, j))

            def h_transposes(pos, g, turn=None, n_tiles=4):
                b = acc(pos, 1 if n_tiles == 4 else 0)
                pe.wait_ge(s_read[b], uses[b] if turn is None else turn + uses[b])
                transposes([h[:, pos, P * i:P * (i + 1)] for i in range(n_tiles)], 4 + 2 * pos,
                           ("hT", g, pos), turn)

            def ffn(f, u0, name, next_name):
                def gate_up(u, pos, j, g, turn=None):
                    for half in range(2):
                        columns_pass(u0 + u + half, half, pos, j, ("gu", f, g, j), turn)

                def turn_of(g, turn=None):
                    columns_pass(u0 + 4 * g + 2, 0, 0, 1, ("gu", f, g, 1), turn)
                    if g == 0:
                        if name == "ln_ffn1_1":
                            x_transposes("kv_norm", 1)
                        x_transposes(name, 1)
                    columns_pass(u0 + 4 * g + 3, 1, 0, 1, ("gu", f, g, 1), turn)
                    if g == 0:
                        if name == "ln_ffn1_1":
                            kv_pass(1)
                        x_ready(name, 1)
                    gate_up(4 * g, 1, 0, g, turn)
                    h_transposes(0, (f, g), turn)
                    gate_up(4 * g + 2, 1, 1, g, turn)
                    gate_up(4 * g + 4, 0, 0, g + 1, turn)
                    h_transposes(1, (f, g), turn)

                x_ready(name, 0)
                gate_up(0, 0, 0, 0)
                turn_of(0)
                at = count[0], list(uses)
                with pe.Fori(0, LOOP_TURNS) as turn:
                    turn_of(1, turn)
                assert count[0] - at[0] == FILLED_PER_TURN
                count[0] += FILLED_PER_TURN * (LOOP_TURNS - 1)
                for b in range(8):
                    uses[b] += (uses[b] - at[1][b]) * (LOOP_TURNS - 1)
                turn_of(4)
                gate_up(20, 1, 0, 5)
                h_transposes(0, (f, 5), n_tiles=2)

                def down(ts, pos):
                    for i in ts:
                        if i == DN_UNITS - 1:
                            pe.wait_ge(s_read[4 + 2 * pos], h_read[pos])
                        rows_pass(u0 + GU_UNITS + i, 2 * i, FT, pos, hT_hi, hT_lo, ("down", f))

                h_read = [uses[4], uses[6] + 1]
                pe.wait_ge(s_read[4], uses[4] - 1)
                down((0, 1), 0)
                h_transposes(1, (f, 5), n_tiles=2)
                down((2,), 0)
                pe.wait_ge(s_read[6], uses[6] - 1)
                down((0, 1, 2), 1)
                down((3, 4, 5, 6), 0)
                down((3, 4, 5, 6), 1)
                down((7, 8, 9, 10), 0)
                down((7, 8, 9), 1)
                if next_name:
                    x_transposes(next_name, 0)
                    if next_name == "kv_norm":
                        x_transposes("ln_ffn1_1", 0)
                    down((10,), 1)
                else:
                    last_rows_pass(u0 + FFN_UNITS - 1, FT - 2, ("down", f))

            def kv_pass(pos):
                x_ready("kv_norm", pos)
                if pos == 0:
                    unit_ready(U_KV)
                take(acc(pos, 1))
                note(("kv", pos), acc(pos, 1))
                w, (hi, lo) = 2 * KVW, w_parts(U_KV)
                for kt in range(KT):
                    cols = slice(w * kt, w * (kt + 1))
                    for i, (xs, ws) in enumerate(((hT_hi, hi), (hT_hi, lo), (hT_lo, hi))):
                        mm = nc.tensor.matmul(bank[acc(pos, 1)][:, 0:w], xs[:, kt, own(pos)], ws[:, cols],
                                              start=(kt == 0 and i == 0), stop=(kt == KT - 1 and i == 2))
                if pos == 0:
                    mm.then_inc(s_used, 1)
                else:
                    fill(mm, ("kv",))

            def scores(layer, pos, r):
                if layer == 1 and pos == 1 and r == 2:
                    in_sbuf(pe, ("qT_b", 1, 1))
                n, keys = per_bank(pos), P * (pos + 1)
                mask = mask_a if layer == 0 else mask_b
                mask = mask[:, 1 - pos:2, :].rearrange("p b k -> p (b k)").unsqueeze(1).to_broadcast([P, n, keys])
                for b in pair(r):
                    take(b)
                    nc.tensor.matmul(bank[b][:, :].rearrange("p (n k) -> p n k", n=n), identb[:, :], mask,
                                     start=True, stop=False, skip_group_check=True)
                for i in range(n):
                    head = n * r + i
                    for c, b in enumerate(pair(r)):
                        rows = slice(HD * c, HD * (c + 1))
                        kT = kT_a[head // 4][rows, head % 4, 0:keys] if layer == 0 else kT_b[rows, head // 4, 0:keys]
                        mm = nc.tensor.matmul(bank[b][:, keys * i:keys * (i + 1)], qT[rows, head, own(pos)], kT,
                                              start=False, stop=(i == n - 1), skip_group_check=True)
                        if i == n - 1:
                            fill(mm, ("scores", layer, pos, r, c))
                            note(("scores", layer, pos, r, c), b)

            def p_transposes(layer, pos, r):
                n, nk = per_bank(pos), pos + 1
                if layer == 0:
                    pe.wait_ge(s_mix, round_no(pos, r) + 1)
                    transposes(tiles(a_mix[:, r % 2, :], 0), pair(r)[1], ("pT", 0, pos, r, 1))
                    return
                in_sbuf(pe, ("scores", 1, pos, r, 1))
                view = probs[r % 2].rearrange("p (i c k q) -> p i c k q", i=n, c=2, k=nk)
                for c, b in enumerate(pair(r)):
                    transposes([view[:, i, c, k, :] for i in range(n) for k in range(nk)], b,
                               ("pT", 1, pos, r, c))

            def values(layer, pos, r):
                n, nk = per_bank(pos), pos + 1
                for c in (1,) if layer == 0 else (0, 1):
                    in_sbuf(pe, ("pT", layer, pos, r, c))
                if layer == 0 and r % (rounds(pos) // 2) == 0:
                    in_sbuf(pe, ("qkv", 2, 2 * r // rounds(pos), pos))
                for i in range(n):
                    head = n * r + i
                    j = head // 4
                    if head % 4 == 0:
                        take(acc(pos, j))
                    for c in range(1 if layer == 0 else 2):
                        for k in range(nk):
                            if layer == 0:
                                lhsT = pT[:, r % 2, P * (nk * i + k):P * (nk * i + k + 1)]
                                v = v_a[:, k, KVW * head:KVW * (head + 1)]
                                o = bank[acc(pos, j)][:, KVW * (head % 4):KVW * (head % 4 + 1)]
                            else:
                                lhsT = pT[:, r % 2, BANK * c + P * (nk * i + k):BANK * c + P * (nk * i + k + 1)]
                                v = kvb[:, k, KVW + HD * j:KVW + HD * (j + 1)]
                                at = HD * (2 * (head % 4) + c)
                                o = bank[acc(pos, j)][:, at:at + HD]
                            mm = nc.tensor.matmul(o, lhsT, v, start=(k == 0), stop=(k == nk - 1))
                    if head % 4 == 3:
                        fill(mm, ("o", layer, pos, j))
                        note(("o", layer, pos, j), acc(pos, j))

            def o_transposes(layer, pos, j):
                if layer == 0:
                    pe.wait_ge(s_on, half_no(pos, j))
                else:
                    in_sbuf(pe, ("o", 1, pos, j))
                transposes(tiles(xn[:, pos, :], j), o_bank(pos, j), ("oT", layer, pos, j))

            def attend(layer, u_wo, next_name):
                def wo(i, pos):
                    if i % 2 == 0:
                        in_sbuf(pe, ("oT", layer, pos, i // 2))
                    rows_pass(u_wo + i, 2 * i, KT, pos, xT_hi, xT_lo, ("wo", layer))

                p_transposes(layer, 1, 0)
                o_transposes(layer, 0, 0)
                if layer == 1:
                    q_transposes(1, 1, acc(1, 1))
                values(layer, 1, 0)
                scores(layer, 1, 2)
                p_transposes(layer, 1, 1)
                wo(0, 0)
                values(layer, 1, 1)
                scores(layer, 1, 3)
                o_transposes(layer, 0, 1)
                p_transposes(layer, 1, 2)
                wo(1, 0)
                values(layer, 1, 2)
                p_transposes(layer, 1, 3)
                o_transposes(layer, 1, 0)
                wo(2, 0)
                values(layer, 1, 3)
                wo(3, 0)
                wo(0, 1)
                o_transposes(layer, 1, 1)
                wo(1, 1)
                x_transposes(next_name, 0)
                wo(2, 1)
                wo(3, 1)

            def q_transposes(pos, j, b):
                pe.wait_ge(s_rope, rotated("q_b", pos, j))
                transposes(tiles(xn[:, pos, :], j), b, ("qT_b", pos, j))

            def warm(n):
                for _ in range(n):
                    nc.tensor.transpose(bank[7][:, 0:P], ident[:, :], ident[:, :])

            pe.wait_ge(s_ident, 2)
            warm(28)
            x_transposes("ln_ffn1_0", 0)
            warm(12)
            ffn(0, U_FFN1_0, "ln_ffn1_0", "ln_mix_0")

            def qk_transposes(which, pos):
                for j in range(2):
                    pe.wait_ge(s_rope, rotated(("q_a", "k_a")[which], pos, j))
                    transposes(tiles((q_a, k_a)[which][:, pos, :], j), qk_bank(which, pos, j),
                               ("qkT", which, pos, j))

            def qk_ready(pos):
                for which in range(2):
                    for j in range(2):
                        in_sbuf(pe, ("qkT", which, pos, j))

            x_ready("ln_mix_0", 0)
            for part in range(3):
                u0 = U_QKV + 4 * part
                for pos in range(NPOS):
                    for i in range(4):
                        if part == 0 and pos == 0 and i == 3:
                            x_transposes("ln_mix_0", 1)
                        if part == 0 and pos == 1 and i == 0:
                            x_ready("ln_mix_0", 1)
                        columns_pass(u0 + i, i % 2, pos, i // 2, ("qkv", part, i // 2))
                        if (part, pos, i) == (1, 0, 3):
                            qk_transposes(0, 0)
                        if (part, pos, i) == (1, 1, 0):
                            qk_transposes(0, 1)
                        if part < 2:
                            continue
                        if (pos, i) == (0, 0):
                            qk_transposes(1, 0)
                        if (pos, i) == (0, 1):
                            pe.wait_ge(s_mask, 4)
                            qk_ready(0)
                            scores(0, 0, 0)
                            scores(0, 0, 1)
                        if (pos, i) == (0, 2):
                            qk_transposes(1, 1)
                        if (pos, i) == (1, 0):
                            p_transposes(0, 0, 0)
                        if (pos, i) == (1, 1):
                            values(0, 0, 0)
                            p_transposes(0, 0, 1)
                            qk_ready(1)
                            scores(0, 1, 0)
                        if (pos, i) == (1, 2):
                            values(0, 0, 1)
                            scores(0, 1, 1)
            attend(0, U_WO_A, "ln_ffn2_0")
            ffn(1, U_FFN2_0, "ln_ffn2_0", "kv_norm")

            kv_pass(0)
            ffn(2, U_FFN1_1, "ln_ffn1_1", "ln_mix_1")

            x_ready("ln_mix_1", 0)
            for pos in range(NPOS):
                for i in range(4):
                    if pos == 0 and i == 2:
                        pe.wait_ge(s_kdup, 2)
                        transposes([kdup[:, t, g, :, :].rearrange("p e d -> p (e d)")
                                    for g in range(2) for t in range(NPOS)], 4, ("kT",))
                    if pos == 0 and i == 3:
                        x_transposes("ln_mix_1", 1)
                    if pos == 1 and i == 0:
                        x_ready("ln_mix_1", 1)
                    columns_pass(U_WQ + i, i % 2, pos, i // 2, ("q_b", i // 2))
                    if (pos, i) == (0, 3):
                        q_transposes(0, 0, 4)
                    if (pos, i) == (1, 0):
                        in_sbuf(pe, ("kT",))
                        in_sbuf(pe, ("qT_b", 0, 0))
                        q_transposes(0, 1, 6)
                        scores(1, 0, 0)
                    if (pos, i) == (1, 1):
                        in_sbuf(pe, ("qT_b", 0, 1))
                        scores(1, 0, 1)
                    if (pos, i) == (1, 2):
                        p_transposes(1, 0, 0)
                        q_transposes(1, 0, acc(0, 1))
            values(1, 0, 0)
            p_transposes(1, 0, 1)
            in_sbuf(pe, ("qT_b", 1, 0))
            scores(1, 1, 0)
            values(1, 0, 1)
            scores(1, 1, 1)
            attend(1, U_WO_B, "ln_ffn2_1")
            ffn(3, U_FFN2_1, "ln_ffn2_1", None)

        @block.sync
        def _(sp):
            def load(u, parts, turn=None):
                if u >= UNITS_HELD:
                    n = u - UNITS_HELD + 1
                    sp.wait_ge(s_lo, n if turn is None else turn * UNITS_HELD + n)
                for i, (dst, src) in enumerate(parts):
                    full = s_gate[u] if u < UNITS_HELD and i == 0 else s_raw[slot(u)]
                    sp.dma_start(dst, src).then_inc(full, 16)

            def gate_up(u0, w_gate, w_up, l):
                gate = w_gate[l].rearrange("(k p) f -> p k f", p=P)
                up = w_up[l].rearrange("(k p) f -> p k f", p=P)

                def unit(u, half, col, turn=None):
                    dst = raw[:, slot(u), :].rearrange("p (k g c) -> p k g c", k=4, g=2)
                    load(u, [(dst[:, :, i, :], w[:, 4 * half:4 * half + 4, bass.ds(col, CH)])
                             for i, w in enumerate((gate, up))], turn)

                for k in range(4):
                    unit(u0 + k, k % 2, CH * (k // 2))
                    if u0 + k == 2:
                        load_x(1)
                with sp.Fori(0, 4) as turn:
                    for k in range(4):
                        unit(u0 + 4 + k, k % 2, turn * (2 * CH) + CH * (2 + k // 2), turn)
                for k in range(2):
                    unit(u0 + 20 + k, k, CH * (N_CHUNK - 1))

            def rows(u0, n, w):
                view = w.rearrange("(k p) n -> p k n", p=P)
                for i in range(n):
                    dst = raw[:, slot(u0 + i), :].rearrange("p (k n) -> p k n", k=2)
                    load(u0 + i, [(dst[:, k, :], view[:, 2 * i + k, :]) for k in range(2)])

            def columns(u0, n_chunks, w):
                view = w.rearrange("(k p) n -> p k n", p=P)
                for c in range(n_chunks):
                    for half in range(2):
                        u = u0 + 2 * c + half
                        dst = raw[:, slot(u), :].rearrange("p (k n) -> p k n", k=4)
                        load(u, [(dst[:, 2 * i:2 * i + 2, :],
                                  view[:, 4 * half + 2 * i:4 * half + 2 * i + 2, BANK * c:BANK * (c + 1)])
                                 for i in range(2)])

            def vector(name):
                src = {"ln_ffn1_0": a["ln_ffn1"][0:1], "ln_mix_0": a["ln_mix"][0:1],
                       "ln_ffn2_0": a["ln_ffn2"][0:1], "kv_norm": a["kv_norm"].unsqueeze(0),
                       "ln_ffn1_1": a["ln_ffn1"][1:2], "ln_mix_1": a["ln_mix"][1:2],
                       "b_b_q": a["b_b_q"][0:1], "b_b_o": a["b_b_o"][0:1],
                       "ln_ffn2_1": a["ln_ffn2"][1:2], "final_norm": a["final_norm"].unsqueeze(0)}[name]
                n = VECS.index(name)
                if n == 2:
                    sp.wait_ge(s_lamd, 1)
                elif n >= VEC_RING:
                    before = VECS[n - VEC_RING]
                    if before == "b_b_q":
                        in_sbuf(sp, ("q_b", 1, 1))
                    else:
                        sp.wait_ge(s_xn, xn_count(before, 1))
                sp.dma_start(vec[:, n % VEC_RING, :], src.to_broadcast([P, D])).then_inc(s_vec[n % VEC_RING], 16)

            def load_x(pos):
                sp.dma_start(x[:, pos, :], a["x"][0, own(pos), :]).then_inc(s_x[pos], 16)

            load_x(0)
            vector("ln_ffn1_0")
            gate_up(U_FFN1_0, a["ffn1_w_gate"], a["ffn1_w_up"], 0)
            vector("ln_mix_0")
            vector("ln_ffn2_0")
            vector("kv_norm")
            rows(U_FFN1_0 + GU_UNITS, DN_UNITS, a["ffn1_w_down"][0])
            columns(U_QKV, 6, a["a_w_qkv"][0])
            rows(U_WO_A, 4, a["a_w_o"][0])
            vector("ln_ffn1_1")
            gate_up(U_FFN2_0, a["ffn2_w_gate"], a["ffn2_w_up"], 0)
            vector("ln_mix_1")
            rows(U_FFN2_0 + GU_UNITS, DN_UNITS, a["ffn2_w_down"][0])
            dst = raw[:, slot(U_KV), :].rearrange("p (k g c) -> p k g c", k=KT, g=2)
            load(U_KV, [(dst[:, :, i, :], a[w].rearrange("(k p) n -> p k n", p=P))
                        for i, w in enumerate(("kv_w_k", "kv_w_v"))])
            gate_up(U_FFN1_1, a["ffn1_w_gate"], a["ffn1_w_up"], 1)
            vector("b_b_q")
            vector("b_b_o")
            rows(U_FFN1_1 + GU_UNITS, DN_UNITS, a["ffn1_w_down"][1])
            columns(U_WQ, 2, a["b_w_q"][0])
            rows(U_WO_B, 4, a["b_w_o"][0])
            vector("ln_ffn2_1")
            gate_up(U_FFN2_1, a["ffn2_w_gate"], a["ffn2_w_up"], 1)
            vector("final_norm")
            rows(U_FFN2_1 + GU_UNITS, DN_UNITS, a["ffn2_w_down"][1])
            sp.wait_ge(s_xn, xn_count("final_norm", 0))
            sp.dma_start(out[0, own(0), :], xn[:, 0, :]).then_inc(s_out, 16)
            for j in range(2):
                cols = slice(BANK * j, BANK * (j + 1))
                sp.wait_ge(s_xn, xn_count("final_norm", 1) + j)
                sp.dma_start(out[0, own(1), cols], xn[:, 1, cols]).then_inc(s_out, 16)
            sp.wait_ge(s_out, 16 * 3)

        @block.gpsimd
        def _(pool):
            t = Tally()

            def link(ins):
                ins.then_inc(s_pool, 1)
                pool.wait_ge(s_pool, t.next("pool"))

            link(nc.gpsimd.memset(ident[:, :], 0.0))
            nc.gpsimd.affine_select(out=ident[:, :], in_=ident[:, :], compare_op=ALU.not_equal, fill=1.0,
                                    base=0, pattern=[[-1, P]], channel_multiplier=1).then_inc(s_ident, 1)
            nc.gpsimd.memset(mhalf[:, :], -0.5).then_inc(s_ident, 1)
            pool.wait_ge(s_ident, 2)

            def norm_scale(pos):
                pool.wait_ge(s_ss, t.next("ss"))
                link(nc.gpsimd.tensor_scalar(ms[:, pos:pos + 1], ss[:, pos:pos + 1], 1.0 / D, EPS,
                                             ALU.mult, ALU.add))
                nc.gpsimd.tensor_tensor(rstd[:, pos:pos + 1], ms[:, pos:pos + 1], mhalf[:, 0:1],
                                        ALU.pow).then_inc(s_rstd, 1)

            norm_scale(0)
            for pos in range(NPOS):
                pool.dma_start(pos_i[:, pos:pos + 1], a["positions"][0, own(pos)].unsqueeze(1)).then_inc(s_pos, 16)
            for i, name in enumerate(("a_lambda_q1", "a_lambda_k1", "a_lambda_q2", "a_lambda_k2")):
                pool.dma_start(lams[:, i, :], a[name][0:1].to_broadcast([P, HD])).then_inc(s_small, 16)
            pool.dma_start(gsub[:, :], a["a_subln"][0:1].to_broadcast([P, KVW])).then_inc(s_small, 16)
            pool.dma_start(sinks[:, :], a["b_sinks"][0:1].to_broadcast([P, 2 * HEADS])).then_inc(s_small, 16)
            for i, name in enumerate(("kv_b_k", "kv_b_v")):
                pool.dma_start(bkv[:, KVW * i:KVW * (i + 1)],
                               a[name].unsqueeze(0).to_broadcast([P, KVW])).then_inc(s_small, 16)
            norm_scale(1)

            for m in (identb[:, :], mask_a[:, :, :], mask_b[:, :, :]):
                link(nc.gpsimd.memset(m, 0.0))
            nc.gpsimd.affine_select(out=identb[:, :], in_=identb[:, :], compare_op=ALU.not_equal, fill=1.0,
                                    base=0, pattern=[[-1, P]], channel_multiplier=1).then_inc(s_mask, 1)
            for m in (mask_a, mask_b):
                nc.gpsimd.affine_select(out=m[:, 1, :], in_=m[:, 1, :], compare_op=ALU.is_ge, fill=MASKED,
                                        base=0, pattern=[[-1, P]], channel_multiplier=1).then_inc(s_mask, 1)
            nc.gpsimd.affine_select(out=mask_b[:, 0, :], in_=mask_b[:, 0, :], compare_op=ALU.is_gt, fill=MASKED,
                                    base=0, pattern=[[1, P]], channel_multiplier=-1).then_inc(s_mask, 1)

            for i in range(ROT // 2):
                freq = float(np.float32(THETA ** (-2.0 * i / ROT)))
                nc.gpsimd.memset(inv_freq[:, i:i + 1], freq).then_inc(s_pool, 1)
                t.next("pool")
            pool.wait_ge(s_pos, 32)
            link(nc.gpsimd.tensor_copy(pos_f[:, :], pos_i[:, :]))
            for pos in range(NPOS):
                link(nc.gpsimd.tensor_scalar(ang[:, pos, :], inv_freq[:, :], pos_f[:, pos:pos + 1], None, ALU.mult))
            NEAREST = 1.5 * 2.0 ** 23
            for unit in (4096.0, 1.0):
                link(nc.gpsimd.tensor_scalar(turns[:, :, :], ang[:, :, :], 1.0 / (2 * math.pi * unit), NEAREST,
                                             ALU.mult, ALU.add))
                link(nc.gpsimd.tensor_scalar(turns[:, :, :], turns[:, :, :], -NEAREST, None, ALU.add))
                for part in split_2pi():
                    link(nc.gpsimd.tensor_scalar(whole[:, :, :], turns[:, :, :], part * unit, None, ALU.mult))
                    link(nc.gpsimd.tensor_tensor(ang[:, :, :], ang[:, :, :], whole[:, :, :], ALU.subtract))
            PI = 3.1415925
            nc.gpsimd.tensor_scalar(ang[:, :, :], ang[:, :, :], PI, -PI, ALU.min, ALU.max).then_inc(s_fold, 1)
            pool.wait_ge(s_small, 16 * 8)
            pairs = lams.rearrange("p (i e) d -> p i e d", e=2)
            link(nc.gpsimd.tensor_tensor(lamp, pairs[:, :, 0, :], pairs[:, :, 1, :], ALU.mult))
            w = HD // 2
            while w:
                dst = lamd[:, :].unsqueeze(2) if w == 1 else lamp[:, :, 0:w]
                ins = nc.gpsimd.tensor_tensor(dst, lamp[:, :, 0:w], lamp[:, :, w:2 * w], ALU.add)
                if w > 1:
                    link(ins)
                w //= 2
            ins.then_inc(s_lamd, 1)
            nc.gpsimd.tensor_scalar(gsub[:, :], gsub[:, :], 1.0 - LAMBDA_INIT, None, ALU.mult).then_inc(s_table, 1)
            nc.gpsimd.tensor_scalar(negsink[:, :], sinks[:, :], -1.0, None, ALU.mult).then_inc(s_table, 1)
            pool.wait_ge(s_trig, 2)
            link(nc.gpsimd.tensor_tensor(turns[:, :, :], half_sin[:, :, :], half_sin[:, :, :], ALU.mult))
            link(nc.gpsimd.tensor_scalar(cos2[:, :, 0, :], turns[:, :, :], -2.0, 1.0, ALU.mult, ALU.add))
            nc.gpsimd.tensor_copy(cos2[:, :, 1, :], cos2[:, :, 0, :]).then_inc(s_table, 1)
            nc.gpsimd.tensor_scalar(sin2[:, :, 0, :], sin2[:, :, 1, :], -1.0, None, ALU.mult).then_inc(s_table, 1)
            pool.wait_ge(s_lame, 1)
            link(nc.gpsimd.tensor_tensor(neglam[:, :], lame[:, 1:2], lame[:, 0:1], ALU.subtract))
            nc.gpsimd.tensor_scalar(neglam[:, :], neglam[:, :], -LAMBDA_INIT, None, ALU.add).then_inc(s_table, 1)

            def rope(view, n, pos):
                half = ROT // 2
                c = cos2[:, pos, :, :].rearrange("p a b -> p (a b)").unsqueeze(1).to_broadcast([P, n, ROT])
                straight, crossed = rot[:, 0, 0:n, :], rot[:, 1, 0:n, :]
                if t.last("rope"):
                    pool.wait_ge(s_rope, t.last("rope"))
                nc.gpsimd.tensor_tensor(straight, view[:, :, 0:ROT], c, ALU.mult).then_inc(s_pool, 1)
                t.next("pool")
                for i in range(2):
                    nc.gpsimd.tensor_tensor(crossed[:, :, half * i:half * (i + 1)],
                                            view[:, :, half * (1 - i):half * (2 - i)],
                                            sin2[:, pos, i:i + 1, :].to_broadcast([P, n, half]),
                                            ALU.mult).then_inc(s_pool, 1)
                    t.next("pool")
                pool.wait_ge(s_pool, t.last("pool"))
                return nc.gpsimd.tensor_tensor(view[:, :, 0:ROT], straight, crossed, ALU.add)

            norm_scale(0)
            norm_scale(1)
            pool.wait_ge(s_table, TABLES)
            for which, view in enumerate((q_a, k_a)):
                for pos in range(NPOS):
                    for j in range(2):
                        in_sbuf(pool, ("qkv", which, j, pos))
                        cols = slice(BANK * j, BANK * (j + 1))
                        rope(view[:, pos, cols].rearrange("p (g d) -> p g d", d=HD), HEADS, pos).then_inc(s_rope, 1)
                        t.next("rope")

            def sub_norm_scale(pos, j):
                heads = slice(4 * j, 4 * j + 4)
                pool.wait_ge(s_oss, half_no(pos, j))
                link(nc.gpsimd.tensor_scalar(oms[:, pos, heads], oss[:, pos, heads], 1.0 / (2 * HD), EPS,
                                             ALU.mult, ALU.add))
                nc.gpsimd.tensor_tensor(orstd[:, pos, heads], oms[:, pos, heads], mhalf[:, 0:4],
                                        ALU.pow).then_inc(s_orstd, 1)

            for pos in range(NPOS):
                for j in range(2):
                    sub_norm_scale(pos, j)
            norm_scale(0)
            norm_scale(1)
            norm_scale(0)
            norm_scale(1)
            for pos in range(NPOS):
                in_sbuf(pool, ("kv", pos))
                keys = kvb[:, pos, 0:KVW].rearrange("p (g d) -> p g d", d=HD)
                link(rope(keys, 2, pos))
                for e in range(2):
                    ins = nc.gpsimd.tensor_copy(kdup[:, pos, :, e, :], keys)
                ins.then_inc(s_kdup, 1)
            norm_scale(0)
            norm_scale(1)
            for pos in range(NPOS):
                for j in range(2):
                    in_sbuf(pool, ("q_b", j, pos))
                    cols = slice(BANK * j, BANK * (j + 1))
                    rope(xn[:, pos, cols].rearrange("p (g d) -> p g d", d=HD), HEADS, pos).then_inc(s_rope, 1)
                    t.next("rope")
            v, n = vec_of("b_b_o")
            pool.wait_ge(s_vec[v], n)
            for pos in range(NPOS):
                nc.gpsimd.tensor_tensor(x[:, pos, :], x[:, pos, :], vec[:, v, :], ALU.add).then_inc(s_bo, 1)
            norm_scale(0)
            norm_scale(1)
            norm_scale(0)
            pool.wait_ge(s_ss, t.next("ss"))
            link(nc.gpsimd.tensor_scalar(ss[:, 1:2], ss_part[:, 0:1], 1.0 / D, EPS, ALU.mult, ALU.add))
            pool.wait_ge(s_ss, t.next("ss"))
            link(nc.gpsimd.tensor_scalar(ms[:, 1:2], ss_part[:, 1:2], 1.0 / D, ss[:, 1:2], ALU.mult, ALU.add))
            nc.gpsimd.tensor_tensor(rstd[:, 1:2], ms[:, 1:2], mhalf[:, 0:1], ALU.pow).then_inc(s_rstd, 1)

        @block.scalar
        def _(act):
            def split(u, turn=None):
                if u >= N_UNITS:
                    return
                grow = 0 if turn is None else turn
                act.wait_ge(s_raw[slot(u)], grow * 32 + 32 * (u // UNITS_HELD + 1) - 16)
                if u >= UNITS_HELD:
                    n = u - UNITS_HELD + 1
                    act.wait_ge(s_used, n if turn is None else turn * UNITS_HELD + n)
                nc.scalar.activation(w_parts(u)[0], raw[:, slot(u), :], ACT.Copy).then_inc(s_hi, 1)

            t = Tally()

            def junk_free():
                for key, done in (("ss", s_ss), ("oss", s_oss)):
                    if t.last(key):
                        act.wait_ge(done, t.last(key))

            def square(pos, key=None):
                if key is None:
                    act.wait_ge(s_x[pos], 16)
                else:
                    in_sbuf(act, (*key, pos, 1))
                junk_free()
                t.next("ss")
                nc.scalar.activation(junk[:, :], x[:, pos, :], ACT.Square,
                                     accum_out=ss[:, pos:pos + 1]).then_inc(s_ss, 1)

            def hi_part(dst, b, key, n_tiles=4, turn=None):
                act.wait_ge(s_filled, filled[key] if turn is None else turn * FILLED_PER_TURN + filled[key])
                src = bank[b][:, 0:P * n_tiles].rearrange("p (k s) -> p k s", k=n_tiles)
                nc.scalar.activation(dst, src, ACT.Copy).then_inc(s_hipart, 1)

            def x_hi(name, pos):
                for j, b in enumerate(x_banks(name, pos)):
                    hi_part(x_parts(name)[0][:, 4 * j:4 * j + 4, own(pos)], b, ("xT", name, pos, j))

            def ffn(f, u0, name, aside=None):
                def silu_gate(pos, j, g, turn=None):
                    if pos == 0:
                        n = filled["gu", f, g, j]
                        act.wait_ge(s_filled, n if turn is None else turn * FILLED_PER_TURN + n)
                    else:
                        n = u0 + 4 * g + 2 * j + 2
                        act.wait_ge(s_used, n if turn is None else turn * UNITS_HELD + n)
                    nc.scalar.activation(silu[:, pos, j, :], bank[acc(pos, j)][:, 0:CH], ACT.Silu).then_inc(s_silu, 1)

                def h_hi(pos, g, turn=None, n_tiles=4):
                    k0 = 4 * g if turn is None else turn * 4 + 4 * g
                    hi_part(hT_hi[:, bass.ds(k0, n_tiles), own(pos)], 4 + 2 * pos, ("hT", (f, g), pos),
                            n_tiles, turn)

                def turn_of(g, turn=None):
                    if g == 0:
                        if name == "ln_ffn1_1":
                            x_hi("kv_norm", 1)
                        x_hi(name, 1)
                    silu_gate(0, 1, g, turn)
                    split(u0 + 4 * g + 4, turn)
                    split(u0 + 4 * g + 5, turn)
                    silu_gate(1, 0, g, turn)
                    h_hi(0, g, turn)
                    split(u0 + 4 * g + 6, turn)
                    split(u0 + 4 * g + 7, turn)
                    silu_gate(1, 1, g, turn)
                    silu_gate(0, 0, g + 1, turn)
                    h_hi(1, g, turn)

                silu_gate(0, 0, 0)
                turn_of(0)
                if aside:
                    aside()
                with act.Fori(0, LOOP_TURNS) as turn:
                    turn_of(1, turn)
                turn_of(4)
                split(u0 + 24)
                split(u0 + 25)
                silu_gate(1, 0, 5)
                h_hi(0, 5, n_tiles=2)
                h_hi(1, 5, n_tiles=2)
                for i in range(26, 33):
                    split(u0 + i)

            def boundary(key, u0, name):
                square(0, key)
                split(u0)
                split(u0 + 1)
                x_hi(name, 0)
                split(u0 + 2)
                split(u0 + 3)
                square(1, key)

            def copy_bank(dst, b, sem_full, n):
                act.wait_ge(sem_full, n)
                return nc.scalar.activation(dst, bank[b][:, :], ACT.Copy)

            def transposed(dst, b, key):
                copy_bank(dst, b, s_filled, filled[key]).then_inc(s_read[b], 1)

            def exps(layer, pos, r):
                act.wait_ge(s_negm, ROUNDS * layer + round_no(pos, r) + 1)
                n, keys = per_bank(pos), P * (pos + 1)
                p = probs[r % 2].rearrange("p (i c k) -> p i c k", i=n, c=2)
                for c, b in enumerate(pair(r)):
                    for i in range(n):
                        head = n * r + i
                        ins = nc.scalar.activation(p[:, i, c, :], bank[b][:, keys * i:keys * (i + 1)], ACT.Exp,
                                                   bias=negm[:, pos, head, c:c + 1], scale=SCALE,
                                                   accum_out=den[:, pos, head, c:c + 1])
                    ins.then_inc(s_read[b], 1)

            def p_transposed(layer, pos, r):
                for c in (1,) if layer == 0 else (0, 1):
                    at = 0 if layer == 0 else BANK * c
                    transposed(pT[:, r % 2, at:at + BANK], pair(r)[c], ("pT", layer, pos, r, c))

            square(0)

            def split_half(u, i):
                act.wait_ge((s_gate, s_raw)[i][u], 16)
                nc.scalar.activation(half_of(w_hi, u, i), half_of(raw, u, i), ACT.Copy).then_inc((s_gate_hi, s_hi)[i], 1)

            split_half(0, 0)
            x_hi("ln_ffn1_0", 0)
            split_half(0, 1)
            for u in range(1, UNITS_HELD):
                split_half(u, 0)
                split_half(u, 1)
                if u == 2:
                    square(1)

            def tables():
                act.wait_ge(s_fold, 1)
                nc.scalar.activation(half_sin[:, :, :], ang[:, :, :], ACT.Sin, scale=0.5).then_inc(s_trig, 1)
                nc.scalar.activation(sin2[:, :, 1, :], ang[:, :, :], ACT.Sin).then_inc(s_trig, 1)
                act.wait_ge(s_lamd, 1)
                nc.scalar.activation(lame[:, :], lamd[:, :], ACT.Exp).then_inc(s_lame, 1)

            ffn(0, U_FFN1_0, "ln_ffn1_0", tables)
            boundary(("down", 0), U_QKV, "ln_mix_0")

            def projection(part, pos, j, dst):
                if pos == 0:
                    ins = copy_bank(dst, acc(0, j), s_filled, filled["qkv", part, j])
                else:
                    ins = copy_bank(dst, acc(1, j), s_used, U_QKV + 4 * part + 2 * j + 2)
                ins.then_inc(s_read[acc(pos, j)], 1)

            def qk_transposed(which, pos):
                for j in range(2):
                    dst = qT[:, 4 * j:4 * j + 4, own(pos)] if which == 0 else kT_a[j][:, :, own(pos)]
                    transposed(dst, qk_bank(which, pos, j), ("qkT", which, pos, j))

            u_v = U_QKV + 8
            projection(0, 0, 0, q_a[:, 0, 0:BANK])
            x_hi("ln_mix_0", 1)
            projection(0, 0, 1, q_a[:, 0, BANK:D])
            split(U_QKV + 4)
            split(U_QKV + 5)
            projection(0, 1, 0, q_a[:, 1, 0:BANK])
            split(U_QKV + 6)
            split(U_QKV + 7)
            projection(0, 1, 1, q_a[:, 1, BANK:D])
            projection(1, 0, 0, k_a[:, 0, 0:BANK])
            projection(1, 0, 1, k_a[:, 0, BANK:D])
            qk_transposed(0, 0)
            split(u_v)
            qk_transposed(0, 1)
            split(u_v + 1)
            projection(1, 1, 0, k_a[:, 1, 0:BANK])
            split(u_v + 2)
            split(u_v + 3)
            projection(1, 1, 1, k_a[:, 1, BANK:D])

            qk_transposed(1, 0)
            projection(2, 0, 0, v_a[:, 0, 0:BANK])
            exps(0, 0, 0)
            qk_transposed(1, 1)
            projection(2, 0, 1, v_a[:, 0, BANK:D])
            exps(0, 0, 1)
            split(U_WO_A)
            p_transposed(0, 0, 0)
            projection(2, 1, 0, v_a[:, 1, 0:BANK])
            p_transposed(0, 0, 1)
            split(U_WO_A + 1)
            exps(0, 1, 0)

            def o_squares(pos, j):
                in_sbuf(act, ("o", 0, pos, j))
                junk_free()
                t.next("oss")
                for head in range(4 * j, 4 * j + 4):
                    ins = nc.scalar.activation(junk[:, KVW * head:KVW * (head + 1)],
                                               xn[:, pos, KVW * head:KVW * (head + 1)], ACT.Square,
                                               accum_out=oss[:, pos, head:head + 1])
                ins.then_inc(s_oss, 1)

            def sink_exp(pos, j):
                act.wait_ge(s_earg, half_no(pos, j))
                e = sink_e[:, pos, 4 * j:4 * j + 4, :]
                nc.scalar.activation(e, e, ACT.Exp).then_inc(s_esink, 1)

            def o_hi(layer, pos, j):
                hi_part(xT_hi[:, 4 * j:4 * j + 4, own(pos)], o_bank(pos, j), ("oT", layer, pos, j))

            def next_phase(layer, u_next, name):
                square(0, ("wo", layer))
                o_hi(layer, 1, 1)
                split(u_next)
                x_hi(name, 0)
                split(u_next + 1)
                split(u_next + 2)
                split(u_next + 3)
                square(1, ("wo", layer))

            o_squares(0, 0)
            split(U_WO_A + 2)
            exps(0, 1, 1)
            p_transposed(0, 1, 0)
            o_hi(0, 0, 0)
            o_squares(0, 1)
            p_transposed(0, 1, 1)
            projection(2, 1, 1, v_a[:, 1, BANK:D])
            exps(0, 1, 2)
            o_squares(1, 0)
            o_hi(0, 0, 1)
            p_transposed(0, 1, 2)
            exps(0, 1, 3)
            split(U_WO_A + 3)
            p_transposed(0, 1, 3)
            o_hi(0, 1, 0)
            o_squares(1, 1)
            next_phase(0, U_FFN2_0, "ln_ffn2_0")
            ffn(1, U_FFN2_0, "ln_ffn2_0")
            square(0, ("down", 1))
            split(U_KV)
            split(U_FFN1_1)
            x_hi("kv_norm", 0)
            x_hi("ln_ffn1_1", 0)
            split(U_FFN1_1 + 1)
            split(U_FFN1_1 + 2)
            square(1, ("down", 1))
            split(U_FFN1_1 + 3)
            ffn(2, U_FFN1_1, "ln_ffn1_1")
            boundary(("down", 2), U_WQ, "ln_mix_1")
            transposed(kT_b.rearrange("p g s -> p (g s)"), 4, ("kT",))
            x_hi("ln_mix_1", 1)
            transposed(qT[:, 0:4, own(0)], 4, ("qT_b", 0, 0))
            split(U_WO_B)
            transposed(qT[:, 4:8, own(0)], 6, ("qT_b", 0, 1))
            exps(1, 0, 0)
            sink_exp(0, 0)
            exps(1, 0, 1)
            sink_exp(0, 1)
            p_transposed(1, 0, 0)
            split(U_WO_B + 1)
            split(U_WO_B + 2)
            transposed(qT[:, 0:4, own(1)], acc(0, 1), ("qT_b", 1, 0))
            p_transposed(1, 0, 1)
            exps(1, 1, 0)
            p_transposed(1, 1, 0)
            o_hi(1, 0, 0)
            split(U_WO_B + 3)
            transposed(qT[:, 4:8, own(1)], acc(1, 1), ("qT_b", 1, 1))
            exps(1, 1, 1)
            sink_exp(1, 0)
            p_transposed(1, 1, 1)
            exps(1, 1, 2)
            o_hi(1, 0, 1)
            p_transposed(1, 1, 2)
            exps(1, 1, 3)
            sink_exp(1, 1)
            p_transposed(1, 1, 3)
            o_hi(1, 1, 0)
            next_phase(1, U_FFN2_1, "ln_ffn2_1")
            ffn(3, U_FFN2_1, "ln_ffn2_1")
            square(0, ("down", 3))
            act.wait_ge(s_ss, t.last("ss"))
            for j in range(2):
                cols = slice(BANK * j, BANK * (j + 1))
                act.wait_ge(s_res, j + 1)
                nc.scalar.activation(junk[:, cols], x[:, 1, cols], ACT.Square,
                                     accum_out=ss_part[:, j:j + 1]).then_inc(s_ss, 1)

        @block.vector
        def _(dve):
            t = Tally()

            def link(ins):
                ins.then_inc(s_dve, 1)
                dve.wait_ge(s_dve, t.next("dve"))

            def split(u, turn=None):
                if u >= N_UNITS:
                    return
                dve.wait_ge(s_hi, u + 1 if turn is None else turn * UNITS_HELD + (u + 1))
                hi, lo = w_parts(u)
                nc.vector.tensor_tensor(lo, raw[:, slot(u), :], hi.bitcast(F32), ALU.subtract).then_inc(s_lo, 1)

            def lo_part(dst, hi, b, n_tiles=4):
                dve.wait_ge(s_hipart, t.next("hipart"))
                src = bank[b][:, 0:P * n_tiles].rearrange("p (k s) -> p k s", k=n_tiles)
                nc.vector.tensor_tensor(dst, src, hi.bitcast(F32), ALU.subtract).then_inc(s_read[b], 1)

            def x_lo(name, pos):
                hi, lo = x_parts(name)
                for j, b in enumerate(x_banks(name, pos)):
                    lo_part(lo[:, 4 * j:4 * j + 4, own(pos)], hi[:, 4 * j:4 * j + 4, own(pos)], b)

            def norm(name, pos, fresh=True):
                if fresh:
                    dve.wait_ge(s_rstd, t.next("rstd"))
                v, n = vec_of(name)
                dve.wait_ge(s_vec[v], n)
                nc.vector.scalar_tensor_tensor(out=xn_of(name, pos), in0=x[:, pos, :], scalar=rstd[:, pos:pos + 1],
                                               in1=vec[:, v, :], op0=ALU.mult, op1=ALU.mult).then_inc(s_xn, 1)

            def residual(key, pos, scale, u_last):
                if pos == 0:
                    dve.wait_ge(s_filled, filled[key])
                else:
                    dve.wait_ge(s_used, u_last + 1)
                for j in range(2):
                    cols = slice(BANK * j, BANK * (j + 1))
                    nc.vector.scalar_tensor_tensor(out=x[:, pos, cols], in0=bank[acc(pos, j)][:, :], scalar=scale,
                                                   in1=x[:, pos, cols], op0=ALU.mult,
                                                   op1=ALU.add).then_inc(s_read[acc(pos, j)], 1)

            def boundary(key, u_last, u0, name, scale=0.5):
                residual(key, 0, scale, u_last)
                norm(name, 0)
                split(u0)
                split(u0 + 1)
                x_lo(name, 0)
                residual(key, 1, scale, u_last)
                split(u0 + 2)
                split(u0 + 3)
                norm(name, 1)

            def add_bias(dst, b, w, bias):
                nc.vector.tensor_tensor(dst, bank[b][:, 0:w], bias, ALU.add).then_inc(s_read[b], 1)

            def ffn(f, u0, name):
                def mul(pos, j):
                    dve.wait_ge(s_silu, t.next("silu"))
                    b = acc(pos, j)
                    nc.vector.tensor_tensor(h[:, pos, CH * j:CH * (j + 1)], silu[:, pos, j, :], bank[b][:, CH:2 * CH],
                                            ALU.mult).then_inc(s_read[b], 1)

                def h_lo(pos, g, turn=None, n_tiles=4):
                    k0 = 4 * g if turn is None else turn * 4 + 4 * g
                    tile = bass.ds(k0, n_tiles)
                    lo_part(hT_lo[:, tile, own(pos)], hT_hi[:, tile, own(pos)], 4 + 2 * pos, n_tiles)

                def turn_of(g, turn=None):
                    if g == 0:
                        if name == "ln_ffn1_1":
                            x_lo("kv_norm", 1)
                        x_lo(name, 1)
                    mul(0, 1)
                    if g == 0 and name == "ln_ffn1_1":
                        dve.wait_ge(s_filled, filled["kv",])
                        add_bias(kvb[:, 1, :], acc(1, 1), 2 * KVW, bkv[:, :])
                    split(u0 + 4 * g + 4, turn)
                    split(u0 + 4 * g + 5, turn)
                    mul(1, 0)
                    h_lo(0, g, turn)
                    split(u0 + 4 * g + 6, turn)
                    split(u0 + 4 * g + 7, turn)
                    mul(1, 1)
                    mul(0, 0)
                    h_lo(1, g, turn)

                mul(0, 0)
                turn_of(0)
                with dve.Fori(0, LOOP_TURNS) as turn:
                    t.enter(turn, {"silu": 4, "hipart": 2})
                    turn_of(1, turn)
                t.leave(LOOP_TURNS)
                turn_of(4)
                split(u0 + 24)
                split(u0 + 25)
                mul(1, 0)
                h_lo(0, 5, n_tiles=2)
                h_lo(1, 5, n_tiles=2)
                for i in range(26, 33):
                    split(u0 + i)

            def maxima(layer, pos, r):
                n, keys = per_bank(pos), P * (pos + 1)
                heads = slice(n * r, n * (r + 1))
                for c, b in enumerate(pair(r)):
                    dve.wait_ge(s_filled, filled["scores", layer, pos, r, c])
                    nc.vector.tensor_reduce(mx[:, pos, heads, c], bank[b][:, :].rearrange("p (i k) -> p i k", i=n),
                                            AX.X, ALU.max).then_inc(s_dve, 1)
                    t.next("dve")
                dve.wait_ge(s_dve, t.last("dve"))
                if layer == 0:
                    ins = nc.vector.tensor_scalar(negm[:, pos, heads, :], mx[:, pos, heads, :], -SCALE, None, ALU.mult)
                else:
                    sink = negsink[:, :].rearrange("p (h c) -> p h c", c=2)
                    ins = nc.vector.scalar_tensor_tensor(out=negm[:, pos, heads, :], in0=mx[:, pos, heads, :],
                                                         scalar=-SCALE, in1=sink[:, heads, :],
                                                         op0=ALU.mult, op1=ALU.min)
                ins.then_inc(s_negm, 1)

            def combine(pos, r):
                n, keys = per_bank(pos), P * (pos + 1)
                heads = slice(n * r, n * (r + 1))
                in_sbuf(dve, ("scores", 0, pos, r, 1))
                link(nc.vector.reciprocal(rden[:, pos, heads, :], den[:, pos, heads, :]))
                link(nc.vector.scalar_tensor_tensor(out=coef[:, pos, heads], in0=den[:, pos, heads, 0],
                                                    scalar=neglam[:, 0:1], in1=rden[:, pos, heads, 1],
                                                    op0=ALU.mult, op1=ALU.mult))
                p = probs[r % 2].rearrange("p (i c k) -> p i c k", i=n, c=2)
                for i in range(n):
                    head = n * r + i
                    ins = nc.vector.scalar_tensor_tensor(out=a_mix[:, r % 2, keys * i:keys * (i + 1)],
                                                         in0=p[:, i, 1, :], scalar=coef[:, pos, head:head + 1],
                                                         in1=p[:, i, 0, :], op0=ALU.mult, op1=ALU.add)
                ins.then_inc(s_mix, 1)

            def output(layer, pos, j):
                heads, b = slice(4 * j, 4 * j + 4), acc(pos, j)
                if layer == 1:
                    dve.wait_ge(s_esink, half_no(pos, j))
                    link(nc.vector.tensor_tensor(den[:, pos, heads, :], den[:, pos, heads, :],
                                                 sink_e[:, pos, heads, :], ALU.add))
                    link(nc.vector.reciprocal(rden[:, pos, heads, :], den[:, pos, heads, :]))
                dve.wait_ge(s_filled, filled["o", layer, pos, j])
                if layer == 0:
                    w, r = 2 * HD, rden[:, pos, heads, 0]
                else:
                    w, r = HD, rden[:, pos, heads, :].rearrange("p h c -> p (h c)")
                n = BANK // w
                nc.vector.tensor_tensor(
                    xn[:, pos, BANK * j:BANK * (j + 1)].rearrange("p (n d) -> p n d", n=n),
                    bank[b][:, :].rearrange("p (n d) -> p n d", n=n),
                    r.unsqueeze(2).to_broadcast([P, n, w]), ALU.mult).then_inc(s_read[b], 1)

            def sub_norm(pos, j):
                dve.wait_ge(s_orstd, half_no(pos, j))
                for head in range(4 * j, 4 * j + 4):
                    o = xn[:, pos, KVW * head:KVW * (head + 1)]
                    ins = nc.vector.scalar_tensor_tensor(out=o, in0=o, scalar=orstd[:, pos, head:head + 1],
                                                         in1=gsub[:, :], op0=ALU.mult, op1=ALU.mult)
                ins.then_inc(s_on, 1)

            def o_lo(pos, j):
                lo_part(xT_lo[:, 4 * j:4 * j + 4, own(pos)], xT_hi[:, 4 * j:4 * j + 4, own(pos)], o_bank(pos, j))

            def next_phase(layer, u0, name):
                residual(("wo", layer), 0, 1.0, None)
                if layer == 0:
                    sub_norm(1, 1)
                o_lo(1, 1)
                norm(name, 0)
                split(u0)
                x_lo(name, 0)
                split(u0 + 1)
                residual(("wo", layer), 1, 1.0, u0 - 1)
                split(u0 + 2)
                split(u0 + 3)
                norm(name, 1)

            norm("ln_ffn1_0", 0)

            def split_half(u, i):
                dve.wait_ge((s_gate_hi, s_hi)[i], u + 1)
                ins = nc.vector.tensor_tensor(half_of(w_lo, u, i), half_of(raw, u, i),
                                              half_of(w_hi, u, i).bitcast(F32), ALU.subtract)
                if i == 1:
                    ins.then_inc(s_lo, 1)

            split_half(0, 0)
            x_lo("ln_ffn1_0", 0)
            split_half(0, 1)
            for u in range(1, UNITS_HELD):
                if u == 3:
                    norm("ln_ffn1_0", 1)
                split_half(u, 0)
                split_half(u, 1)

            ffn(0, U_FFN1_0, "ln_ffn1_0")
            boundary(("down", 0), U_QKV - 1, U_QKV, "ln_mix_0")

            dve.wait_ge(s_table, TABLES)
            x_lo("ln_mix_0", 1)
            for i in range(4, 12):
                split(U_QKV + i)
            maxima(0, 0, 0)
            maxima(0, 0, 1)
            combine(0, 0)
            combine(0, 1)
            split(U_WO_A)
            maxima(0, 1, 0)
            output(0, 0, 0)
            split(U_WO_A + 1)
            combine(1, 0)
            output(0, 0, 1)
            maxima(0, 1, 1)
            sub_norm(0, 0)
            combine(1, 1)
            o_lo(0, 0)
            split(U_WO_A + 2)
            maxima(0, 1, 2)
            sub_norm(0, 1)
            combine(1, 2)
            output(0, 1, 0)
            maxima(0, 1, 3)
            o_lo(0, 1)
            sub_norm(1, 0)
            combine(1, 3)
            split(U_WO_A + 3)
            o_lo(1, 0)
            output(0, 1, 1)
            next_phase(0, U_FFN2_0, "ln_ffn2_0")

            ffn(1, U_FFN2_0, "ln_ffn2_0")
            residual(("down", 1), 0, 0.5, None)
            norm("kv_norm", 0)
            norm("ln_ffn1_1", 0, fresh=False)
            split(U_KV)
            split(U_FFN1_1)
            x_lo("kv_norm", 0)
            x_lo("ln_ffn1_1", 0)
            residual(("down", 1), 1, 0.5, U_KV - 1)
            split(U_FFN1_1 + 1)
            dve.wait_ge(s_used, U_KV + 1)
            add_bias(kvb[:, 0, :], acc(0, 1), 2 * KVW, bkv[:, :])
            split(U_FFN1_1 + 2)
            norm("kv_norm", 1)
            norm("ln_ffn1_1", 1, fresh=False)
            split(U_FFN1_1 + 3)
            ffn(2, U_FFN1_1, "ln_ffn1_1")
            boundary(("down", 2), U_WQ - 1, U_WQ, "ln_mix_1")

            v, n = vec_of("b_b_q")
            dve.wait_ge(s_vec[v], n)

            def queries(pos, j):
                cols = slice(BANK * j, BANK * (j + 1))
                if pos == 0:
                    dve.wait_ge(s_filled, filled["q_b", j])
                else:
                    dve.wait_ge(s_used, U_WQ + 2 * j + 2)
                add_bias(xn[:, pos, cols], acc(pos, j), BANK, vec[:, v, cols])

            def sink_minus_max(pos, j):
                dve.wait_ge(s_negm, ROUNDS + round_no(pos, rounds(pos) // 2 * (j + 1)))
                heads = slice(4 * j, 4 * j + 4)
                nc.vector.tensor_tensor(sink_e[:, pos, heads, :], negm[:, pos, heads, :],
                                        sinks[:, :].rearrange("p (h c) -> p h c", c=2)[:, heads, :],
                                        ALU.add).then_inc(s_earg, 1)

            queries(0, 0)
            x_lo("ln_mix_1", 1)
            queries(0, 1)
            split(U_WO_B)
            maxima(1, 0, 0)
            sink_minus_max(0, 0)
            queries(1, 0)
            maxima(1, 0, 1)
            sink_minus_max(0, 1)
            split(U_WO_B + 1)
            queries(1, 1)
            output(1, 0, 0)
            maxima(1, 1, 0)
            split(U_WO_B + 2)
            output(1, 0, 1)
            maxima(1, 1, 1)
            sink_minus_max(1, 0)
            o_lo(0, 0)
            split(U_WO_B + 3)
            maxima(1, 1, 2)
            maxima(1, 1, 3)
            sink_minus_max(1, 1)
            o_lo(0, 1)
            output(1, 1, 0)
            o_lo(1, 0)
            output(1, 1, 1)
            dve.wait_ge(s_bo, 2)
            next_phase(1, U_FFN2_1, "ln_ffn2_1")

            ffn(3, U_FFN2_1, "ln_ffn2_1")
            residual(("down", 3), 0, 0.5, None)
            norm("final_norm", 0)
            for j in range(2):
                cols = slice(BANK * j, BANK * (j + 1))
                if j == 0:
                    dve.wait_ge(s_filled, filled["down", 3, 0])
                else:
                    dve.wait_ge(s_used, N_UNITS)
                nc.vector.scalar_tensor_tensor(out=x[:, 1, cols], in0=bank[acc(1, j)][:, :], scalar=0.5,
                                               in1=x[:, 1, cols], op0=ALU.mult, op1=ALU.add).then_inc(s_res, 1)
            dve.wait_ge(s_rstd, t.next("rstd"))
            v, _ = vec_of("final_norm")
            for j in range(2):
                cols = slice(BANK * j, BANK * (j + 1))
                nc.vector.scalar_tensor_tensor(out=xn[:, 1, cols], in0=x[:, 1, cols], scalar=rstd[:, 1:2],
                                               in1=vec[:, v, cols], op0=ALU.mult, op1=ALU.mult).then_inc(s_xn, 1)


_INS = ["x", "positions", "ln_ffn1", "ffn1_w_gate", "ffn1_w_up", "ffn1_w_down", "ln_mix", "ln_ffn2",
        "ffn2_w_gate", "ffn2_w_up", "ffn2_w_down", "a_w_qkv", "a_w_o", "a_lambda_q1", "a_lambda_k1",
        "a_lambda_q2", "a_lambda_k2", "a_subln", "b_w_q", "b_b_q", "b_sinks", "b_w_o", "b_b_o", "kv_norm",
        "kv_w_k", "kv_b_k", "kv_w_v", "kv_b_v", "final_norm"]


def kernel(**inputs):
    import concourse.bacc as bacc
    from concourse.bass_utils import run_bass_kernel_spmd

    nc = bacc.Bacc("TRN2", target_bir_lowering=False, num_devices=1)
    arrays, args = {}, {}
    for name in _INS:
        arr = np.ascontiguousarray(inputs[name])
        arrays[f"in_{name}"] = arr
        args[name] = nc.dram_tensor(f"in_{name}", arr.shape, mybir.dt.from_np(arr.dtype), kind="ExternalInput").ap()
    out = nc.dram_tensor("out_h", (1, SEQ, D), F32, kind="ExternalOutput").ap()
    trunk(nc, args, out)
    r = run_bass_kernel_spmd(nc, [arrays], core_ids=[0])
    return r.results[0]["out_h"]
```
